# Optimizing a Trainium2 kernel written in Bass

```python
import math
import jax
import jax.numpy as jnp
from jax import lax
import numpy as np

D_MODEL = 2048
BATCH = 1
SEQ = 256
DEPTH = 2

N_A = DEPTH // 2
N_B = DEPTH - N_A

EXPAND = 2
D_INNER = EXPAND * D_MODEL
SSM_HEAD_DIM = 64
N_SSM_HEADS = D_INNER // SSM_HEAD_DIM
D_STATE = 128
N_GROUPS = 8
HEADS_PER_GROUP = N_SSM_HEADS // N_GROUPS
CONV_W = 4
CONV_DIM = D_INNER + 2 * N_GROUPS * D_STATE
IN_DIM = D_INNER + CONV_DIM + N_SSM_HEADS
CHUNK = 128

DIFF_HEAD_DIM = 64
N_DIFF_HEADS = D_MODEL // (2 * DIFF_HEAD_DIM)
Q_BLOCK = 128

NUM_BUCKETS = 32
MAX_DISTANCE = 128

D_FF = 4 * D_MODEL

NORM_EPS = 1e-6

kernel_name = "yoco_mamba2_diffattn_block"

def rms_norm(x, w, eps=NORM_EPS):
    xf = x.astype(jnp.float32)
    y = xf * lax.rsqrt(jnp.mean(xf * xf, axis=-1, keepdims=True) + eps)
    return (y * w.astype(jnp.float32)).astype(x.dtype)

def sq_relu_mlp(u, w1, w2):
    return jnp.square(jax.nn.relu(u @ w1)) @ w2

def causal_depthwise_conv(x, w, b):
    out = lax.conv_general_dilated(
        x, w[:, None, :], window_strides=(1,), padding=[(CONV_W - 1, 0)],
        dimension_numbers=("NWC", "WIO", "NWC"), feature_group_count=x.shape[-1])
    return out + b

def ssd_chunked_scan(xs, dt, A, Bm, Cm):
    bsz, L = xs.shape[0], xs.shape[1]
    nc = L // CHUNK

    def to_chunks(t):
        return jnp.moveaxis(t.reshape((bsz, nc, CHUNK) + t.shape[2:]), 1, 0)

    causal = jnp.tril(jnp.ones((CHUNK, CHUNK), dtype=bool))[None, :, :, None, None]

    def step(state, inp):
        x, d, b, c = inp
        a = d * A
        cum = jnp.cumsum(a, axis=1)
        seg = cum[:, :, None] - cum[:, None, :]
        decay = jnp.where(causal, jnp.exp(jnp.where(causal, seg, 0.0)), 0.0)
        cb = jnp.einsum("bign,bjgn->bijg", c, b)
        y_intra = jnp.einsum("bijg,bijgr,bjgr,bjgrp->bigrp", cb, decay, d, x)
        y_inter = jnp.einsum("bign,bgrpn,bigr->bigrp", c, state, jnp.exp(cum))
        to_end = jnp.exp(cum[:, -1:] - cum) * d
        new_state = (state * jnp.exp(cum[:, -1])[..., None, None]
                     + jnp.einsum("bjgn,bjgr,bjgrp->bgrpn", b, to_end, x))
        return new_state, y_intra + y_inter

    state0 = jnp.zeros((bsz, N_GROUPS, HEADS_PER_GROUP, SSM_HEAD_DIM, D_STATE), jnp.float32)
    _, ys = lax.scan(step, state0, (to_chunks(xs), to_chunks(dt), to_chunks(Bm), to_chunks(Cm)))
    return jnp.moveaxis(ys, 0, 1).reshape(xs.shape)

def mamba2_mixer(u, in_proj, conv_w, conv_b, dt_bias, A_log, D_skip, gate_norm_w, out_proj):
    bsz, L, _ = u.shape
    zxbcdt = u @ in_proj
    z = zxbcdt[..., :D_INNER]
    xbc = zxbcdt[..., D_INNER:D_INNER + CONV_DIM]
    dt_raw = zxbcdt[..., D_INNER + CONV_DIM:]
    xbc = jax.nn.silu(causal_depthwise_conv(xbc, conv_w, conv_b))
    xs = xbc[..., :D_INNER].astype(jnp.float32).reshape(bsz, L, N_GROUPS, HEADS_PER_GROUP, SSM_HEAD_DIM)
    Bm = xbc[..., D_INNER:D_INNER + N_GROUPS * D_STATE].astype(jnp.float32).reshape(bsz, L, N_GROUPS, D_STATE)
    Cm = xbc[..., D_INNER + N_GROUPS * D_STATE:].astype(jnp.float32).reshape(bsz, L, N_GROUPS, D_STATE)
    dt = jax.nn.softplus(dt_raw.astype(jnp.float32) + dt_bias.astype(jnp.float32))
    dt = dt.reshape(bsz, L, N_GROUPS, HEADS_PER_GROUP)
    A = -jnp.exp(A_log.astype(jnp.float32)).reshape(N_GROUPS, HEADS_PER_GROUP)
    y = ssd_chunked_scan(xs, dt, A, Bm, Cm)
    y = y + D_skip.astype(jnp.float32).reshape(N_GROUPS, HEADS_PER_GROUP)[:, :, None] * xs
    y = y.reshape(bsz, L, D_INNER)
    g = y * jax.nn.silu(z.astype(jnp.float32))
    g = g.reshape(bsz, L, N_GROUPS, D_INNER // N_GROUPS)
    g = g * lax.rsqrt(jnp.mean(g * g, axis=-1, keepdims=True) + 1e-5)
    g = g.reshape(bsz, L, D_INNER) * gate_norm_w.astype(jnp.float32)
    return g.astype(u.dtype) @ out_proj

def t5_causal_bucket(dist):
    n = jnp.maximum(dist, 0)
    max_exact = NUM_BUCKETS // 2
    nf = jnp.maximum(n, 1).astype(jnp.float32)
    large = max_exact + (jnp.log(nf / max_exact) / math.log(MAX_DISTANCE / max_exact)
                         * (NUM_BUCKETS - max_exact)).astype(jnp.int32)
    large = jnp.minimum(large, NUM_BUCKETS - 1)
    return jnp.where(n < max_exact, n, large)

def diff_attention(u, k, v, w_q, lq1, lk1, lq2, lk2, subln_w, out_proj, rel_bias, lambda_init):
    bsz, S, _ = u.shape
    q = (u @ w_q).reshape(bsz, S, N_DIFF_HEADS, 2, DIFF_HEAD_DIM)
    lam = (jnp.exp(jnp.sum(lq1.astype(jnp.float32) * lk1.astype(jnp.float32)))
           - jnp.exp(jnp.sum(lq2.astype(jnp.float32) * lk2.astype(jnp.float32)))
           + lambda_init)
    scale = DIFF_HEAD_DIM ** -0.5
    kpos = jnp.arange(S, dtype=jnp.int32)

    def block(i):
        start = i * Q_BLOCK
        qb = lax.dynamic_slice_in_dim(q, start, Q_BLOCK, axis=1)
        logits = jnp.einsum("bqhcd,bkhcd->bhcqk", qb, k).astype(jnp.float32) * scale
        qpos = start + jnp.arange(Q_BLOCK, dtype=jnp.int32)
        dist = qpos[:, None] - kpos[None, :]
        bias = jnp.transpose(rel_bias[t5_causal_bucket(dist)], (2, 0, 1))
        logits = logits + bias.astype(jnp.float32)[None, :, None]
        logits = jnp.where((dist >= 0)[None, None, None], logits, -jnp.inf)
        p = jax.nn.softmax(logits, axis=-1)
        attn = p[:, :, 0] - lam * p[:, :, 1]
        return jnp.einsum("bhqk,bkhe->bqhe", attn.astype(v.dtype), v)

    o = lax.map(block, jnp.arange(S // Q_BLOCK))
    o = jnp.moveaxis(o, 0, 1).reshape(bsz, S, N_DIFF_HEADS, 2 * DIFF_HEAD_DIM)
    o = rms_norm(o, subln_w, eps=1e-5) * (1.0 - lambda_init)
    return o.reshape(bsz, S, D_MODEL) @ out_proj

def setup_inputs(seed: int = 0) -> dict:
    key = jax.random.key(seed)
    ks = jax.random.split(key, 32)
    f32 = jnp.float32

    def nrm(k, shape, fan_in):
        return jax.random.normal(k, shape, f32) * (fan_in ** -0.5)

    def gain(k, shape):
        return 1.0 + 0.05 * jax.random.normal(k, shape, f32)

    x = jax.random.normal(ks[0], (BATCH, SEQ, D_MODEL), f32)
    a_in_proj = nrm(ks[1], (N_A, D_MODEL, IN_DIM), D_MODEL)
    a_conv_w = nrm(ks[2], (N_A, CONV_W, CONV_DIM), CONV_W)
    a_conv_b = 0.01 * jax.random.normal(ks[3], (N_A, CONV_DIM), f32)
    dt0 = jnp.exp(jax.random.uniform(ks[4], (N_A, N_SSM_HEADS), f32, math.log(1e-3), math.log(1e-1)))
    a_dt_bias = dt0 + jnp.log(-jnp.expm1(-dt0))
    a_A_log = jnp.log(jax.random.uniform(ks[5], (N_A, N_SSM_HEADS), f32, 1.0, 16.0))
    a_D = gain(ks[6], (N_A, N_SSM_HEADS))
    a_gate_norm_w = gain(ks[7], (N_A, D_INNER))
    a_out_proj = nrm(ks[8], (N_A, D_INNER, D_MODEL), D_INNER)
    kv_norm_w = gain(ks[9], (D_MODEL,))
    w_k = nrm(ks[10], (D_MODEL, N_DIFF_HEADS * 2 * DIFF_HEAD_DIM), D_MODEL)
    w_v = nrm(ks[11], (D_MODEL, N_DIFF_HEADS * 2 * DIFF_HEAD_DIM), D_MODEL)
    rel_bias = 0.5 * jax.random.normal(ks[12], (NUM_BUCKETS, N_DIFF_HEADS), f32)
    b_w_q = nrm(ks[13], (N_B, D_MODEL, N_DIFF_HEADS * 2 * DIFF_HEAD_DIM), D_MODEL)
    b_lambda_q1 = 0.1 * jax.random.normal(ks[14], (N_B, DIFF_HEAD_DIM), f32)
    b_lambda_k1 = 0.1 * jax.random.normal(ks[15], (N_B, DIFF_HEAD_DIM), f32)
    b_lambda_q2 = 0.1 * jax.random.normal(ks[16], (N_B, DIFF_HEAD_DIM), f32)
    b_lambda_k2 = 0.1 * jax.random.normal(ks[17], (N_B, DIFF_HEAD_DIM), f32)
    b_subln_w = gain(ks[18], (N_B, 2 * DIFF_HEAD_DIM))
    b_out_proj = nrm(ks[19], (N_B, D_MODEL, D_MODEL), D_MODEL)
    norm_pre_mix = gain(ks[20], (DEPTH, D_MODEL))
    norm_post_mix = gain(ks[21], (DEPTH, D_MODEL))
    norm_pre_mlp = gain(ks[22], (DEPTH, D_MODEL))
    norm_post_mlp = gain(ks[23], (DEPTH, D_MODEL))
    mlp_w1 = nrm(ks[24], (DEPTH, D_MODEL, D_FF), D_MODEL)
    mlp_w2 = nrm(ks[25], (DEPTH, D_FF, D_MODEL), D_FF)
    return {
        "x": x,
        "a_in_proj": a_in_proj, "a_conv_w": a_conv_w, "a_conv_b": a_conv_b,
        "a_dt_bias": a_dt_bias, "a_A_log": a_A_log, "a_D": a_D,
        "a_gate_norm_w": a_gate_norm_w, "a_out_proj": a_out_proj,
        "kv_norm_w": kv_norm_w, "w_k": w_k, "w_v": w_v, "rel_bias": rel_bias,
        "b_w_q": b_w_q, "b_lambda_q1": b_lambda_q1, "b_lambda_k1": b_lambda_k1,
        "b_lambda_q2": b_lambda_q2, "b_lambda_k2": b_lambda_k2,
        "b_subln_w": b_subln_w, "b_out_proj": b_out_proj,
        "norm_pre_mix": norm_pre_mix, "norm_post_mix": norm_post_mix,
        "norm_pre_mlp": norm_pre_mlp, "norm_post_mlp": norm_post_mlp,
        "mlp_w1": mlp_w1, "mlp_w2": mlp_w2,
    }

def reference(x, a_in_proj, a_conv_w, a_conv_b, a_dt_bias, a_A_log, a_D, a_gate_norm_w, a_out_proj,
              kv_norm_w, w_k, w_v, rel_bias,
              b_w_q, b_lambda_q1, b_lambda_k1, b_lambda_q2, b_lambda_k2, b_subln_w, b_out_proj,
              norm_pre_mix, norm_post_mix, norm_pre_mlp, norm_post_mlp, mlp_w1, mlp_w2):
    bsz, S, _ = x.shape
    h = x
    k_shared = None
    v_shared = None
    for l in range(DEPTH):
        u = rms_norm(h, norm_pre_mix[l])
        if l < N_A:
            mix = mamba2_mixer(u, a_in_proj[l], a_conv_w[l], a_conv_b[l], a_dt_bias[l], a_A_log[l],
                               a_D[l], a_gate_norm_w[l], a_out_proj[l])
        else:
            if l == N_A:
                kv_in = rms_norm(h, kv_norm_w)
                k_shared = (kv_in @ w_k).reshape(bsz, S, N_DIFF_HEADS, 2, DIFF_HEAD_DIM)
                v_shared = (kv_in @ w_v).reshape(bsz, S, N_DIFF_HEADS, 2 * DIFF_HEAD_DIM)
            j = l - N_A
            lambda_init = 0.8 - 0.6 * math.exp(-0.3 * l)
            mix = diff_attention(u, k_shared, v_shared, b_w_q[j], b_lambda_q1[j], b_lambda_k1[j],
                                 b_lambda_q2[j], b_lambda_k2[j], b_subln_w[j], b_out_proj[j],
                                 rel_bias, lambda_init)
        h = h + rms_norm(mix, norm_post_mix[l])
        m = sq_relu_mlp(rms_norm(h, norm_pre_mlp[l]), mlp_w1[l], mlp_w2[l])
        h = h + rms_norm(m, norm_post_mlp[l])
    return h


_drawn_inputs = setup_inputs


def setup_inputs(seed=0):
    import zlib

    import numpy as np

    out = dict(_drawn_inputs(seed))
    spreads = {}
    factors = {'a_conv_b': 4.878, 'b_lambda_q1': 200.0, 'b_lambda_q2': 4.089}
    for name, (base, spread) in spreads.items():
        noise = np.random.default_rng([zlib.crc32(name.encode()), seed]).standard_normal(out[name].shape)
        drawn = base * np.exp(spread * noise) if base else spread * noise
        out[name] = jnp.asarray(drawn.astype(out[name].dtype))
    for name, factor in factors.items():
        out[name] = (out[name] * factor).astype(out[name].dtype)
    return out
```

```python
from contextlib import ExitStack

import numpy as np
import concourse.bass as bass
from concourse import mybir

F32 = mybir.dt.float32
F32R = mybir.dt.float32r
I32 = mybir.dt.int32
BF16 = mybir.dt.bfloat16
ALU = mybir.AluOpType
ACT = mybir.ActivationFunctionType
AX = mybir.AxisListType.X

P = 128
D = 2048
S = 256
MT = S // P
DI = 2 * D
G = 8
R = 8
PD = 64
NS = 128
NH = G * R
TAPS = 4
XBC0 = DI
B0 = XBC0 + DI
C0 = B0 + G * NS
DT0 = C0 + G * NS
HEADS = 16
HG = 4
QG = HEADS // HG
DH = 64
FF = 4 * D
BLK = 512
KT = D // P
NT = D // BLK
BUCKETS = 32
MAX_DISTANCE = 128
LAMBDA_INIT = 0.8 - 0.6 * float(np.exp(-0.3))
MASKED = -1.0e30
LEAD = 4
SLAB = 1024
RING = 4


def bucket_bounds():
    exact = BUCKETS // 2
    n = np.arange(S)
    large = exact + (np.log(np.maximum(n, 1).astype(np.float32) / exact)
                     / np.float32(np.log(MAX_DISTANCE / exact)) * (BUCKETS - exact)).astype(np.int32)
    bucket = np.where(n < exact, n, np.minimum(large, BUCKETS - 1))
    return [int(np.argmax(bucket >= b)) for b in range(BUCKETS)] + [S]


class Slab:

    def __init__(self, n, number):
        self.n = number
        self.raw, self.split = n % RING, n % LEAD
        self.used = number + 1
        self.arrived = 16 * (n // RING + 1)


class Phase:

    def __init__(self, slabs, blocks, before, per_block=1):
        self.slabs, self.blocks, self.per_block, self.next = slabs, blocks, per_block, None
        self.first = self.block0 = self.ready0 = 0
        if before:
            before.next = self
            self.first = before.first + before.slabs
            self.block0 = before.block0 + before.blocks
            self.ready0 = before.ready0 + before.blocks * before.per_block

    def slab(self, k, t=0, per=0):
        if per == 0 and k >= self.slabs:
            return self.next.slab(k - self.slabs) if self.next else None
        assert per % LEAD == 0 and per % RING == 0
        n = self.first + k
        slab = Slab(n, n + t * per)
        slab.arrived += t * (16 * per // RING)
        return slab

    def features(self, b):
        return self.ready0 + self.per_block * (b + 1)


def above(value, floor=0):
    return not isinstance(value, int) or value > floor


class Tally:

    def __init__(self, engine, sem):
        self.engine, self.sem, self.base, self.k, self.at = engine, sem, 0, 0, 0

    def mark(self, ins):
        ins.then_inc(self.sem, 1)
        self.k += 1

    def wait(self, back=0):
        self.engine.wait_ge(self.sem, self.at + self.k - back)

    def enter(self, t, per):
        self.base, self.k = self.base + self.k, 0
        self.at = self.base + t * per

    def leave(self, trips, per):
        assert self.k == per, f"{self.k} marks in the loop body, not {per}"
        self.base, self.k = self.base + per * trips, 0
        self.at = self.base


def column_bcast(ap, n):
    return ap.unsqueeze(2).to_broadcast([ap.shape[0], ap.shape[1], n])


def build(nc, w, out):
    mix = Phase(1 + 20 + 7 * 28 + 8, G, None)
    mlp0 = Phase(8 + 7 * 32 + 24, FF // BLK, mix)
    att = Phase(24 + 3 * 32 + 8, QG, mlp0, per_block=HG)
    mlp1 = Phase(8 + 7 * 32 + 24, FF // BLK, att)

    in_proj, out_proj = w["a_in_proj"][0], w["a_out_proj"][0]
    w_q, w_k, w_v, o_proj = w["b_w_q"][0], w["w_k"], w["w_v"], w["b_out_proj"][0]

    def units(*names):
        return [(n, i) for n, c in names for i in range(c)]

    MIX_FIRST = units(("xs", 8), ("bc", 4), ("z", 8))
    MIX_BODY = units(("xs", 8), ("bc", 4), ("acc", 8), ("z", 8))
    ACC = units(("acc", 8))
    MLP_FIRST = units(("up", 8))
    MLP_BODY = units(("up1", 8), ("acc0", 8), ("up0", 8), ("acc1", 8))
    MLP_LAST = units(("up1", 8), ("acc0", 8), ("acc1", 8))
    ATT_FIRST = units(("q", 8), ("k", 8), ("v", 8))
    ATT_BODY = units(("q", 8), ("k", 8), ("v", 8), ("acc", 8))
    SPREAD = {True: ("z", 3), False: ("acc", 7)}
    STATE = {True: ("z", 5), False: ("z", 3)}
    SILU_BC = {True: ("z", 0), False: ("acc", 0)}
    DECAY = {True: ("z", 2), False: ("acc", 3)}

    ctx = ExitStack()
    with ctx:
        def sb(name, shape, dt=F32, stack=ctx):
            return stack.enter_context(nc.sbuf_tensor(name, shape, dt))

        def sem(name):
            return ctx.enter_context(nc.semaphore(name))

        h = sb("h", [P, MT, D])
        y = sb("y", [P, MT, D])
        raw = sb("raw", [P, RING, SLAB])
        whi = sb("whi", [P, LEAD, SLAB], F32R)
        wlo = sb("wlo", [P, LEAD, SLAB], F32R)
        xhi = sb("xhi", [P, KT, S], F32R)
        xlo = sb("xlo", [P, KT, S], F32R)
        bhi = [sb("bhi0", [P, 4, S], F32R)]
        blo = [sb("blo0", [P, 4, S], F32R)]
        postw = sb("postw", [P, D])
        junk = sb("junk", [P, MT, D], BF16)
        ident = sb("ident", [P, P])
        par = sb("par", [P, 4 * P])
        subw = sb("subw", [P, 1])
        stat = sb("stat", [P, 24])
        ssy, ssh, rsy, rsh, ssg, rsg = (stat[:, 2 * i:2 * i + 2] for i in range(6))
        ssa, rsa, rs_x, rs_a = (stat[:, 2 * i:2 * i + 2] for i in range(6, 10))
        neglam = sb("neglam", [P, 4])
        relrow = sb("relrow", [HEADS, BUCKETS])
        bias_row = sb("bias_row", [HEADS, S + P])
        lamv = sb("lamv", [P, 4, DH])
        ps = ctx.enter_context(nc.psum_tensor("ps", [P, 8, BLK], F32))

        mem = ExitStack()

        def mb(name, shape, dt=F32):
            return sb(name, shape, dt, mem)

        par_rows = mb("par_rows", [P, 4, P])
        pre = mb("pre", [P, 6, TAPS - 1 + S])
        conv = mb("conv", [P, 6, S])
        xs = mb("xs", [P, MT, BLK])
        xd = mb("xd", [P, MT, BLK])
        xe = mb("xe", [P, BLK])
        yg = mb("yg", [P, MT, BLK])
        zs = mb("zs", [P, MT, BLK])
        cumb = mb("cumb", [P, R, S])
        m = mb("m", [P, MT, R, P])
        cbm = mb("cbm", [P, MT, P])
        bt = mb("bt", [P, NS])
        state = mb("state", [NS, BLK])
        causal = mb("causal", [P, P])
        ones = mb("ones", [P, P])
        hd = mb("hd", [P, 3, NH])
        dt = mb("dt", [P, MT, NH])
        da = mb("da", [P, MT, NH])
        cum = mb("cum", [P, MT, NH])
        todend = mb("todend", [P, NH])
        ecum = mb("ecum", [P, NH])
        tmp = mb("tmp", [P, 4, MT, NH])
        cumt = mb("cumt", [NH, S])
        cpar = mb("cpar", [P, TAPS + 1, 6])
        gpar = mb("gpar", [P, 4])
        gcum = mb("gcum", [P, MT, R])
        mem.close()

        mem = ExitStack()
        relu = mb("relu", [P, MT, BLK])
        sq = mb("sq", [P, MT, BLK])
        bhi.append(mb("bhi1", [P, 4, S], F32R))
        blo.append(mb("blo1", [P, 4, S], F32R))
        mem.close()

        mem = ExitStack()
        khi = mb("khi", [P, KT, S], F32R)
        klo = mb("klo", [P, KT, S], F32R)
        qt = mb("qt", [P, HG, S])
        kt_ = mb("kt", [P, HG, S])
        v = mb("v", [P, MT, BLK])
        tab = mb("tab", [P, HG, S])
        lg = [mb(f"lg{i}", [P, 2, S + P]) for i in range(2)]
        at = [mb(f"at{i}", [P, S + P]) for i in range(2)]
        att_t = mb("att_t", [P, S + P])
        ob = mb("ob", [P, MT, P])
        nmax = [mb(f"nmax{i}", [P, 4]) for i in range(2)]
        psum_ = [mb(f"psums{i}", [P, 4]) for i in range(2)]
        rinv = mb("rinv", [P, 4])
        mem.close()

        cum_dram = nc.dram_tensor("cum_scratch", [NH, S], F32, kind="Internal").ap()
        bias_dram = nc.dram_tensor("bias_scratch", [HEADS, P, S + P], F32, kind="Internal").ap()


        raw_in = [sem(f"raw_in{i}") for i in range(RING)]
        hi_ready, lo_ready, slab_used = sem("hi_ready"), sem("lo_ready"), sem("slab_used")
        consts_ready, small_in, x_in = sem("consts_ready"), sem("small_in"), sem("x_in")
        heads_in, rel_in, lam_in = sem("heads_in"), sem("rel_in"), sem("lam_in")
        par_t, par_ready = sem("par_t"), sem("par_ready")
        postw_in, cum_out, cumb_in, bias_out, tab_in = (
            sem("postw_in"), sem("cum_out"), sem("cumb_in"), sem("bias_out"), sem("tab_in"))
        y_zeroed, acc_added = sem("y_zeroed"), sem("acc_added")
        y_sq, h_new, h_sq, xn_ready = sem("y_sq"), sem("h_new"), sem("h_sq"), sem("xn_ready")
        xt_done, x_hi, x_lo = sem("xt_done"), sem("x_hi"), sem("x_lo")
        b_hi, h_ready = sem("b_hi"), sem("h_ready")
        dve_chain, act_chain, pool_chain = sem("dve_chain"), sem("act_chain"), sem("pool_chain")
        dt_done, dt_v, dt_e, dt_l, da_ready, cum_done, cum_ready = (
            sem("dt_done"), sem("dt_v"), sem("dt_e"), sem("dt_l"), sem("da_ready"), sem("cum_done"), sem("cum_ready"))
        cumt_done, cumt_ready, expd_ready = sem("cumt_done"), sem("cumt_ready"), sem("expd_ready")
        cpar_ready = sem("cpar_ready")
        pre_ready, conv_done, silu_done = sem("pre_ready"), sem("conv_done"), sem("silu_done")
        seg_done, decay_done = sem("seg_done"), sem("decay_done")
        spread_done, xs_ready, pool_ready, cb_ready, mt_ready = (
            sem("spread_done"), sem("xs_ready"), sem("pool_ready"), sem("cb_ready"), sem("mt_ready"))
        state_done, state_ready, y_done, zs_ready = (
            sem("state_done"), sem("state_ready"), sem("y_done"), sem("zs_ready"))
        gated, g_sq, g_ready, gt_done = sem("gated"), sem("g_sq"), sem("g_ready"), sem("gt_done")
        q_copied, k_copied, v_copied = sem("q_copied"), sem("k_copied"), sem("v_copied")
        lg_done, lg_ready, ex_ready, at_ready, at_t, at_copied = (
            sem("lg_done"), sem("lg_ready"), sem("ex_ready"), sem("at_ready"), sem("at_t"), sem("at_copied"))
        o_done, o_sq, o_ready, ot_done = sem("o_done"), sem("o_sq"), sem("o_ready"), sem("ot_done")
        lam_ready, lam_e, subw_ready = sem("lam_ready"), sem("lam_e"), sem("subw_ready")
        stored = sem("stored")

        block = ctx.enter_context(nc.Block())

        @block.sync
        def _(sp):
            def load(s, src, tiles):
                free = sp.lower_val(s.n + 1 - RING if isinstance(s.n, int) else sp.snap(s.n + 1 - RING))
                dst = raw[:, s.raw, :].rearrange("p (t n) -> p t n", t=tiles)
                dma = sp.dma_start(dst, src.rearrange("(t p) n -> p t n", p=P))
                if above(s.n, RING - 1):
                    dma.wait_op(lo_ready, free, "sem-ge")
                dma.then_inc(raw_in[s.raw], 16)

            def tile(mat, row, rows, col, cols):
                return mat[bass.ds(row, rows), bass.ds(col, cols)]

            def mix_load(s, unit, i, g):
                if unit == "xs":
                    load(s, tile(in_proj, 256 * i, 256, XBC0 + g * BLK, BLK), 2)
                elif unit == "bc":
                    load(s, tile(in_proj, 1024 * (i % 2), 1024, (B0, C0)[i // 2] + g * NS, NS), 8)
                elif unit == "z":
                    load(s, tile(in_proj, 256 * i, 256, g * BLK, BLK), 2)
                else:
                    load(s, tile(out_proj, (g - 1) * BLK + 256 * (i % 2), 256, BLK * (i // 2), BLK), 2)

            for t in range(MT):
                sp.dma_start(h[:, t, :], w["x"][0, t * P:(t + 1) * P, :]).then_inc(x_in, 16)
            load(mix.slab(0), in_proj[:, DT0:DT0 + NH], 16)
            for k, (unit, i) in enumerate(MIX_FIRST):
                mix_load(mix.slab(1 + k), unit, i, 0)
            with sp.Fori(0, G - 1) as t:
                for k, (unit, i) in enumerate(MIX_BODY):
                    mix_load(mix.slab(21 + k, t, 28), unit, i, t + 1)
            for k, (unit, i) in enumerate(ACC):
                mix_load(mix.slab(217 + k), unit, i, G)

            def mlp(ph, layer):
                w1, w2 = w["mlp_w1"][layer], w["mlp_w2"][layer]

                def up(s, i, b):
                    load(s, tile(w1, 256 * i, 256, b * BLK, BLK), 2)

                def down(s, i, b):
                    load(s, tile(w2, b * BLK + 256 * (i % 2), 256, BLK * (i // 2), BLK), 2)

                for k, (unit, i) in enumerate(MLP_FIRST):
                    up(ph.slab(k), i, 0)
                with sp.Fori(0, 7) as t:
                    for k, (unit, i) in enumerate(MLP_BODY):
                        s = ph.slab(8 + k, t, 32)
                        if unit == "up1":
                            up(s, i, 2 * t + 1)
                        elif unit == "up0":
                            up(s, i, 2 * t + 2)
                        else:
                            down(s, i, 2 * t + (unit == "acc1"))
                for k, (unit, i) in enumerate(MLP_LAST):
                    s = ph.slab(232 + k)
                    if unit == "up1":
                        up(s, i, 15)
                    else:
                        down(s, i, 14 + (unit == "acc1"))

            mlp(mlp0, 0)

            def att_load(s, unit, i, g):
                if unit == "acc":
                    load(s, tile(o_proj, (g - 1) * BLK + 256 * (i % 2), 256, BLK * (i // 2), BLK), 2)
                else:
                    load(s, tile({"q": w_q, "k": w_k, "v": w_v}[unit], 256 * i, 256, g * BLK, BLK), 2)

            for k, (unit, i) in enumerate(ATT_FIRST):
                att_load(att.slab(k), unit, i, 0)
            with sp.Fori(0, QG - 1) as t:
                for k, (unit, i) in enumerate(ATT_BODY):
                    att_load(att.slab(24 + k, t, 32), unit, i, t + 1)
            for k, (unit, i) in enumerate(ACC):
                att_load(att.slab(120 + k), unit, i, QG)
            mlp(mlp1, 1)
            for t in range(MT):
                sp.wait_ge(h_new, 6 + t + 1)
                sp.dma_start(out[0, t * P:(t + 1) * P, :], h[:, t, :]).then_inc(stored, 16)
            sp.wait_ge(stored, 16 * MT)

        @block.gpsimd
        def _(pool):
            chain = Tally(pool, pool_chain)
            g_ = nc.gpsimd

            def rows(dst, lo, vec):
                n = vec.shape[0] // P
                pool.dma_start(dst[lo:lo + n, :], vec.rearrange("(r c) -> r c", c=P)).then_inc(small_in, 16)

            chain.mark(g_.memset(par_rows[:, :, :], 0.0))
            chain.wait()
            for i in range(2):
                rows(par_rows[:, 0, :], 16 * i, w["norm_pre_mix"][i])
                rows(par_rows[:, 0, :], 32 + 16 * i, w["norm_pre_mlp"][i])
            rows(par_rows[:, 0, :], 64, w["kv_norm_w"])
            rows(par_rows[:, 0, :], 80, w["a_gate_norm_w"][0])
            rows(par_rows[:, 0, :], 112, w["b_subln_w"][0])
            for tap in range(TAPS):
                rows(par_rows[:, 1 + tap // 2, :], 48 * (tap % 2), w["a_conv_w"][0, tap])
            rows(par_rows[:, 3, :], 0, w["a_conv_b"][0])
            for i, name in enumerate(("a_dt_bias", "a_A_log", "a_D")):
                pool.dma_start(hd[:, i, :], w[name][0].partition_broadcast(P)).then_inc(heads_in, 16)
            for i, name in enumerate(("b_lambda_q1", "b_lambda_k1", "b_lambda_q2", "b_lambda_k2")):
                pool.dma_start(lamv[:, i, :], w[name][0].partition_broadcast(P)).then_inc(lam_in, 16)
            pool.dma_start(relrow[:, :], w["rel_bias"].rearrange("b h -> h b"), allow_slow_non_contiguous=True)\
                .then_inc(rel_in, 16)
            pool.dma_start(postw[:, :], w["norm_post_mix"][0].partition_broadcast(P)).then_inc(postw_in, 16)

            g_.memset(pre[:, :, 0:TAPS - 1], 0.0)
            g_.memset(ones[:, :], 1.0)
            chain.mark(g_.memset(ident[:, :], 0.0))
            chain.mark(g_.memset(causal[:, :], 1.0))
            chain.wait()
            g_.affine_select(out=ident[:, :], in_=ident[:, :], compare_op=ALU.not_equal, fill=1.0, base=0,
                             pattern=[[-1, P]], channel_multiplier=1)
            g_.affine_select(out=causal[:, :], in_=causal[:, :], compare_op=ALU.is_ge, fill=0.0, base=0,
                             pattern=[[1, P]], channel_multiplier=-1).then_inc(consts_ready, 1)

            pool.wait_ge(rel_in, 16)
            bounds = bucket_bounds()
            g_.memset(bias_row[:, S:S + P], MASKED)
            for b in range(BUCKETS):
                lo, hi = S - bounds[b + 1], S - bounds[b]
                last = g_.tensor_copy(bias_row[:, lo:hi], relrow[:, b:b + 1].to_broadcast([HEADS, hi - lo]))
            chain.mark(last)
            chain.wait()
            pool.dma_start(bias_dram, bias_row[:, :].unsqueeze(1).to_broadcast([HEADS, P, S + P])).then_inc(bias_out, 16)

            def zero_y(r):
                pool.wait_ge(xt_done, 8 * (r + 1))
                g_.memset(y[:, :, :], 0.0).then_inc(y_zeroed, 1)

            def next_postw(r, vec):
                pool.wait_ge(h_new, 2 * r)
                pool.dma_start(postw[:, :], vec.partition_broadcast(P)).then_inc(postw_in, 16)

            zero_y(0)

            def group(g):
                if above(g):
                    pool.wait_ge(silu_done, 2 * g)
                    pool.wait_ge(seg_done, g)
                for lo, n, at0 in ((0, 4, g * 4), (4, 1, 32 + g), (5, 1, 40 + g)):
                    for tp in range(TAPS + 1):
                        col = P * (1 + tp // 2) + 48 * (tp % 2)
                        g_.tensor_copy(cpar[:, tp, lo:lo + n], par[:, bass.ds(col + at0, n)])
                g_.tensor_copy(gcum[:, :, :], cum[:, :, bass.ds(g * R, R)]).then_inc(cpar_ready, 1)
                if not above(g):
                    pool.wait_ge(cumt_ready, 1)
                    pool.dma_start(cum_dram, cumt[:, :]).then_inc(cum_out, 16)
                    pool.wait_ge(cum_out, 16)
                src = cum_dram[bass.ds(g * R, R), :].rearrange("r s -> (r s)").partition_broadcast(P)
                pool.dma_start(cumb[:, :, :].rearrange("p r s -> p (r s)"), src).then_inc(cumb_in, 16)
                pool.wait_ge(xs_ready, g + 1)
                if above(g):
                    pool.wait_ge(gt_done, g)
                    pool.wait_ge(h_ready, g)
                chain.mark(g_.tensor_copy(gpar[:, :], par[:, bass.ds(80 + g * 4, 4)]))
                for c in range(MT):
                    last = g_.tensor_tensor(
                        out=xd[:, c, :].rearrange("p (r d) -> p r d", r=R), in0=xs[:, c, :].rearrange("p (r d) -> p r d", r=R),
                        in1=column_bcast(dt[:, c, bass.ds(g * R, R)], PD), op=ALU.mult)
                    chain.mark(last)
                    if c == 0:
                        chain.wait()
                        g_.tensor_tensor(out=xe[:, :].rearrange("p (r d) -> p r d", r=R),
                                         in0=xd[:, 0, :].rearrange("p (r d) -> p r d", r=R),
                                         in1=column_bcast(todend[:, bass.ds(g * R, R)], PD),
                                         op=ALU.mult)
                for c in range(MT):
                    last = g_.tensor_tensor(
                        out=yg[:, c, :].rearrange("p (r d) -> p r d", r=R), in0=xs[:, c, :].rearrange("p (r d) -> p r d", r=R),
                        in1=column_bcast(hd[:, 2, bass.ds(g * R, R)], PD), op=ALU.mult)
                last.then_inc(pool_ready, 1)

            pool.wait_ge(expd_ready, 1)
            pool.wait_ge(par_ready, 1)
            group(0)
            with pool.Fori(0, G - 1) as t:
                chain.enter(t, 3)
                group(t + 1)
            chain.leave(G - 1, 3)
            next_postw(1, w["norm_post_mlp"][0])
            zero_y(1)
            next_postw(2, w["norm_post_mix"][1])
            zero_y(2)

            def tab_load(g):
                src = bass.AP(tensor=bias_dram.tensor, offset=g * (HG * P * (S + P)) + P - 1,
                              ap=[[S + P - 1, P], [P * (S + P), HG], [1, S]])
                pool.dma_start(tab[:, :, :], src).then_inc(tab_in, 16)

            pool.wait_ge(bias_out, 16)
            pool.wait_ge(h_new, 4)
            tab_load(0)
            with pool.Fori(0, QG - 1) as t:
                pool.wait_ge(lg_ready, HG * (t + 1))
                tab_load(t + 1)
            next_postw(3, w["norm_post_mlp"][1])
            zero_y(3)
            pool.wait_ge(postw_in, 64)

        @block.scalar
        def _(act):
            chain = Tally(act, act_chain)
            sc = nc.scalar

            def split(s):
                act.wait_ge(raw_in[s.raw], s.arrived)
                if above(s.n, LEAD - 1):
                    act.wait_ge(slab_used, s.n - LEAD + 1)
                sc.activation(whi[:, s.split, :], raw[:, s.raw, :], ACT.Copy).then_inc(hi_ready, 1)

            def square_sum(t, src, dst, done):
                sc.activation(junk[:, t, 0:src.shape[-1]], src, ACT.Square, accum_out=dst).then_inc(done, 1)

            def normed(r, first_h, cols, outs):
                for t in range(MT):
                    if first_h:
                        act.wait_ge(x_in, 16 * MT)
                    else:
                        act.wait_ge(h_new, 2 * (r - 1) + t + 1)
                    square_sum(t, h[:, t, :], ssh[:, t:t + 1], h_sq)
                for i in range(KT // 2):
                    act.wait_ge(xt_done, 8 * r + i + 1)
                    for dst, col in zip(outs, cols):
                        for j in range(2):
                            k = 2 * i + j
                            last = sc.activation(dst[:, k, :], ps[:, i, j * S:(j + 1) * S], ACT.Copy,
                                                 scale=par[:, col + k:col + k + 1])
                    last.then_inc(x_hi, 1)

            def output_norm(ph):
                act.wait_ge(acc_added, NT * (ph.block0 + ph.blocks))
                for t in range(MT):
                    square_sum(t, y[:, t, :], ssy[:, t:t + 1], y_sq)

            def block_hi():
                for f in range(4):
                    last = sc.activation(bhi[0][:, f, :], ps[:, 5 + f // 2, (f % 2) * S:(f % 2 + 1) * S], ACT.Copy,
                                         scale=gpar[:, f:f + 1])
                last.then_inc(b_hi, 1)

            for k in range(LEAD):
                split(mix.slab(k))
            act.wait_ge(par_t, 1)
            sc.activation(par[:, :], ps[:, 0, :], ACT.Copy).then_inc(par_ready, 1)
            act.wait_ge(par_ready, 1)
            sc.mul(subw[:, :], par[:, 112:113], 1.0 - LAMBDA_INIT).then_inc(subw_ready, 1)
            normed(0, True, (0,), (xhi,))
            split(mix.slab(LEAD))
            act.wait_ge(dt_v, 1)
            sc.activation(tmp[:, 1, :, :], tmp[:, 0, :, :], ACT.Exp, scale=-1.0)
            sc.activation(hd[:, 1, :], hd[:, 1, :], ACT.Exp).then_inc(dt_e, 1)
            act.wait_ge(dt_l, 1)
            sc.activation(tmp[:, 3, :, :], tmp[:, 2, :, :], ACT.Ln).then_inc(dt_e, 1)
            act.wait_ge(lam_ready, 1)
            sc.activation(neglam[:, 2:4], neglam[:, 0:2], ACT.Exp).then_inc(lam_e, 1)

            def mix_step(first, g, unit, i):
                if (unit, i) == ("xs", 1) and not first:
                    act.wait_ge(gated, g)
                    for c in range(MT):
                        square_sum(c, yg[:, c, :], ssg[:, c:c + 1], g_sq)
                if (unit, i) == ("xs", 7):
                    if not first:
                        act.wait_ge(silu_done, 2 * g)
                    for b in range(2):
                        sc.activation(pre[:, 2 * b:2 * b + 2, TAPS - 1:], ps[:, b, :].rearrange("p (f s) -> p f s", f=2),
                                      ACT.Copy).then_inc(pre_ready, 1)
                    if first:
                        act.wait_ge(cum_ready, 1)
                        sc.activation(todend[:, :], todend[:, :], ACT.Exp)
                        sc.activation(ecum[:, :], cum[:, 1, :], ACT.Exp).then_inc(expd_ready, 1)
                    else:
                        act.wait_ge(gt_done, g)
                        block_hi()
                if (unit, i) == ("bc", 3):
                    sc.activation(pre[:, 4:6, TAPS - 1:], ps[:, 2, :].rearrange("p (f s) -> p f s", f=2),
                                  ACT.Copy).then_inc(pre_ready, 1)
                    act.wait_ge(conv_done, 2 * g + 1)
                    for f in range(4):
                        last = sc.activation(conv[:, f, :], conv[:, f, :], ACT.Silu, bias=cpar[:, TAPS, f:f + 1])
                    last.then_inc(silu_done, 1)
                if (unit, i) == SILU_BC[first]:
                    act.wait_ge(conv_done, 2 * g + 2)
                    for f in range(4, 6):
                        last = sc.activation(conv[:, f, :], conv[:, f, :], ACT.Silu, bias=cpar[:, TAPS, f:f + 1])
                    last.then_inc(silu_done, 1)
                if (unit, i) == DECAY[first]:
                    act.wait_ge(seg_done, g + 1)
                    for c in range(MT):
                        sc.activation(m[:, c, :, :], m[:, c, :, :], ACT.Exp).then_inc(decay_done, 1)
                if (unit, i) == SPREAD[first]:
                    act.wait_ge(spread_done, 2 * g + 1)
                    for c in range(MT):
                        last = sc.activation(xs[:, c, :], ps[:, c, :], ACT.Copy)
                    last.then_inc(xs_ready, 1)
                if (unit, i) == STATE[first]:
                    act.wait_ge(state_done, g + 1)
                    sc.activation(state[:, :], ps[:, 7, :], ACT.Copy).then_inc(state_ready, 1)
                if (unit, i) == ("z", 7):
                    sc.activation(zs[:, :, :], ps[:, 3:5, :], ACT.Silu).then_inc(zs_ready, 1)

            def steps(ph, first_k, order, body, t=0, per=0):
                for k, (unit, i) in enumerate(order):
                    ahead = ph.slab(first_k + k + LEAD, t, per)
                    if ahead:
                        split(ahead)
                        act.wait_ge(hi_ready, ahead.used)
                    else:
                        act.wait_ge(slab_used, ph.slab(first_k + k).used)
                    body(unit, i)

            steps(mix, 1, MIX_FIRST, lambda u, i: mix_step(True, 0, u, i))
            with act.Fori(0, G - 1) as t:
                steps(mix, 21, MIX_BODY, lambda u, i: mix_step(False, t + 1, u, i), t, 28)
            act.wait_ge(gated, G)
            for c in range(MT):
                square_sum(c, yg[:, c, :], ssg[:, c:c + 1], g_sq)
            act.wait_ge(gt_done, G)
            block_hi()
            steps(mix, 217, ACC, lambda u, i: None)
            output_norm(mix)

            def mlp(ph):
                def up(which, b):
                    if above(b):
                        act.wait_ge(h_ready, ph.features(b - 1))
                    for n in range(2):
                        chain.mark(sc.activation(relu[:, n, :], ps[:, n, :], ACT.Relu))
                    chain.wait()
                    for n in range(2):
                        last = sc.activation(bhi[which][:, 2 * n:2 * n + 2, :].rearrange("p f s -> p (f s)"),
                                             relu[:, n, :], ACT.Square)
                    last.then_inc(b_hi, 1)

                def step(unit, i, b):
                    if i == 7 and unit[:2] == "up":
                        up(int(unit[2:] or 0), b + {"up": 0, "up1": 1, "up0": 2}[unit])

                steps(ph, 0, MLP_FIRST, lambda u, i: step(u, i, 0))
                with act.Fori(0, 7) as t:
                    chain.enter(t, 4)
                    steps(ph, 8, MLP_BODY, lambda u, i: step(u, i, 2 * t), t, 32)
                chain.leave(7, 4)
                steps(ph, 232, MLP_LAST, lambda u, i: step(u, i, 14))
                output_norm(ph)

            normed(1, False, (32,), (xhi,))
            mlp(mlp0)
            normed(2, False, (16, 64), (xhi, khi))

            def attend(j, p):
                for i in range(HG):
                    n = HG * p + i
                    if j == 2 * i + 1:
                        act.wait_ge(lg_ready, n + 1)
                        for c in range(2):
                            sc.activation(lg[i % 2][:, c, 0:S], lg[i % 2][:, c, 0:S], ACT.Exp,
                                          bias=nmax[i % 2][:, c:c + 1], accum_out=psum_[i % 2][:, c:c + 1])
                            last = sc.activation(lg[i % 2][:, c, S:], lg[i % 2][:, c, S:], ACT.Exp,
                                                 bias=nmax[i % 2][:, 2 + c:3 + c], accum_out=psum_[i % 2][:, 2 + c:3 + c])
                        last.then_inc(ex_ready, 1)
                    if j == 2 * i + 4:
                        act.wait_ge(at_t, n + 1)
                        sc.activation(att_t[:, :], ps[:, 5, 0:S + P], ACT.Copy).then_inc(at_copied, 1)
                    if j == 2 * i + 6:
                        act.wait_ge(o_done, n + 1)
                        for c in range(MT):
                            square_sum(c, ps[:, 6, c * P:(c + 1) * P], ssa[:, c:c + 1], o_sq)
                    if j == 2 * i + 7:
                        act.wait_ge(ot_done, n + 1)
                        sc.activation(bhi[0][:, i, :], ps[:, 6, S:2 * S], ACT.Copy, scale=subw[:, :]).then_inc(b_hi, 1)

            def att_step(first, g, unit, i):
                if unit in "qk" and not first:
                    attend(i + 8 * (unit == "k"), g - 1)
                if i == 7 and unit == "q":
                    sc.activation(qt[:, :, :].rearrange("p f s -> p (f s)"), ps[:, 0:2, :].rearrange("p b n -> p (b n)"),
                                  ACT.Copy).then_inc(q_copied, 1)
                if i == 7 and unit == "k":
                    sc.activation(kt_[:, :, :].rearrange("p f s -> p (f s)"), ps[:, 3:5, :].rearrange("p b n -> p (b n)"),
                                  ACT.Copy).then_inc(k_copied, 1)
                if i == 7 and unit == "v":
                    sc.activation(v[:, :, :], ps[:, 5:7, :], ACT.Copy).then_inc(v_copied, 1)

            steps(att, 0, ATT_FIRST, lambda u, i: att_step(True, 0, u, i))
            with act.Fori(0, QG - 1) as t:
                steps(att, 24, ATT_BODY, lambda u, i: att_step(False, t + 1, u, i), t, 32)
            for j in range(16):
                attend(j, QG - 1)
            steps(att, 120, ACC, lambda u, i: None)
            output_norm(att)
            normed(3, False, (48,), (xhi,))
            mlp(mlp1)

        @block.vector
        def _(dve):
            chain = Tally(dve, dve_chain)
            ve = nc.vector

            def split(s):
                dve.wait_ge(hi_ready, s.n + 1)
                ve.tensor_tensor(out=wlo[:, s.split, :], in0=raw[:, s.raw, :], in1=whi[:, s.split, :].bitcast(F32),
                                 op=ALU.subtract).then_inc(lo_ready, 1)

            def link(ins):
                chain.mark(ins)
                chain.wait()

            def inverse_rms(dst, src, n, eps):
                c = src.shape[-1]
                x, a = rs_x[:, 0:c], rs_a[:, 0:c]
                link(ve.tensor_scalar(x, src, 1.0 / n, eps, ALU.mult, ALU.add))
                link(ve.tensor_scalar(a.bitcast(I32), x.bitcast(I32), 1, None, ALU.logical_shift_right))
                link(ve.tensor_scalar(dst.bitcast(I32), a.bitcast(I32), -1.0, float(0x5F3759DF), ALU.mult, ALU.add))
                for _ in range(3):
                    link(ve.tensor_tensor(out=a, in0=dst, in1=dst, op=ALU.mult))
                    link(ve.scalar_tensor_tensor(out=a, in0=a, scalar=-0.5, in1=x, op0=ALU.mult, op1=ALU.mult))
                    link(ve.scalar_tensor_tensor(out=dst, in0=a, scalar=1.5, in1=dst, op0=ALU.add, op1=ALU.mult))

            def steps(ph, first_k, order, body, t=0, per=0):
                for k, (unit, i) in enumerate(order):
                    ahead = ph.slab(first_k + k + LEAD, t, per)
                    if ahead:
                        split(ahead)
                        dve.wait_ge(lo_ready, ahead.used)
                    else:
                        dve.wait_ge(slab_used, ph.slab(first_k + k).used)
                    body(unit, i)

            def add_output(ph, b, i):
                if i % 2 == 0:
                    return
                nt = i // 2
                cols = y[:, :, nt * BLK:(nt + 1) * BLK]
                bank = 3 + 2 * (nt % 2)
                ve.tensor_tensor(out=cols, in0=cols, in1=ps[:, bank:bank + 2, :], op=ALU.add).then_inc(acc_added, 1)

            def normed(r, cols, his, los):
                for t in range(MT):
                    dve.wait_ge(h_sq, 2 * r + t + 1)
                    inverse_rms(rsh[:, t:t + 1], ssh[:, t:t + 1], D, 1e-6)
                    ve.tensor_scalar(y[:, t, :], h[:, t, :], rsh[:, t:t + 1], None, ALU.mult).then_inc(xn_ready, 1)
                for i in range(KT // 2):
                    dve.wait_ge(x_hi, 8 * r + i + 1)
                    for hi, lo, col in zip(his, los, cols):
                        for j in range(2):
                            k = 2 * i + j
                            last = ve.scalar_tensor_tensor(
                                out=lo[:, k, :], in0=ps[:, i, j * S:(j + 1) * S], scalar=par[:, col + k:col + k + 1],
                                in1=hi[:, k, :].bitcast(F32), op0=ALU.mult, op1=ALU.subtract)
                    last.then_inc(x_lo, 1)

            def residual(r):
                dve.wait_ge(postw_in, 16 * (r + 1))
                for t in range(MT):
                    dve.wait_ge(y_sq, 2 * r + t + 1)
                    inverse_rms(rsy[:, t:t + 1], ssy[:, t:t + 1], D, 1e-6)
                    link(ve.scalar_tensor_tensor(out=y[:, t, :], in0=y[:, t, :], scalar=rsy[:, t:t + 1],
                                                 in1=postw[:, :], op0=ALU.mult, op1=ALU.mult))
                    ve.tensor_tensor(out=h[:, t, :], in0=h[:, t, :], in1=y[:, t, :], op=ALU.add).then_inc(h_new, 1)

            def block_lo():
                for f in range(4):
                    last = ve.scalar_tensor_tensor(
                        out=blo[0][:, f, :], in0=ps[:, 5 + f // 2, (f % 2) * S:(f % 2 + 1) * S], scalar=gpar[:, f:f + 1],
                        in1=bhi[0][:, f, :].bitcast(F32), op0=ALU.mult, op1=ALU.subtract)
                last.then_inc(h_ready, 1)

            for k in range(LEAD):
                split(mix.slab(k))
            dve.wait_ge(par_ready, 1)
            normed(0, (0,), (xhi,), (xlo,))
            split(mix.slab(LEAD))

            dve.wait_ge(heads_in, 48)
            dve.wait_ge(slab_used, mix.slab(0).used)
            link(ve.tensor_tensor(out=dt[:, :, :], in0=ps[:, 7, 0:2 * NH].rearrange("p (c n) -> p c n", c=MT),
                                  in1=hd[:, 0, :].unsqueeze(1).to_broadcast([P, MT, NH]), op=ALU.add))
            link(ve.tensor_scalar(tmp[:, 0, :, :], dt[:, :, :], -1.0, None, ALU.mult))
            ve.tensor_tensor(out=tmp[:, 0, :, :], in0=tmp[:, 0, :, :], in1=dt[:, :, :], op=ALU.max).then_inc(dt_v, 1)
            link(ve.tensor_scalar(dt[:, :, :], dt[:, :, :], 0.0, None, ALU.max))
            dve.wait_ge(dt_e, 1)
            ve.tensor_scalar(tmp[:, 2, :, :], tmp[:, 1, :, :], 1.0, None, ALU.add).then_inc(dt_l, 1)
            dve.wait_ge(dt_l, 1)
            link(ve.tensor_scalar(tmp[:, 0, :, :], tmp[:, 2, :, :], 1.0, None, ALU.is_equal))
            dve.wait_ge(dt_e, 2)
            link(ve.scalar_tensor_tensor(out=tmp[:, 2, :, :], in0=tmp[:, 2, :, :], scalar=-1.0,
                                         in1=tmp[:, 0, :, :], op0=ALU.add, op1=ALU.add))
            link(ve.tensor_tensor(out=tmp[:, 3, :, :], in0=tmp[:, 3, :, :], in1=tmp[:, 0, :, :], op=ALU.add))
            link(ve.reciprocal(tmp[:, 2, :, :], tmp[:, 2, :, :]))
            link(ve.tensor_tensor(out=tmp[:, 3, :, :], in0=tmp[:, 3, :, :], in1=tmp[:, 1, :, :], op=ALU.mult))
            link(ve.tensor_tensor(out=tmp[:, 3, :, :], in0=tmp[:, 3, :, :], in1=tmp[:, 2, :, :], op=ALU.mult))
            link(ve.tensor_tensor(out=dt[:, :, :], in0=dt[:, :, :], in1=tmp[:, 3, :, :], op=ALU.add))
            ve.scalar_tensor_tensor(out=da[:, :, :], in0=dt[:, :, :], scalar=-1.0,
                                    in1=hd[:, 1, :].unsqueeze(1).to_broadcast([P, MT, NH]),
                                    op0=ALU.mult, op1=ALU.mult).then_inc(da_ready, 1)
            dve.wait_ge(lam_in, 64)
            for i in range(2):
                link(ve.tensor_tensor(out=lamv[:, 2 * i, :], in0=lamv[:, 2 * i, :], in1=lamv[:, 2 * i + 1, :], op=ALU.mult))
                last = ve.reduce_sum(neglam[:, i:i + 1], lamv[:, 2 * i, :], AX)
            last.then_inc(lam_ready, 1)
            dve.wait_ge(lam_e, 1)
            link(ve.tensor_tensor(out=neglam[:, 1:2], in0=neglam[:, 3:4], in1=neglam[:, 2:3], op=ALU.subtract))
            link(ve.tensor_scalar(neglam[:, 0:1], neglam[:, 1:2], -LAMBDA_INIT, None, ALU.add))

            def mix_cum():
                dve.wait_ge(cum_done, 1)
                link(ve.tensor_copy(cum[:, :, :], ps[:, 7, 0:2 * NH].rearrange("p (c n) -> p c n", c=MT)))
                ve.tensor_tensor(out=todend[:, :], in0=ps[:, 7, 2 * NH:3 * NH], in1=cum[:, 0, :],
                                 op=ALU.subtract).then_inc(cum_ready, 1)
                dve.wait_ge(cumt_done, 1)
                ve.tensor_copy(cumt[:, :], ps[0:NH, 7, 0:S]).then_inc(cumt_ready, 1)

            def mix_step(first, g, unit, i):
                if (unit, i) == ("xs", 2) and not first:
                    dve.wait_ge(g_sq, 2 * g)
                    inverse_rms(rsg, ssg, BLK, 1e-5)
                    for c in range(MT):
                        ve.tensor_scalar(yg[:, c, :], yg[:, c, :], rsg[:, c:c + 1], None, ALU.mult).then_inc(g_ready, 1)
                if (unit, i) == ("xs", 4) or (first and (unit, i) == ("z", 1)):
                    if first and unit == "xs":
                        return
                    dve.wait_ge(cumb_in, 16 * (g + 1))
                    dve.wait_ge(cpar_ready, g + 1)
                    if not first:
                        dve.wait_ge(y_done, g)
                    for c in range(MT):
                        for r in range(R):
                            last = ve.tensor_scalar(m[:, c, r, :], cumb[:, r, c * P:(c + 1) * P], gcum[:, c, r:r + 1], 0.0,
                                                    ALU.subtract, ALU.min)
                    last.then_inc(seg_done, 1)
                if (unit, i) in (("xs", 7), ("bc", 3)):
                    lo, hi = (0, 4) if unit == "xs" else (4, 6)
                    if (unit, i) == ("xs", 7) and not first:
                        dve.wait_ge(b_hi, g)
                        block_lo()
                    if first and unit == "xs":
                        mix_cum()
                    dve.wait_ge(cpar_ready, g + 1)
                    dve.wait_ge(pre_ready, 3 * g + (2 if unit == "xs" else 3))
                    if not first:
                        dve.wait_ge(spread_done, 2 * g)
                        dve.wait_ge(y_done, g)
                    for f in range(lo, hi):
                        chain.mark(ve.tensor_scalar(conv[:, f, :], pre[:, f, 0:S], cpar[:, 0, f:f + 1], None, ALU.mult))
                    for tap in range(1, TAPS):
                        for f in range(lo, hi):
                            chain.wait(back=hi - lo - 1)
                            ins = ve.scalar_tensor_tensor(
                                out=conv[:, f, :], in0=pre[:, f, tap:tap + S], scalar=cpar[:, tap, f:f + 1],
                                in1=conv[:, f, :], op0=ALU.mult, op1=ALU.add)
                            if (tap, f) == (TAPS - 1, hi - 1):
                                ins.then_inc(conv_done, 1)
                            else:
                                chain.mark(ins)
                if unit == "acc":
                    add_output(mix, g - 1, i)
                if (unit, i) == SPREAD[first]:
                    dve.wait_ge(spread_done, 2 * g + 2)
                    ve.tensor_copy(bt[:, :], ps[:, 2, 0:P])
                    ve.tensor_tensor(out=cbm[:, :, :], in0=ps[:, 2, P:3 * P].rearrange("p (c i) -> p c i", c=MT),
                                     in1=causal[:, :].unsqueeze(1).to_broadcast([P, MT, P]), op=ALU.mult)\
                        .then_inc(cb_ready, 1)
                    dve.wait_ge(cb_ready, g + 1)
                    for c in range(MT):
                        dve.wait_ge(decay_done, 2 * g + c + 1)
                        ve.tensor_tensor(out=m[:, c, :, :], in0=m[:, c, :, :],
                                         in1=cbm[:, c, :].unsqueeze(1).to_broadcast([P, R, P]), op=ALU.mult)\
                            .then_inc(mt_ready, 1)
                if (unit, i) == ("z", 7):
                    dve.wait_ge(y_done, g + 1)
                    dve.wait_ge(pool_ready, g + 1)
                    by_head = lambda ap: ap.rearrange("p (r d) -> p r d", r=R)
                    chain.mark(ve.tensor_tensor(out=by_head(xd[:, 1, :]), in0=by_head(ps[:, 6, :]),
                                                in1=column_bcast(ecum[:, bass.ds(g * R, R)], PD), op=ALU.mult))
                    chain.mark(ve.tensor_tensor(out=yg[:, :, :], in0=yg[:, :, :], in1=ps[:, 0:2, :], op=ALU.add))
                    chain.wait()
                    link(ve.tensor_tensor(out=yg[:, 1, :], in0=yg[:, 1, :], in1=xd[:, 1, :], op=ALU.add))
                    dve.wait_ge(zs_ready, g + 1)
                    ve.tensor_tensor(out=yg[:, :, :], in0=yg[:, :, :], in1=zs[:, :, :], op=ALU.mult).then_inc(gated, 1)

            dve.wait_ge(y_zeroed, 1)
            steps(mix, 1, MIX_FIRST, lambda u, i: mix_step(True, 0, u, i))
            with dve.Fori(0, G - 1) as t:
                chain.enter(t, 37)
                steps(mix, 21, MIX_BODY, lambda u, i: mix_step(False, t + 1, u, i), t, 28)
            chain.leave(G - 1, 37)
            dve.wait_ge(g_sq, 2 * G)
            inverse_rms(rsg, ssg, BLK, 1e-5)
            for c in range(MT):
                ve.tensor_scalar(yg[:, c, :], yg[:, c, :], rsg[:, c:c + 1], None, ALU.mult).then_inc(g_ready, 1)
            dve.wait_ge(b_hi, G)
            block_lo()
            steps(mix, 217, ACC, lambda u, i: add_output(mix, G - 1, i))
            residual(0)
            normed(1, (32,), (xhi,), (xlo,))

            def mlp(ph, r):
                def up(which, b):
                    dve.wait_ge(b_hi, ph.features(b))
                    for n in range(2):
                        chain.mark(ve.tensor_tensor(out=sq[:, n, :], in0=relu[:, n, :], in1=relu[:, n, :], op=ALU.mult))
                    for n in range(2):
                        chain.wait(back=1 - n)
                        last = ve.tensor_tensor(
                            out=blo[which][:, 2 * n:2 * n + 2, :].rearrange("p f s -> p (f s)"), in0=sq[:, n, :],
                            in1=bhi[which][:, 2 * n:2 * n + 2, :].rearrange("p f s -> p (f s)").bitcast(F32), op=ALU.subtract)
                    last.then_inc(h_ready, 1)

                def step(unit, i, b):
                    if unit[:2] == "up" and i == 7:
                        up(int(unit[2:] or 0), b + {"up": 0, "up1": 1, "up0": 2}[unit])
                    if unit[:3] == "acc":
                        add_output(ph, b + int(unit[3:]), i)

                dve.wait_ge(y_zeroed, r + 1)
                steps(ph, 0, MLP_FIRST, lambda u, i: step(u, i, 0))
                with dve.Fori(0, 7) as t:
                    chain.enter(t, 4)
                    steps(ph, 8, MLP_BODY, lambda u, i: step(u, i, 2 * t), t, 32)
                chain.leave(7, 4)
                steps(ph, 232, MLP_LAST, lambda u, i: step(u, i, 14))

            mlp(mlp0, 1)
            residual(1)
            normed(2, (16, 64), (xhi, khi), (xlo, klo))

            def attend(j, p):
                for i in range(HG):
                    n = HG * p + i
                    if j == 2 * i:
                        dve.wait_ge(lg_done, n + 1)
                        dve.wait_ge(tab_in, 16 * (p + 1))
                        l = lg[i % 2]
                        for cols, bias in ((slice(0, S), tab[:, i, :]), (slice(S, S + P), tab[:, i, P:])):
                            for c in range(2):
                                last = ve.scalar_tensor_tensor(out=l[:, c, cols], in0=ps[:, 2 + 5 * c, cols], scalar=DH ** -0.5,
                                                               in1=bias, op0=ALU.mult, op1=ALU.add)
                            chain.mark(last)
                        chain.wait(back=1)
                        ve.tensor_reduce(nmax[i % 2][:, 0:2], l[:, :, 0:S], AX, ALU.max, negate=True)
                        chain.wait()
                        ve.tensor_reduce(nmax[i % 2][:, 2:4], l[:, :, S:], AX, ALU.max, negate=True).then_inc(lg_ready, 1)
                    if j == 2 * i + 2:
                        dve.wait_ge(ex_ready, n + 1)
                        if i >= 2:
                            dve.wait_ge(at_t, n - 1)
                        l, a = lg[i % 2], at[i % 2]
                        link(ve.reciprocal(rinv[:, :], psum_[i % 2][:, :]))
                        link(ve.tensor_tensor(out=rinv[:, 1:4:2], in0=rinv[:, 1:4:2],
                                              in1=neglam[:, 0:1].to_broadcast([P, 2]), op=ALU.mult))
                        for q, cols in enumerate((slice(0, S), slice(S, S + P))):
                            chain.mark(ve.tensor_scalar(l[:, 1, cols], l[:, 1, cols], rinv[:, 2 * q + 1:2 * q + 2], None,
                                                        ALU.mult))
                        for q, cols in enumerate((slice(0, S), slice(S, S + P))):
                            chain.wait(back=1 - q)
                            last = ve.scalar_tensor_tensor(out=a[:, cols], in0=l[:, 0, cols], scalar=rinv[:, 2 * q:2 * q + 1],
                                                           in1=l[:, 1, cols], op0=ALU.mult, op1=ALU.add)
                        last.then_inc(at_ready, 1)
                    if j == 2 * i + 6:
                        dve.wait_ge(o_sq, 2 * n + 2)
                        inverse_rms(rsa, ssa, P, 1e-5)
                        ve.tensor_tensor(out=ob[:, :, :], in0=ps[:, 6, 0:S].rearrange("p (c e) -> p c e", c=MT),
                                         in1=column_bcast(rsa, P), op=ALU.mult).then_inc(o_ready, 1)
                    if j == 2 * i + 7:
                        dve.wait_ge(b_hi, att.ready0 + n + 1)
                        ve.scalar_tensor_tensor(out=blo[0][:, i, :], in0=ps[:, 6, S:2 * S], scalar=subw[:, :],
                                                in1=bhi[0][:, i, :].bitcast(F32), op0=ALU.mult, op1=ALU.subtract)\
                            .then_inc(h_ready, 1)

            def att_step(first, g, unit, i):
                if unit in "qk" and not first:
                    attend(i + 8 * (unit == "k"), g - 1)
                if unit == "acc":
                    add_output(att, g - 1, i)

            dve.wait_ge(y_zeroed, 3)
            dve.wait_ge(subw_ready, 1)
            steps(att, 0, ATT_FIRST, lambda u, i: att_step(True, 0, u, i))
            with dve.Fori(0, QG - 1) as t:
                chain.enter(t, 72)
                steps(att, 24, ATT_BODY, lambda u, i: att_step(False, t + 1, u, i), t, 32)
            chain.leave(QG - 1, 72)
            for j in range(16):
                attend(j, QG - 1)
            steps(att, 120, ACC, lambda u, i: add_output(att, QG - 1, i))
            residual(2)
            normed(3, (48,), (xhi,), (xlo,))
            mlp(mlp1, 3)
            residual(3)

        @block.tensor
        def _(pe):
            te = nc.tensor

            def three(outs, lhs, rhs, start, stop):
                (lh, ll), (rh, rl) = lhs, rhs
                te.matmul(outs, lh, rh, start=start, stop=False, skip_group_check=True)
                te.matmul(outs, lh, rl, start=False, stop=False, skip_group_check=True)
                return te.matmul(outs, ll, rh, start=False, stop=stop, skip_group_check=True)

            def slot(s, tiles):
                return [t[:, s.split, :].rearrange("p (t n) -> p t n", t=tiles) for t in (whi, wlo)]

            def feature_major(s, i, bank, x, tiles=2, cols=BLK, half=0, last_i=7):
                pe.wait_ge(lo_ready, s.n + 1)
                wh, wl = slot(s, tiles)
                for f in range(cols // P):
                    for j in range(tiles):
                        k = i * tiles + j
                        dst = ps[:, bank + f // 2, (f % 2 + half) * S:(f % 2 + half + 1) * S]
                        c = slice(f * P, (f + 1) * P)
                        last = three(dst, (wh[:, j, c], wl[:, j, c]), (x[0][:, k, :], x[1][:, k, :]),
                                     start=(k == 0 and f % 2 + half == 0), stop=(i == last_i and j == tiles - 1))
                last.then_inc(slab_used, 1)

            def token_major(s, i, slabs, bank, x, tiles=2, cols=BLK):
                pe.wait_ge(lo_ready, s.n + 1)
                wh, wl = slot(s, tiles)
                for t in range(MT):
                    for j in range(tiles):
                        k = i * tiles + j
                        c = slice(t * P, (t + 1) * P)
                        if cols == BLK:
                            dst, start = ps[:, bank + t, :], k == 0
                        else:
                            dst, start = ps[:, bank, t * cols:(t + 1) * cols], k == 0 and t == 0
                        last = three(dst, (x[0][:, k, c], x[1][:, k, c]), (wh[:, j, :], wl[:, j, :]),
                                     start=start, stop=(i == slabs - 1 and j == tiles - 1))
                last.then_inc(slab_used, 1)

            def output(ph, s, i, b, which=0):
                nt = i // 2
                if i == 0:
                    pe.wait_ge(h_ready, ph.features(b))
                a = 4 * (ph.block0 + b) + nt
                if i % 2 == 0 and (nt >= 2 or ph in (mlp0, mlp1)):
                    pe.wait_ge(acc_added, a - 1)
                token_major(s, i % 2, 2, 3 + 2 * (nt % 2), (bhi[which], blo[which]))

            def transpose_x(r):
                pe.wait_ge(xn_ready, 2 * (r + 1))
                for i in range(KT // 2):
                    for j in range(2):
                        for t in range(MT):
                            k = 2 * i + j
                            last = te.transpose(ps[:, i, j * S + t * P:j * S + (t + 1) * P], y[:, t, k * P:(k + 1) * P],
                                                ident[:, :])
                    last.then_inc(xt_done, 1)

            x, xk = (xhi, xlo), (khi, klo)

            pe.wait_ge(consts_ready, 1)
            pe.wait_ge(small_in, 16 * 12)
            for i in range(4):
                last = te.transpose(ps[:, 0, i * P:(i + 1) * P], par_rows[:, i, :], ident[:, :])
            last.then_inc(par_t, 1)
            pe.wait_ge(par_ready, 1)
            transpose_x(0)
            pe.wait_ge(x_lo, 8)
            token_major(mix.slab(0), 0, 1, 7, x, tiles=16, cols=NH)

            def spread(g):
                pe.wait_ge(silu_done, 2 * g + 2)
                for c in range(MT):
                    for f in range(4):
                        last = te.transpose(ps[:, c, f * P:(f + 1) * P], conv[:, f, c * P:(c + 1) * P], ident[:, :])
                last.then_inc(spread_done, 1)
                te.transpose(ps[:, 2, 0:P], conv[:, 4, 0:P], ident[:, :])
                for c in range(MT):
                    cs = slice(c * P, (c + 1) * P)
                    last = te.matmul(ps[:, 2, (c + 1) * P:(c + 2) * P], conv[:, 4, cs], conv[:, 5, cs],
                                     start=True, stop=True, skip_group_check=True)
                last.then_inc(spread_done, 1)

            def mix_step(first, g, unit, i, s):
                if unit == "xs":
                    if i == 0 and not first:
                        pe.wait_ge(gated, g)
                    feature_major(s, i, 0, x)
                if unit == "bc":
                    feature_major(s, i % 2, 2, x, tiles=8, cols=P, half=i // 2, last_i=1)
                if unit == "z":
                    if i == 0 and not first:
                        pe.wait_ge(acc_added, 4 * g - 1)
                    token_major(s, i, 8, 3, x)
                if unit == "acc":
                    output(mix, s, i, g - 1)
                if (unit, i) == ("xs", 7) and not first:
                    transpose_block(g)
                if first and (unit, i) == ("xs", 3):
                    decays()
                if (unit, i) == SPREAD[first]:
                    spread(g)
                if (unit, i) == STATE[first]:
                    pe.wait_ge(cb_ready, g + 1)
                    pe.wait_ge(pool_ready, g + 1)
                    te.matmul(ps[:, 7, :], bt[:, :], xe[:, :], start=True, stop=True).then_inc(state_done, 1)
                if (unit, i) == ("z", 7):
                    for c in range(MT):
                        pe.wait_ge(mt_ready, 2 * g + c + 1)
                        for r in range(R):
                            te.matmul(ps[:, c, r * PD:(r + 1) * PD], m[:, c, r, :], xd[:, c, r * PD:(r + 1) * PD],
                                      start=True, stop=True, skip_group_check=True)
                    pe.wait_ge(state_ready, g + 1)
                    if not first:
                        pe.wait_ge(acc_added, 4 * g)
                    te.matmul(ps[:, 6, :], conv[:, 5, P:], state[:, :], start=True, stop=True).then_inc(y_done, 1)

            def decays():
                pe.wait_ge(da_ready, 1)
                for c in range(MT):
                    te.matmul(ps[:, 7, c * NH:(c + 1) * NH], causal[:, :], da[:, c, :], start=True, stop=True,
                              skip_group_check=True)
                te.matmul(ps[:, 7, 2 * NH:3 * NH], ones[:, :], da[:, 0, :], start=True, stop=True,
                          skip_group_check=True).then_inc(cum_done, 1)

            def transpose_block(g):
                pe.wait_ge(g_ready, 2 * g)
                for c in range(MT):
                    for f in range(4):
                        last = te.transpose(ps[:, 5 + f // 2, (f % 2) * S + c * P:(f % 2) * S + (c + 1) * P],
                                            yg[:, c, f * P:(f + 1) * P], ident[:, :])
                last.then_inc(gt_done, 1)

            for k, (unit, i) in enumerate(MIX_FIRST):
                mix_step(True, 0, unit, i, mix.slab(1 + k))
                if (unit, i) == ("xs", 7):
                    pe.wait_ge(cum_ready, 1)
                    for c in range(MT):
                        last = te.transpose(ps[0:NH, 7, c * P:(c + 1) * P], cum[:, c, :], ident[:, :])
                    last.then_inc(cumt_done, 1)
            with pe.Fori(0, G - 1) as t:
                for k, (unit, i) in enumerate(MIX_BODY):
                    mix_step(False, t + 1, unit, i, mix.slab(21 + k, t, 28))
            transpose_block(G)
            for k, (unit, i) in enumerate(ACC):
                output(mix, mix.slab(217 + k), i, G - 1)
            transpose_x(1)

            def mlp(ph, r):
                def up(s, i, b):
                    if i == 0 and above(b):
                        pe.wait_ge(b_hi, ph.features(b - 1))
                    feature_major(s, i, 0, x)

                def step(unit, i, b, s):
                    if unit[:2] == "up":
                        up(s, i, b + {"up": 0, "up1": 1, "up0": 2}[unit])
                    else:
                        output(ph, s, i, b + int(unit[3:]), int(unit[3:]))

                pe.wait_ge(x_lo, 8 * (r + 1))
                for k, (unit, i) in enumerate(MLP_FIRST):
                    step(unit, i, 0, ph.slab(k))
                with pe.Fori(0, 7) as t:
                    for k, (unit, i) in enumerate(MLP_BODY):
                        step(unit, i, 2 * t, ph.slab(8 + k, t, 32))
                for k, (unit, i) in enumerate(MLP_LAST):
                    step(unit, i, 14, ph.slab(232 + k))

            mlp(mlp0, 1)
            transpose_x(2)

            def attend(j, p):
                for i in range(HG):
                    n = HG * p + i
                    if j == 2 * i:
                        if i > 0:
                            pe.wait_ge(lg_ready, n)
                        for c in range(2):
                            cs = slice(c * DH, (c + 1) * DH)
                            te.matmul(ps[:, 2 + 5 * c, 0:S], qt[cs, i, P:], kt_[cs, i, :], start=True, stop=True,
                                      skip_group_check=True)
                            last = te.matmul(ps[:, 2 + 5 * c, S:S + P], qt[cs, i, 0:P], kt_[cs, i, 0:P], start=True,
                                             stop=True, skip_group_check=True)
                        last.then_inc(lg_done, 1)
                    if j == 2 * i + 6:
                        pe.wait_ge(at_copied, n + 1)
                        if above(n):
                            pe.wait_ge(h_ready, att.ready0 + n)
                        te.matmul(ps[:, 6, P:2 * P], att_t[:, 0:P], v[:, 0, i * P:(i + 1) * P], start=True, stop=False,
                                  skip_group_check=True)
                        te.matmul(ps[:, 6, P:2 * P], att_t[:, P:2 * P], v[:, 1, i * P:(i + 1) * P], start=False, stop=True,
                                  skip_group_check=True)
                        te.matmul(ps[:, 6, 0:P], att_t[:, 2 * P:], v[:, 0, i * P:(i + 1) * P], start=True, stop=True,
                                  skip_group_check=True).then_inc(o_done, 1)
                    if j == 2 * i + 4:
                        pe.wait_ge(at_ready, n + 1)
                        if i > 0:
                            pe.wait_ge(at_copied, n)
                        for b in range(3):
                            last = te.transpose(ps[:, 5, b * P:(b + 1) * P], at[i % 2][:, b * P:(b + 1) * P], ident[:, :])
                        last.then_inc(at_t, 1)
                    if j == 2 * i + 7:
                        pe.wait_ge(o_ready, n + 1)
                        for c in range(MT):
                            last = te.transpose(ps[:, 6, S + c * P:S + (c + 1) * P], ob[:, c, :], ident[:, :])
                        last.then_inc(ot_done, 1)

            def att_step(first, g, unit, i, s):
                if unit == "q":
                    feature_major(s, i, 0, x)
                if unit == "k":
                    feature_major(s, i, 3, xk)
                if unit == "v":
                    if i == 0 and not first:
                        pe.wait_ge(h_ready, att.features(g - 1))
                    token_major(s, i, 8, 5, xk)
                if unit == "acc":
                    if i == 0:
                        pe.wait_ge(k_copied, g + 1)
                    if i == 2:
                        pe.wait_ge(v_copied, g + 1)
                    output(att, s, i, g - 1)
                if unit in "qk" and not first:
                    if (unit, i) == ("q", 0):
                        pe.wait_ge(v_copied, g)
                    if (unit, i) == ("q", 3):
                        pe.wait_ge(acc_added, NT * (att.block0 + g - 1))
                    attend(i + 8 * (unit == "k"), g - 1)

            pe.wait_ge(x_lo, 24)
            for k, (unit, i) in enumerate(ATT_FIRST):
                att_step(True, 0, unit, i, att.slab(k))
            with pe.Fori(0, QG - 1) as t:
                for k, (unit, i) in enumerate(ATT_BODY):
                    att_step(False, t + 1, unit, i, att.slab(24 + k, t, 32))
            pe.wait_ge(v_copied, QG)
            for j in range(16):
                attend(j, QG - 1)
            for k, (unit, i) in enumerate(ACC):
                output(att, att.slab(120 + k), i, QG - 1)
            transpose_x(3)
            mlp(mlp1, 3)


INPUTS = ["x", "a_in_proj", "a_conv_w", "a_conv_b", "a_dt_bias", "a_A_log", "a_D", "a_gate_norm_w", "a_out_proj",
          "kv_norm_w", "w_k", "w_v", "rel_bias", "b_w_q", "b_lambda_q1", "b_lambda_k1", "b_lambda_q2", "b_lambda_k2",
          "b_subln_w", "b_out_proj", "norm_pre_mix", "norm_post_mix", "norm_pre_mlp", "norm_post_mlp",
          "mlp_w1", "mlp_w2"]


def kernel(**inputs):
    import concourse.bacc as bacc
    from concourse.bass_utils import run_bass_kernel_spmd

    nc = bacc.Bacc("TRN2", target_bir_lowering=False, num_devices=1)
    arrays, aps = {}, {}
    for name in INPUTS:
        arrays[name] = np.ascontiguousarray(inputs[name])
        aps[name] = nc.dram_tensor(name, arrays[name].shape, mybir.dt.from_np(arrays[name].dtype),
                                   kind="ExternalInput").ap()
    out = nc.dram_tensor("out", (1, S, D), F32, kind="ExternalOutput").ap()
    build(nc, aps, out)
    return run_bass_kernel_spmd(nc, [arrays], core_ids=[0]).results[0]["out"]
```

```python
from contextlib import ExitStack

import numpy as np
import concourse.bass as bass
from concourse import mybir

F32 = mybir.dt.float32
F32R = mybir.dt.float32r
I32 = mybir.dt.int32
BF16 = mybir.dt.bfloat16
ALU = mybir.AluOpType
ACT = mybir.ActivationFunctionType
AX = mybir.AxisListType.X

P = 128
D = 2048
S = 256
MT = S // P
DI = 2 * D
G = 8
R = 8
PD = 64
NS = 128
NH = G * R
TAPS = 4
XBC0 = DI
B0 = XBC0 + DI
C0 = B0 + G * NS
DT0 = C0 + G * NS
HEADS = 16
HG = 4
QG = HEADS // HG
DH = 64
FF = 4 * D
BLK = 512
KT = D // P
NT = D // BLK
PIECES = 4
BUCKETS = 32
MAX_DISTANCE = 128
LAMBDA_INIT = 0.8 - 0.6 * float(np.exp(-0.3))
MASKED = -1.0e30
LEAD = 4
SLAB = 1024
SMALL_LOADS = 10
RING = 4


def bucket_bounds():
    exact = BUCKETS // 2
    n = np.arange(S)
    large = exact + (np.log(np.maximum(n, 1).astype(np.float32) / exact)
                     / np.float32(np.log(MAX_DISTANCE / exact)) * (BUCKETS - exact)).astype(np.int32)
    bucket = np.where(n < exact, n, np.minimum(large, BUCKETS - 1))
    return [int(np.argmax(bucket >= b)) for b in range(BUCKETS)] + [S]


class Slab:

    def __init__(self, n, number):
        self.n = number
        self.raw, self.split = n % RING, n % LEAD
        self.used = number + 1
        self.arrived = 16 * (n // RING + 1)


class Phase:

    def __init__(self, slabs, blocks, before, per_block=1):
        self.slabs, self.blocks, self.per_block, self.next = slabs, blocks, per_block, None
        self.first = self.block0 = self.ready0 = 0
        if before:
            before.next = self
            self.first = before.first + before.slabs
            self.block0 = before.block0 + before.blocks
            self.ready0 = before.ready0 + before.blocks * before.per_block

    def slab(self, k, t=0, per=0):
        if per == 0 and k >= self.slabs:
            return self.next.slab(k - self.slabs) if self.next else None
        assert per % LEAD == 0 and per % RING == 0
        n = self.first + k
        slab = Slab(n, n + t * per)
        slab.arrived += t * (16 * per // RING)
        return slab

    def features(self, b):
        return self.ready0 + self.per_block * (b + 1)


def above(value, floor=0):
    return not isinstance(value, int) or value > floor


class Tally:

    def __init__(self, engine, sem):
        self.engine, self.sem, self.base, self.k, self.at = engine, sem, 0, 0, 0

    def mark(self, ins):
        ins.then_inc(self.sem, 1)
        self.k += 1

    def wait(self, back=0):
        self.engine.wait_ge(self.sem, self.at + self.k - back)

    def enter(self, t, per):
        self.base, self.k = self.base + self.k, 0
        self.at = self.base + t * per

    def leave(self, trips, per):
        assert self.k == per, f"{self.k} marks in the loop body, not {per}"
        self.base, self.k = self.base + per * trips, 0
        self.at = self.base


def column_bcast(ap, n):
    return ap.unsqueeze(2).to_broadcast([ap.shape[0], ap.shape[1], n])


def piece(n):
    return slice(n * D // PIECES, (n + 1) * D // PIECES)


def build(nc, w, out):
    mix = Phase(1 + 20 + 7 * 28 + 8, G, None)
    mlp0 = Phase(8 + 7 * 32 + 24, FF // BLK, mix)
    att = Phase(24 + 3 * 32 + 8, QG, mlp0, per_block=HG)
    mlp1 = Phase(8 + 7 * 32 + 24, FF // BLK, att)

    in_proj, out_proj = w["a_in_proj"][0], w["a_out_proj"][0]
    w_q, w_k, w_v, o_proj = w["b_w_q"][0], w["w_k"], w["w_v"], w["b_out_proj"][0]

    def units(*names):
        return [(n, i) for n, c in names for i in range(c)]

    MIX_FIRST = units(("xs", 8), ("bc", 4), ("z", 8))
    MIX_BODY = units(("xs", 8), ("bc", 4), ("acc", 8), ("z", 8))
    ACC = units(("acc", 8))
    MLP_FIRST = units(("up", 8))
    MLP_BODY = units(("up1", 8), ("acc0", 8), ("up0", 8), ("acc1", 8))
    MLP_LAST = units(("up1", 8), ("acc0", 8), ("acc1", 8))
    ATT_FIRST = units(("q", 8), ("k", 8), ("v", 8))
    ATT_BODY = units(("q", 8), ("k", 8), ("v", 8), ("acc", 8))
    SPREAD = {True: ("z", 3), False: ("acc", 7)}
    STATE = {True: ("z", 6), False: ("z", 3)}
    SILU_BC = {True: ("z", 0), False: ("acc", 0)}
    HEADS_AT = ((0, 3, 5, 7), (9, 11, 13, 15))
    LAST_AT = ((0, 2, 4, 6), (8, 10, 12, 14))
    DECAY = {True: ("z", 4), False: ("acc", 3)}
    INTRA = {True: ("z", 4), False: ("acc", 7)}

    ctx = ExitStack()
    with ctx:
        def sb(name, shape, dt=F32, stack=ctx):
            return stack.enter_context(nc.sbuf_tensor(name, shape, dt))

        def sem(name):
            return ctx.enter_context(nc.semaphore(name))

        h = sb("h", [P, MT, D])
        y = sb("y", [P, MT, D])
        raw = sb("raw", [P, RING, SLAB])
        whi = sb("whi", [P, LEAD, SLAB], F32R)
        wlo = sb("wlo", [P, LEAD, SLAB], F32R)
        xhi = sb("xhi", [P, KT, S], F32R)
        xlo = sb("xlo", [P, KT, S], F32R)
        bhi = [sb("bhi0", [P, 4, S], F32R)]
        blo = [sb("blo0", [P, 4, S], F32R)]
        postw = sb("postw", [P, D])
        junk = sb("junk", [P, MT, D], BF16)
        ident = sb("ident", [P, P])
        par = sb("par", [P, 4 * P])
        subw = sb("subw", [P, 1])
        diag = sb("diag", [P, MT, P])
        part = sb("part", [P, MT, NT + PIECES])
        ssy, ssh = part[:, :, 0:NT], part[:, :, NT:]
        stat = sb("stat", [P, 24])
        sum_y, sum_h, rsy, rsh, ssg, rsg, ssa, rsa, rs_x, rs_h, rs_a = (stat[:, 2 * i:2 * i + 2] for i in range(11))
        neglam = sb("neglam", [P, 4])
        relrow = sb("relrow", [HEADS, BUCKETS])
        bias_row = sb("bias_row", [HEADS, S + P])
        lamv = sb("lamv", [P, 4, DH])
        ps = ctx.enter_context(nc.psum_tensor("ps", [P, 8, BLK], F32))

        mem = ExitStack()

        def mb(name, shape, dt=F32):
            return sb(name, shape, dt, mem)

        par_rows = mb("par_rows", [P, 4, P])
        pre = mb("pre", [P, 6, TAPS - 1 + S])
        conv = mb("conv", [P, 6, S])
        xs = mb("xs", [P, MT, BLK])
        xd = mb("xd", [P, MT, BLK])
        xe = mb("xe", [P, BLK])
        yg = mb("yg", [P, MT, BLK])
        zs = mb("zs", [P, MT, BLK])
        cumb = mb("cumb", [P, R, S])
        m = mb("m", [P, MT, R, P])
        cbm = mb("cbm", [P, MT, P])
        bt = mb("bt", [P, NS])
        state = mb("state", [NS, BLK])
        causal = mb("causal", [P, P])
        ones = mb("ones", [P, P])
        hd = mb("hd", [P, 3, NH])
        dt = mb("dt", [P, MT, NH])
        da = mb("da", [P, MT, NH])
        cum = mb("cum", [P, MT, NH])
        todend = mb("todend", [P, NH])
        ecum = mb("ecum", [P, NH])
        tmp = mb("tmp", [P, 4, MT, NH])
        cumt = mb("cumt", [NH, S])
        cpar = mb("cpar", [P, TAPS + 1, 6])
        gpar = mb("gpar", [P, 4])
        gcum = mb("gcum", [P, MT, R])
        mem.close()

        mem = ExitStack()
        relu = mb("relu", [P, MT, BLK])
        sq = mb("sq", [P, MT, BLK])
        bhi.append(mb("bhi1", [P, 4, S], F32R))
        blo.append(mb("blo1", [P, 4, S], F32R))
        mem.close()

        mem = ExitStack()
        khi = mb("khi", [P, KT, S], F32R)
        klo = mb("klo", [P, KT, S], F32R)
        qt = mb("qt", [P, HG, S])
        kt_ = mb("kt", [P, HG, S])
        v = mb("v", [P, MT, BLK])
        tab = mb("tab", [P, HG, S])
        lg = [mb(f"lg{i}", [P, 2, S + P]) for i in range(2)]
        at = [mb(f"at{i}", [P, S + P]) for i in range(2)]
        att_t = mb("att_t", [P, S + P])
        ob = mb("ob", [P, MT, P])
        nmax = [mb(f"nmax{i}", [P, 4]) for i in range(2)]
        psum_ = [mb(f"psums{i}", [P, 4]) for i in range(2)]
        rinv = mb("rinv", [P, 4])
        mem.close()

        cum_dram = nc.dram_tensor("cum_scratch", [NH, S], F32, kind="Internal").ap()
        bias_dram = nc.dram_tensor("bias_scratch", [HEADS, P, S + P], F32, kind="Internal").ap()


        raw_in = [sem(f"raw_in{i}") for i in range(RING)]
        hi_ready, lo_ready, slab_used = sem("hi_ready"), sem("lo_ready"), sem("slab_used")
        consts_ready, small_in, x_in = sem("consts_ready"), sem("small_in"), sem("x_in")
        heads_in, rel_in, lam_in = sem("heads_in"), sem("rel_in"), sem("lam_in")
        par_t, par_ready = sem("par_t"), sem("par_ready")
        postw_in, cum_out, cumb_in, bias_out, tab_in = (
            sem("postw_in"), sem("cum_out"), sem("cumb_in"), sem("bias_out"), sem("tab_in"))
        y_zeroed, acc_added = sem("y_zeroed"), sem("acc_added")
        y_sq, yw_ready, h_new, h_sq, rms_ready = sem("y_sq"), sem("yw_ready"), sem("h_new"), sem("h_sq"), sem("rms_ready")
        rows_cleared = sem("rows_cleared")
        xt_done, x_hi, x_lo = sem("xt_done"), sem("x_hi"), sem("x_lo")
        b_hi, h_ready = sem("b_hi"), sem("h_ready")
        dve_chain, act_chain, pool_chain = sem("dve_chain"), sem("act_chain"), sem("pool_chain")
        dt_done, dt_v, dt_e, dt_l, da_ready, cum_done, cum_ready = (
            sem("dt_done"), sem("dt_v"), sem("dt_e"), sem("dt_l"), sem("da_ready"), sem("cum_done"), sem("cum_ready"))
        cumt_done, cumt_ready, expd_ready = sem("cumt_done"), sem("cumt_ready"), sem("expd_ready")
        cpar_ready = sem("cpar_ready")
        pre_ready, conv_done, silu_done = sem("pre_ready"), sem("conv_done"), sem("silu_done")
        seg_done, decay_done = sem("seg_done"), sem("decay_done")
        spread_done, xs_ready, pool_ready, cb_ready, mt_ready = (
            sem("spread_done"), sem("xs_ready"), sem("pool_ready"), sem("cb_ready"), sem("mt_ready"))
        state_done, state_ready, y_done, zs_ready = (
            sem("state_done"), sem("state_ready"), sem("y_done"), sem("zs_ready"))
        gated, g_sq, g_ready, gt_done = sem("gated"), sem("g_sq"), sem("g_ready"), sem("gt_done")
        q_copied, k_copied, v_copied = sem("q_copied"), sem("k_copied"), sem("v_copied")
        lg_done, lg_ready, ex_ready, at_ready, at_t, at_copied = (
            sem("lg_done"), sem("lg_ready"), sem("ex_ready"), sem("at_ready"), sem("at_t"), sem("at_copied"))
        o_done, o_sq, o_ready, ot_done = sem("o_done"), sem("o_sq"), sem("o_ready"), sem("ot_done")
        lam_ready, lam_e, subw_ready = sem("lam_ready"), sem("lam_e"), sem("subw_ready")
        stored = sem("stored")

        block = ctx.enter_context(nc.Block())

        @block.sync
        def _(sp):
            def load(s, src, tiles):
                free = sp.lower_val(s.n + 1 - RING if isinstance(s.n, int) else sp.snap(s.n + 1 - RING))
                dst = raw[:, s.raw, :].rearrange("p (t n) -> p t n", t=tiles)
                dma = sp.dma_start(dst, src.rearrange("(t p) n -> p t n", p=P))
                if above(s.n, RING - 1):
                    dma.wait_op(lo_ready, free, "sem-ge")
                dma.then_inc(raw_in[s.raw], 16)

            def tile(mat, row, rows, col, cols):
                return mat[bass.ds(row, rows), bass.ds(col, cols)]

            def mix_load(s, unit, i, g):
                if unit == "xs":
                    load(s, tile(in_proj, 256 * i, 256, XBC0 + g * BLK, BLK), 2)
                elif unit == "bc":
                    load(s, tile(in_proj, 1024 * (i % 2), 1024, (B0, C0)[i // 2] + g * NS, NS), 8)
                elif unit == "z":
                    load(s, tile(in_proj, 256 * i, 256, g * BLK, BLK), 2)
                else:
                    load(s, tile(out_proj, (g - 1) * BLK + 256 * (i % 2), 256, BLK * (i // 2), BLK), 2)

            for t in range(MT):
                sp.dma_start(h[:, t, :], w["x"][0, t * P:(t + 1) * P, :]).then_inc(x_in, 16)
            sp.wait_ge(small_in, 16 * SMALL_LOADS)
            load(mix.slab(0), in_proj[:, DT0:DT0 + NH], 16)
            for k, (unit, i) in enumerate(MIX_FIRST):
                mix_load(mix.slab(1 + k), unit, i, 0)
            with sp.Fori(0, G - 1) as t:
                for k, (unit, i) in enumerate(MIX_BODY):
                    mix_load(mix.slab(21 + k, t, 28), unit, i, t + 1)
            for k, (unit, i) in enumerate(ACC):
                mix_load(mix.slab(217 + k), unit, i, G)

            def mlp(ph, layer):
                w1, w2 = w["mlp_w1"][layer], w["mlp_w2"][layer]

                def up(s, i, b):
                    load(s, tile(w1, 256 * i, 256, b * BLK, BLK), 2)

                def down(s, i, b):
                    load(s, tile(w2, b * BLK + 256 * (i % 2), 256, BLK * (i // 2), BLK), 2)

                for k, (unit, i) in enumerate(MLP_FIRST):
                    up(ph.slab(k), i, 0)
                with sp.Fori(0, 7) as t:
                    for k, (unit, i) in enumerate(MLP_BODY):
                        s = ph.slab(8 + k, t, 32)
                        if unit == "up1":
                            up(s, i, 2 * t + 1)
                        elif unit == "up0":
                            up(s, i, 2 * t + 2)
                        else:
                            down(s, i, 2 * t + (unit == "acc1"))
                for k, (unit, i) in enumerate(MLP_LAST):
                    s = ph.slab(232 + k)
                    if unit == "up1":
                        up(s, i, 15)
                    else:
                        down(s, i, 14 + (unit == "acc1"))

            mlp(mlp0, 0)

            def att_load(s, unit, i, g):
                if unit == "acc":
                    load(s, tile(o_proj, (g - 1) * BLK + 256 * (i % 2), 256, BLK * (i // 2), BLK), 2)
                else:
                    load(s, tile({"q": w_q, "k": w_k, "v": w_v}[unit], 256 * i, 256, g * BLK, BLK), 2)

            for k, (unit, i) in enumerate(ATT_FIRST):
                att_load(att.slab(k), unit, i, 0)
            with sp.Fori(0, QG - 1) as t:
                for k, (unit, i) in enumerate(ATT_BODY):
                    att_load(att.slab(24 + k, t, 32), unit, i, t + 1)
            for k, (unit, i) in enumerate(ACC):
                att_load(att.slab(120 + k), unit, i, QG)
            mlp(mlp1, 1)
            for n in range(MT * PIECES):
                sp.wait_ge(h_new, 3 * MT * PIECES + n + 1)
                t, cols = n // PIECES, piece(n % PIECES)
                sp.dma_start(out[0, t * P:(t + 1) * P, cols], h[:, t, cols]).then_inc(stored, 16)
            sp.wait_ge(stored, 16 * MT * PIECES)

        @block.gpsimd
        def _(pool):
            chain = Tally(pool, pool_chain)
            g_ = nc.gpsimd

            g_.memset(pre[:, :, 0:TAPS - 1], 0.0)
            g_.memset(ones[:, :], 1.0)
            chain.mark(g_.memset(ident[:, :], 0.0))
            chain.mark(g_.memset(causal[:, :], 1.0))
            chain.wait()
            g_.affine_select(out=ident[:, :], in_=ident[:, :], compare_op=ALU.not_equal, fill=1.0, base=0,
                             pattern=[[-1, P]], channel_multiplier=1)
            g_.affine_select(out=causal[:, :], in_=causal[:, :], compare_op=ALU.is_ge, fill=0.0, base=0,
                             pattern=[[1, P]], channel_multiplier=-1).then_inc(consts_ready, 1)

            for i, name in enumerate(("a_dt_bias", "a_A_log", "a_D")):
                pool.dma_start(hd[:, i, :], w[name][0].partition_broadcast(P)).then_inc(heads_in, 16)
            for i, name in enumerate(("b_lambda_q1", "b_lambda_k1", "b_lambda_q2", "b_lambda_k2")):
                pool.dma_start(lamv[:, i, :], w[name][0].partition_broadcast(P)).then_inc(lam_in, 16)
            pool.dma_start(relrow[:, :], w["rel_bias"].rearrange("b h -> h b"), allow_slow_non_contiguous=True)\
                .then_inc(rel_in, 16)
            pool.dma_start(postw[:, :], w["norm_post_mix"][0].partition_broadcast(P)).then_inc(postw_in, 16)

            pool.wait_ge(rel_in, 16)
            bounds = bucket_bounds()
            g_.memset(bias_row[:, S:S + P], MASKED)
            for b in range(BUCKETS):
                lo, hi = S - bounds[b + 1], S - bounds[b]
                last = g_.tensor_copy(bias_row[:, lo:hi], relrow[:, b:b + 1].to_broadcast([HEADS, hi - lo]))
            chain.mark(last)
            chain.wait()
            pool.dma_start(bias_dram, bias_row[:, :].unsqueeze(1).to_broadcast([HEADS, P, S + P])).then_inc(bias_out, 16)

            def zero_y(r):
                if r > 0:
                    pool.wait_ge(h_new, MT * PIECES * r)
                g_.memset(y[:, :, :], 0.0).then_inc(y_zeroed, 1)

            def weigh_y(r):
                pool.wait_ge(postw_in, 16 * (r + 1))
                for nt in range(NT):
                    pool.wait_ge(y_sq, MT * (NT * r + nt + 1))
                    cols = slice(nt * BLK, (nt + 1) * BLK)
                    g_.tensor_tensor(out=y[:, :, cols], in0=y[:, :, cols],
                                     in1=postw[:, cols].unsqueeze(1).to_broadcast([P, MT, BLK]),
                                     op=ALU.mult).then_inc(yw_ready, 1)

            def next_postw(r, vec):
                pool.wait_ge(yw_ready, NT * r)
                pool.dma_start(postw[:, :], vec.partition_broadcast(P)).then_inc(postw_in, 16)

            zero_y(0)

            def group(g):
                if above(g):
                    pool.wait_ge(silu_done, 2 * g)
                    pool.wait_ge(seg_done, g)
                for lo, n, at0 in ((0, 4, g * 4), (4, 1, 32 + g), (5, 1, 40 + g)):
                    for tp in range(TAPS + 1):
                        col = P * (1 + tp // 2) + 48 * (tp % 2)
                        g_.tensor_copy(cpar[:, tp, lo:lo + n], par[:, bass.ds(col + at0, n)])
                g_.tensor_copy(gcum[:, :, :], cum[:, :, bass.ds(g * R, R)]).then_inc(cpar_ready, 1)
                if not above(g):
                    pool.wait_ge(cumt_ready, 1)
                    pool.dma_start(cum_dram, cumt[:, :]).then_inc(cum_out, 16)
                    pool.wait_ge(cum_out, 16)
                src = cum_dram[bass.ds(g * R, R), :].rearrange("r s -> (r s)").partition_broadcast(P)
                pool.dma_start(cumb[:, :, :].rearrange("p r s -> p (r s)"), src).then_inc(cumb_in, 16)
                pool.wait_ge(xs_ready, g + 1)
                if above(g):
                    pool.wait_ge(gt_done, g)
                    pool.wait_ge(h_ready, g)
                chain.mark(g_.tensor_copy(gpar[:, :], par[:, bass.ds(80 + g * 4, 4)]))
                for c in range(MT):
                    last = g_.tensor_tensor(
                        out=xd[:, c, :].rearrange("p (r d) -> p r d", r=R), in0=xs[:, c, :].rearrange("p (r d) -> p r d", r=R),
                        in1=column_bcast(dt[:, c, bass.ds(g * R, R)], PD), op=ALU.mult)
                    chain.mark(last)
                    if c == 0:
                        chain.wait()
                        g_.tensor_tensor(out=xe[:, :].rearrange("p (r d) -> p r d", r=R),
                                         in0=xd[:, 0, :].rearrange("p (r d) -> p r d", r=R),
                                         in1=column_bcast(todend[:, bass.ds(g * R, R)], PD),
                                         op=ALU.mult)
                for c in range(MT):
                    last = g_.tensor_tensor(
                        out=yg[:, c, :].rearrange("p (r d) -> p r d", r=R), in0=xs[:, c, :].rearrange("p (r d) -> p r d", r=R),
                        in1=column_bcast(hd[:, 2, bass.ds(g * R, R)], PD), op=ALU.mult)
                last.then_inc(pool_ready, 1)

            pool.wait_ge(expd_ready, 1)
            pool.wait_ge(par_ready, 1)
            group(0)
            with pool.Fori(0, G - 1) as t:
                chain.enter(t, 3)
                group(t + 1)
            chain.leave(G - 1, 3)
            weigh_y(0)
            next_postw(1, w["norm_post_mlp"][0])
            zero_y(1)
            weigh_y(1)
            next_postw(2, w["norm_post_mix"][1])
            zero_y(2)

            def tab_load(g):
                src = bass.AP(tensor=bias_dram.tensor, offset=g * (HG * P * (S + P)) + P - 1,
                              ap=[[S + P - 1, P], [P * (S + P), HG], [1, S]])
                pool.dma_start(tab[:, :, :], src).then_inc(tab_in, 16)

            pool.wait_ge(bias_out, 16)
            pool.wait_ge(h_new, 2 * MT * PIECES)
            tab_load(0)
            with pool.Fori(0, QG - 1) as t:
                pool.wait_ge(lg_ready, HG * (t + 1))
                tab_load(t + 1)
            weigh_y(2)
            next_postw(3, w["norm_post_mlp"][1])
            zero_y(3)
            weigh_y(3)

        @block.scalar
        def _(act):
            chain = Tally(act, act_chain)
            sc = nc.scalar

            def split(s):
                act.wait_ge(raw_in[s.raw], s.arrived)
                if above(s.n, LEAD - 1):
                    act.wait_ge(slab_used, s.n - LEAD + 1)
                sc.activation(whi[:, s.split, :], raw[:, s.raw, :], ACT.Copy).then_inc(hi_ready, 1)

            def square_sum(t, src, dst, done, at0=0):
                sc.activation(junk[:, t, at0:at0 + src.shape[-1]], src, ACT.Square, accum_out=dst).then_inc(done, 1)

            def square_sums(r, first_h=False):
                for n in range(MT * PIECES):
                    t, p = n // PIECES, n % PIECES
                    if first_h:
                        act.wait_ge(x_in, 16 * MT)
                    else:
                        act.wait_ge(h_new, MT * PIECES * (r - 1) + n + 1)
                    square_sum(t, h[:, t, piece(p)], ssh[:, t, p:p + 1], h_sq, p * D // PIECES)

            def normed(r, cols, outs):
                for i in range(KT // 2):
                    act.wait_ge(xt_done, 8 * r + i + 1)
                    for dst, col in zip(outs, cols):
                        for j in range(2):
                            k = 2 * i + j
                            last = sc.activation(dst[:, k, :], ps[:, i, j * S:(j + 1) * S], ACT.Copy,
                                                 scale=par[:, col + k:col + k + 1])
                    last.then_inc(x_hi, 1)

            def output_norm(ph, i):
                for nt in {2: (0,), 4: (1,), 6: (2,), 7: (3,)}.get(i, ()):
                    act.wait_ge(acc_added, NT * (ph.block0 + ph.blocks - 1) + nt + 1)
                    for t in range(MT):
                        square_sum(t, y[:, t, nt * BLK:(nt + 1) * BLK], ssy[:, t, nt:nt + 1], y_sq,
                                   nt * BLK)

            def block_hi():
                for f in range(4):
                    last = sc.activation(bhi[0][:, f, :], ps[:, 5 + f // 2, (f % 2) * S:(f % 2 + 1) * S], ACT.Copy,
                                         scale=gpar[:, f:f + 1])
                last.then_inc(b_hi, 1)

            def rows(dst, lo, vec):
                n = vec.shape[0] // P
                act.dma_start(dst[lo:lo + n, :], vec.rearrange("(r c) -> r c", c=P)).then_inc(small_in, 16)

            act.wait_ge(rows_cleared, 1)
            rows(par_rows[:, 0, :], 0, w["norm_pre_mix"].rearrange("l d -> (l d)"))
            rows(par_rows[:, 0, :], 32, w["norm_pre_mlp"].rearrange("l d -> (l d)"))
            rows(par_rows[:, 0, :], 64, w["kv_norm_w"])
            rows(par_rows[:, 0, :], 80, w["a_gate_norm_w"][0])
            rows(par_rows[:, 0, :], 112, w["b_subln_w"][0])
            for tap in range(TAPS):
                rows(par_rows[:, 1 + tap // 2, :], 48 * (tap % 2), w["a_conv_w"][0, tap])
            rows(par_rows[:, 3, :], 0, w["a_conv_b"][0])
            square_sums(0, True)
            act.wait_ge(par_t, 1)
            sc.activation(par[:, :], ps[:, 0, :], ACT.Copy).then_inc(par_ready, 1)
            act.wait_ge(par_ready, 1)
            sc.mul(subw[:, :], par[:, 112:113], 1.0 - LAMBDA_INIT).then_inc(subw_ready, 1)
            for k in range(LEAD):
                split(mix.slab(k))
            normed(0, (0,), (xhi,))
            split(mix.slab(LEAD))
            act.wait_ge(dt_v, 1)
            sc.activation(tmp[:, 1, :, :], tmp[:, 0, :, :], ACT.Exp, scale=-1.0)
            sc.activation(hd[:, 1, :], hd[:, 1, :], ACT.Exp).then_inc(dt_e, 1)
            act.wait_ge(dt_l, 1)
            sc.activation(tmp[:, 3, :, :], tmp[:, 2, :, :], ACT.Ln).then_inc(dt_e, 1)
            act.wait_ge(lam_ready, 1)
            sc.activation(neglam[:, 2:4], neglam[:, 0:2], ACT.Exp).then_inc(lam_e, 1)

            def mix_step(first, g, unit, i):
                if (unit, i) == ("xs", 1) and not first:
                    act.wait_ge(gated, g)
                    for c in range(MT):
                        square_sum(c, yg[:, c, :], ssg[:, c:c + 1], g_sq)
                if (unit, i) == ("xs", 7):
                    if not first:
                        act.wait_ge(silu_done, 2 * g)
                    for b in range(2):
                        sc.activation(pre[:, 2 * b:2 * b + 2, TAPS - 1:], ps[:, b, :].rearrange("p (f s) -> p f s", f=2),
                                      ACT.Copy).then_inc(pre_ready, 1)
                    if first:
                        act.wait_ge(cum_ready, 1)
                        sc.activation(todend[:, :], todend[:, :], ACT.Exp)
                        sc.activation(ecum[:, :], cum[:, 1, :], ACT.Exp).then_inc(expd_ready, 1)
                    else:
                        act.wait_ge(gt_done, g)
                        block_hi()
                if (unit, i) == ("bc", 3):
                    sc.activation(pre[:, 4:6, TAPS - 1:], ps[:, 2, :].rearrange("p (f s) -> p f s", f=2),
                                  ACT.Copy).then_inc(pre_ready, 1)
                    act.wait_ge(conv_done, 2 * g + 1)
                    for f in range(4):
                        last = sc.activation(conv[:, f, :], conv[:, f, :], ACT.Silu, bias=cpar[:, TAPS, f:f + 1])
                    last.then_inc(silu_done, 1)
                if (unit, i) == SILU_BC[first]:
                    act.wait_ge(conv_done, 2 * g + 2)
                    for f in range(4, 6):
                        last = sc.activation(conv[:, f, :], conv[:, f, :], ACT.Silu, bias=cpar[:, TAPS, f:f + 1])
                    last.then_inc(silu_done, 1)
                if (unit, i) == DECAY[first]:
                    act.wait_ge(seg_done, g + 1)
                    for c in range(MT):
                        sc.activation(m[:, c, :, :], m[:, c, :, :], ACT.Exp).then_inc(decay_done, 1)
                if (unit, i) == SPREAD[first]:
                    act.wait_ge(spread_done, 2 * g + 1)
                    for c in range(MT):
                        last = sc.activation(xs[:, c, :], ps[:, c, :], ACT.Copy)
                    last.then_inc(xs_ready, 1)
                if (unit, i) == STATE[first]:
                    act.wait_ge(state_done, g + 1)
                    sc.activation(state[:, :], ps[:, 7, :], ACT.Copy).then_inc(state_ready, 1)
                if (unit, i) == ("z", 7):
                    sc.activation(zs[:, :, :], ps[:, 3:5, :], ACT.Silu).then_inc(zs_ready, 1)

            def steps(ph, first_k, order, body, t=0, per=0, urgent=False):
                for k, (unit, i) in enumerate(order):
                    ahead = ph.slab(first_k + k + LEAD, t, per)
                    if urgent and k == len(order) - 1:
                        body(unit, i)
                        if ahead:
                            split(ahead)
                        continue
                    if ahead:
                        split(ahead)
                        act.wait_ge(hi_ready, ahead.used)
                    else:
                        act.wait_ge(slab_used, ph.slab(first_k + k).used)
                    body(unit, i)

            steps(mix, 1, MIX_FIRST, lambda u, i: mix_step(True, 0, u, i))
            with act.Fori(0, G - 1) as t:
                steps(mix, 21, MIX_BODY, lambda u, i: mix_step(False, t + 1, u, i), t, 28)
            act.wait_ge(gated, G)
            for c in range(MT):
                square_sum(c, yg[:, c, :], ssg[:, c:c + 1], g_sq)
            act.wait_ge(gt_done, G)
            block_hi()
            steps(mix, 217, ACC, lambda u, i: output_norm(mix, i), urgent=True)

            def mlp(ph):
                def up(which, b):
                    if above(b):
                        act.wait_ge(h_ready, ph.features(b - 1))
                    for n in range(2):
                        chain.mark(sc.activation(relu[:, n, :], ps[:, n, :], ACT.Relu))
                    chain.wait()
                    for n in range(2):
                        last = sc.activation(bhi[which][:, 2 * n:2 * n + 2, :].rearrange("p f s -> p (f s)"),
                                             relu[:, n, :], ACT.Square)
                    last.then_inc(b_hi, 1)

                def step(unit, i, b):
                    if i == 7 and unit[:2] == "up":
                        up(int(unit[2:] or 0), b + {"up": 0, "up1": 1, "up0": 2}[unit])

                steps(ph, 0, MLP_FIRST, lambda u, i: step(u, i, 0))
                with act.Fori(0, 7) as t:
                    chain.enter(t, 4)
                    steps(ph, 8, MLP_BODY, lambda u, i: step(u, i, 2 * t), t, 32)
                chain.leave(7, 4)
                steps(ph, 232, MLP_LAST, lambda u, i: output_norm(ph, i) if u == "acc1" else step(u, i, 14), urgent=True)

            square_sums(1)
            normed(1, (32,), (xhi,))
            mlp(mlp0)
            square_sums(2)
            normed(2, (16, 64), (xhi, khi))

            def attend(j, p, at_steps=HEADS_AT):
                for i in range(HG):
                    n = HG * p + i
                    if j == at_steps[0][i] + 1:
                        act.wait_ge(lg_ready, n + 1)
                        for c in range(2):
                            sc.activation(lg[i % 2][:, c, 0:S], lg[i % 2][:, c, 0:S], ACT.Exp,
                                          bias=nmax[i % 2][:, c:c + 1], accum_out=psum_[i % 2][:, c:c + 1])
                            last = sc.activation(lg[i % 2][:, c, S:], lg[i % 2][:, c, S:], ACT.Exp,
                                                 bias=nmax[i % 2][:, 2 + c:3 + c], accum_out=psum_[i % 2][:, 2 + c:3 + c])
                        last.then_inc(ex_ready, 1)
                    if j == at_steps[0][i] + 4:
                        act.wait_ge(at_t, n + 1)
                        sc.activation(att_t[:, :], ps[:, 5, 0:S + P], ACT.Copy).then_inc(at_copied, 1)
                    if j == at_steps[0][i] + 6:
                        act.wait_ge(o_done, n + 1)
                        for c in range(MT):
                            square_sum(c, ps[:, 6, c * P:(c + 1) * P], ssa[:, c:c + 1], o_sq)
                    if j == at_steps[1][i]:
                        act.wait_ge(ot_done, n + 1)
                        sc.activation(bhi[0][:, i, :], ps[:, i % 2, 0:S], ACT.Copy, scale=subw[:, :]).then_inc(b_hi, 1)

            def att_step(first, g, unit, i):
                if unit in "qk" and not first:
                    attend(i + 8 * (unit == "k"), g - 1)
                if i == 0 and unit == "k":
                    sc.activation(qt[:, :, :].rearrange("p f s -> p (f s)"), ps[:, 0:2, :].rearrange("p b n -> p (b n)"),
                                  ACT.Copy).then_inc(q_copied, 1)
                if i == 7 and unit == "k":
                    sc.activation(kt_[:, :, :].rearrange("p f s -> p (f s)"), ps[:, 3:5, :].rearrange("p b n -> p (b n)"),
                                  ACT.Copy).then_inc(k_copied, 1)
                if i == 7 and unit == "v":
                    sc.activation(v[:, :, :], ps[:, 5:7, :], ACT.Copy).then_inc(v_copied, 1)

            steps(att, 0, ATT_FIRST, lambda u, i: att_step(True, 0, u, i))
            with act.Fori(0, QG - 1) as t:
                steps(att, 24, ATT_BODY, lambda u, i: att_step(False, t + 1, u, i), t, 32)
            for j in range(15):
                attend(j, QG - 1, LAST_AT)
            steps(att, 120, ACC, lambda u, i: output_norm(att, i), urgent=True)
            square_sums(3)
            normed(3, (48,), (xhi,))
            mlp(mlp1)

        @block.vector
        def _(dve):
            chain = Tally(dve, dve_chain)
            ve = nc.vector

            def split(s):
                dve.wait_ge(hi_ready, s.n + 1)
                ve.tensor_tensor(out=wlo[:, s.split, :], in0=raw[:, s.raw, :], in1=whi[:, s.split, :].bitcast(F32),
                                 op=ALU.subtract).then_inc(lo_ready, 1)

            def link(ins):
                chain.mark(ins)
                chain.wait()

            def inverse_rms(dst, src, n, eps):
                chain.mark(ve.tensor_scalar(rs_x, src, 1.0 / n, eps, ALU.mult, ALU.add))
                chain.mark(ve.tensor_scalar(rs_h, src, -0.5 / n, -0.5 * eps, ALU.mult, ALU.add))
                chain.wait(back=1)
                link(ve.tensor_scalar(rs_a.bitcast(I32), rs_x.bitcast(I32), 1, None, ALU.logical_shift_right))
                link(ve.tensor_scalar(dst.bitcast(I32), rs_a.bitcast(I32), -1.0, float(0x5F3759DF), ALU.mult, ALU.add))
                for step in range(3):
                    for c in (slice(0, 1), slice(1, 2)):
                        if step > 0:
                            chain.wait(back=1)
                        chain.mark(ve.scalar_tensor_tensor(out=rs_a[:, c], in0=dst[:, c], scalar=rs_h[:, c], in1=dst[:, c],
                                                           op0=ALU.mult, op1=ALU.mult))
                    for c in (slice(0, 1), slice(1, 2)):
                        chain.wait(back=1)
                        chain.mark(ve.scalar_tensor_tensor(out=dst[:, c], in0=rs_a[:, c], scalar=1.5, in1=dst[:, c],
                                                           op0=ALU.add, op1=ALU.mult))
                chain.wait()

            def diagonal(rs, done):
                for t in range(MT):
                    ve.tensor_scalar(diag[:, t, :], ident[:, :], rs[:, t:t + 1], None, ALU.mult).then_inc(done, 1)

            def steps(ph, first_k, order, body, t=0, per=0, urgent=False):
                for k, (unit, i) in enumerate(order):
                    ahead = ph.slab(first_k + k + LEAD, t, per)
                    if urgent and k == len(order) - 1:
                        dve.wait_ge(slab_used, ph.slab(first_k + k).used)
                        body(unit, i)
                        if ahead:
                            split(ahead)
                        continue
                    if ahead:
                        split(ahead)
                        dve.wait_ge(lo_ready, ahead.used)
                    else:
                        dve.wait_ge(slab_used, ph.slab(first_k + k).used)
                    body(unit, i)

            def add_output(ph, b, i):
                if i % 2 == 0:
                    return
                nt = i // 2
                cols = y[:, :, nt * BLK:(nt + 1) * BLK]
                bank = 3 + 2 * (nt % 2)
                ve.tensor_tensor(out=cols, in0=cols, in1=ps[:, bank:bank + 2, :], op=ALU.add).then_inc(acc_added, 1)

            def normed(r, cols, his, los):
                dve.wait_ge(h_sq, MT * PIECES * (r + 1))
                link(ve.reduce_sum(sum_h, ssh, AX))
                inverse_rms(rsh, sum_h, D, 1e-6)
                if r == 0:
                    dve.wait_ge(consts_ready, 1)
                diagonal(rsh, rms_ready)
                if r == 0:
                    for k in range(LEAD):
                        split(mix.slab(k))
                    dve.wait_ge(par_ready, 1)
                for i in range(KT // 2):
                    dve.wait_ge(x_hi, 8 * r + i + 1)
                    for hi, lo, col in zip(his, los, cols):
                        for j in range(2):
                            k = 2 * i + j
                            last = ve.scalar_tensor_tensor(
                                out=lo[:, k, :], in0=ps[:, i, j * S:(j + 1) * S], scalar=par[:, col + k:col + k + 1],
                                in1=hi[:, k, :].bitcast(F32), op0=ALU.mult, op1=ALU.subtract)
                    last.then_inc(x_lo, 1)

            def residual(r):
                dve.wait_ge(y_sq, MT * NT * (r + 1))
                link(ve.reduce_sum(sum_y, ssy, AX))
                inverse_rms(rsy, sum_y, D, 1e-6)
                dve.wait_ge(yw_ready, NT * (r + 1))
                for t in range(MT):
                    for p in range(PIECES):
                        ve.scalar_tensor_tensor(out=h[:, t, piece(p)], in0=y[:, t, piece(p)], scalar=rsy[:, t:t + 1],
                                                in1=h[:, t, piece(p)], op0=ALU.mult, op1=ALU.add).then_inc(h_new, 1)

            def block_lo():
                for f in range(4):
                    last = ve.scalar_tensor_tensor(
                        out=blo[0][:, f, :], in0=ps[:, 5 + f // 2, (f % 2) * S:(f % 2 + 1) * S], scalar=gpar[:, f:f + 1],
                        in1=bhi[0][:, f, :].bitcast(F32), op0=ALU.mult, op1=ALU.subtract)
                last.then_inc(h_ready, 1)

            ve.memset(par_rows[:, :, :], 0.0).then_inc(rows_cleared, 1)
            normed(0, (0,), (xhi,), (xlo,))
            split(mix.slab(LEAD))

            dve.wait_ge(heads_in, 48)
            dve.wait_ge(slab_used, mix.slab(0).used)
            link(ve.tensor_tensor(out=dt[:, :, :], in0=ps[:, 7, 0:2 * NH].rearrange("p (c n) -> p c n", c=MT),
                                  in1=hd[:, 0, :].unsqueeze(1).to_broadcast([P, MT, NH]), op=ALU.add))
            link(ve.tensor_scalar(tmp[:, 0, :, :], dt[:, :, :], -1.0, None, ALU.mult))
            ve.tensor_tensor(out=tmp[:, 0, :, :], in0=tmp[:, 0, :, :], in1=dt[:, :, :], op=ALU.max).then_inc(dt_v, 1)
            link(ve.tensor_scalar(dt[:, :, :], dt[:, :, :], 0.0, None, ALU.max))
            dve.wait_ge(dt_e, 1)
            ve.tensor_scalar(tmp[:, 2, :, :], tmp[:, 1, :, :], 1.0, None, ALU.add).then_inc(dt_l, 1)
            dve.wait_ge(dt_l, 1)
            link(ve.tensor_scalar(tmp[:, 0, :, :], tmp[:, 2, :, :], 1.0, None, ALU.is_equal))
            dve.wait_ge(dt_e, 2)
            link(ve.scalar_tensor_tensor(out=tmp[:, 2, :, :], in0=tmp[:, 2, :, :], scalar=-1.0,
                                         in1=tmp[:, 0, :, :], op0=ALU.add, op1=ALU.add))
            link(ve.tensor_tensor(out=tmp[:, 3, :, :], in0=tmp[:, 3, :, :], in1=tmp[:, 0, :, :], op=ALU.add))
            link(ve.reciprocal(tmp[:, 2, :, :], tmp[:, 2, :, :]))
            link(ve.tensor_tensor(out=tmp[:, 3, :, :], in0=tmp[:, 3, :, :], in1=tmp[:, 1, :, :], op=ALU.mult))
            link(ve.tensor_tensor(out=tmp[:, 3, :, :], in0=tmp[:, 3, :, :], in1=tmp[:, 2, :, :], op=ALU.mult))
            link(ve.tensor_tensor(out=dt[:, :, :], in0=dt[:, :, :], in1=tmp[:, 3, :, :], op=ALU.add))
            ve.scalar_tensor_tensor(out=da[:, :, :], in0=dt[:, :, :], scalar=-1.0,
                                    in1=hd[:, 1, :].unsqueeze(1).to_broadcast([P, MT, NH]),
                                    op0=ALU.mult, op1=ALU.mult).then_inc(da_ready, 1)
            dve.wait_ge(lam_in, 64)
            for i in range(2):
                link(ve.tensor_tensor(out=lamv[:, 2 * i, :], in0=lamv[:, 2 * i, :], in1=lamv[:, 2 * i + 1, :], op=ALU.mult))
                last = ve.reduce_sum(neglam[:, i:i + 1], lamv[:, 2 * i, :], AX)
            last.then_inc(lam_ready, 1)
            dve.wait_ge(lam_e, 1)
            link(ve.tensor_tensor(out=neglam[:, 1:2], in0=neglam[:, 3:4], in1=neglam[:, 2:3], op=ALU.subtract))
            link(ve.tensor_scalar(neglam[:, 0:1], neglam[:, 1:2], -LAMBDA_INIT, None, ALU.add))

            def mix_cum():
                dve.wait_ge(cum_done, 1)
                link(ve.tensor_copy(cum[:, :, :], ps[:, 7, 0:2 * NH].rearrange("p (c n) -> p c n", c=MT)))
                ve.tensor_tensor(out=todend[:, :], in0=ps[:, 7, 2 * NH:3 * NH], in1=cum[:, 0, :],
                                 op=ALU.subtract).then_inc(cum_ready, 1)

            def mix_step(first, g, unit, i):
                if first and (unit, i) == ("xs", 4):
                    mix_cum()
                if (unit, i) == ("xs", 2) and not first:
                    dve.wait_ge(g_sq, 2 * g)
                    inverse_rms(rsg, ssg, BLK, 1e-5)
                    diagonal(rsg, g_ready)
                if (unit, i) == ("xs", 4) or (first and (unit, i) == ("z", 1)):
                    if first and unit == "xs":
                        return
                    dve.wait_ge(cumb_in, 16 * (g + 1))
                    dve.wait_ge(cpar_ready, g + 1)
                    if not first:
                        dve.wait_ge(y_done, g)
                    for c in range(MT):
                        for r in range(R):
                            last = ve.tensor_scalar(m[:, c, r, :], cumb[:, r, c * P:(c + 1) * P], gcum[:, c, r:r + 1], 0.0,
                                                    ALU.subtract, ALU.min)
                    last.then_inc(seg_done, 1)
                if (unit, i) in (("xs", 7), ("bc", 3)):
                    lo, hi = (0, 4) if unit == "xs" else (4, 6)
                    if first and unit == "xs":
                        dve.wait_ge(cumt_done, 1)
                        ve.tensor_copy(cumt[:, :], ps[0:NH, 7, 0:S]).then_inc(cumt_ready, 1)
                    dve.wait_ge(cpar_ready, g + 1)
                    dve.wait_ge(pre_ready, 3 * g + (2 if unit == "xs" else 3))
                    if not first:
                        dve.wait_ge(spread_done, 2 * g)
                        dve.wait_ge(y_done, g)
                    for f in range(lo, hi):
                        chain.mark(ve.tensor_scalar(conv[:, f, :], pre[:, f, 0:S], cpar[:, 0, f:f + 1], None, ALU.mult))
                    for tap in range(1, TAPS):
                        for f in range(lo, hi):
                            chain.wait(back=hi - lo - 1)
                            ins = ve.scalar_tensor_tensor(
                                out=conv[:, f, :], in0=pre[:, f, tap:tap + S], scalar=cpar[:, tap, f:f + 1],
                                in1=conv[:, f, :], op0=ALU.mult, op1=ALU.add)
                            if (tap, f) == (TAPS - 1, hi - 1):
                                ins.then_inc(conv_done, 1)
                            else:
                                chain.mark(ins)
                    if (unit, i) == ("xs", 7) and not first:
                        dve.wait_ge(b_hi, g)
                        block_lo()
                if unit == "acc":
                    add_output(mix, g - 1, i)
                if (unit, i) == SPREAD[first]:
                    dve.wait_ge(spread_done, 2 * g + 2)
                    ve.tensor_copy(bt[:, :], ps[:, 2, 0:P])
                    ve.tensor_tensor(out=cbm[:, :, :], in0=ps[:, 2, P:3 * P].rearrange("p (c i) -> p c i", c=MT),
                                     in1=causal[:, :].unsqueeze(1).to_broadcast([P, MT, P]), op=ALU.mult)\
                        .then_inc(cb_ready, 1)
                if (unit, i) == INTRA[first]:
                    dve.wait_ge(cb_ready, g + 1)
                    for c in range(MT):
                        dve.wait_ge(decay_done, 2 * g + c + 1)
                        ve.tensor_tensor(out=m[:, c, :, :], in0=m[:, c, :, :],
                                         in1=cbm[:, c, :].unsqueeze(1).to_broadcast([P, R, P]), op=ALU.mult)\
                            .then_inc(mt_ready, 1)
                if (unit, i) == ("z", 7):
                    dve.wait_ge(y_done, g + 1)
                    dve.wait_ge(pool_ready, g + 1)
                    by_head = lambda ap: ap.rearrange("p (r d) -> p r d", r=R)
                    chain.mark(ve.tensor_tensor(out=by_head(xd[:, 1, :]), in0=by_head(ps[:, 2, :]),
                                                in1=column_bcast(ecum[:, bass.ds(g * R, R)], PD), op=ALU.mult))
                    chain.mark(ve.tensor_tensor(out=yg[:, :, :], in0=yg[:, :, :], in1=ps[:, 5:7, :], op=ALU.add))
                    chain.wait()
                    link(ve.tensor_tensor(out=yg[:, 1, :], in0=yg[:, 1, :], in1=xd[:, 1, :], op=ALU.add))
                    dve.wait_ge(zs_ready, g + 1)
                    ve.tensor_tensor(out=yg[:, :, :], in0=yg[:, :, :], in1=zs[:, :, :], op=ALU.mult).then_inc(gated, 1)

            dve.wait_ge(y_zeroed, 1)
            steps(mix, 1, MIX_FIRST, lambda u, i: mix_step(True, 0, u, i))
            with dve.Fori(0, G - 1) as t:
                chain.enter(t, 41)
                steps(mix, 21, MIX_BODY, lambda u, i: mix_step(False, t + 1, u, i), t, 28)
            chain.leave(G - 1, 41)
            dve.wait_ge(g_sq, 2 * G)
            inverse_rms(rsg, ssg, BLK, 1e-5)
            diagonal(rsg, g_ready)
            dve.wait_ge(b_hi, G)
            block_lo()
            steps(mix, 217, ACC, lambda u, i: add_output(mix, G - 1, i), urgent=True)
            residual(0)
            normed(1, (32,), (xhi,), (xlo,))

            def mlp(ph, r):
                def up(which, b):
                    dve.wait_ge(b_hi, ph.features(b))
                    for n in range(2):
                        chain.mark(ve.tensor_tensor(out=sq[:, n, :], in0=relu[:, n, :], in1=relu[:, n, :], op=ALU.mult))
                    for n in range(2):
                        chain.wait(back=1 - n)
                        last = ve.tensor_tensor(
                            out=blo[which][:, 2 * n:2 * n + 2, :].rearrange("p f s -> p (f s)"), in0=sq[:, n, :],
                            in1=bhi[which][:, 2 * n:2 * n + 2, :].rearrange("p f s -> p (f s)").bitcast(F32), op=ALU.subtract)
                    last.then_inc(h_ready, 1)

                def step(unit, i, b):
                    if unit[:2] == "up" and i == 7:
                        up(int(unit[2:] or 0), b + {"up": 0, "up1": 1, "up0": 2}[unit])
                    if unit[:3] == "acc":
                        add_output(ph, b + int(unit[3:]), i)

                dve.wait_ge(y_zeroed, r + 1)
                steps(ph, 0, MLP_FIRST, lambda u, i: step(u, i, 0))
                with dve.Fori(0, 7) as t:
                    chain.enter(t, 4)
                    steps(ph, 8, MLP_BODY, lambda u, i: step(u, i, 2 * t), t, 32)
                chain.leave(7, 4)
                steps(ph, 232, MLP_LAST, lambda u, i: step(u, i, 14), urgent=True)

            mlp(mlp0, 1)
            residual(1)
            normed(2, (16, 64), (xhi, khi), (xlo, klo))

            def attend(j, p, at_steps=HEADS_AT):
                for i in range(HG):
                    n = HG * p + i
                    if j == at_steps[0][i]:
                        dve.wait_ge(lg_done, n + 1)
                        dve.wait_ge(tab_in, 16 * (p + 1))
                        l = lg[i % 2]
                        for cols, bias in ((slice(0, S), tab[:, i, :]), (slice(S, S + P), tab[:, i, P:])):
                            for c in range(2):
                                last = ve.scalar_tensor_tensor(out=l[:, c, cols], in0=ps[:, 2 + 5 * c, cols], scalar=DH ** -0.5,
                                                               in1=bias, op0=ALU.mult, op1=ALU.add)
                            chain.mark(last)
                        chain.wait(back=1)
                        ve.tensor_reduce(nmax[i % 2][:, 0:2], l[:, :, 0:S], AX, ALU.max, negate=True)
                        chain.wait()
                        ve.tensor_reduce(nmax[i % 2][:, 2:4], l[:, :, S:], AX, ALU.max, negate=True).then_inc(lg_ready, 1)
                    if j == at_steps[0][i] + 2:
                        dve.wait_ge(ex_ready, n + 1)
                        if i >= 2:
                            dve.wait_ge(at_t, n - 1)
                        l, a = lg[i % 2], at[i % 2]
                        link(ve.reciprocal(rinv[:, :], psum_[i % 2][:, :]))
                        link(ve.tensor_tensor(out=rinv[:, 1:4:2], in0=rinv[:, 1:4:2],
                                              in1=neglam[:, 0:1].to_broadcast([P, 2]), op=ALU.mult))
                        for q, cols in enumerate((slice(0, S), slice(S, S + P))):
                            chain.mark(ve.tensor_scalar(l[:, 1, cols], l[:, 1, cols], rinv[:, 2 * q + 1:2 * q + 2], None,
                                                        ALU.mult))
                        for q, cols in enumerate((slice(0, S), slice(S, S + P))):
                            chain.wait(back=1 - q)
                            last = ve.scalar_tensor_tensor(out=a[:, cols], in0=l[:, 0, cols], scalar=rinv[:, 2 * q:2 * q + 1],
                                                           in1=l[:, 1, cols], op0=ALU.mult, op1=ALU.add)
                        last.then_inc(at_ready, 1)
                    if j == at_steps[0][i] + 6:
                        dve.wait_ge(o_sq, 2 * n + 2)
                        ve.tensor_copy(ob[:, :, :], ps[:, 6, 0:S].rearrange("p (c e) -> p c e", c=MT)).then_inc(o_ready, 1)
                        inverse_rms(rsa, ssa, P, 1e-5)
                        diagonal(rsa, o_ready)
                    if j == at_steps[1][i]:
                        dve.wait_ge(b_hi, att.ready0 + n + 1)
                        ve.scalar_tensor_tensor(out=blo[0][:, i, :], in0=ps[:, i % 2, 0:S], scalar=subw[:, :],
                                                in1=bhi[0][:, i, :].bitcast(F32), op0=ALU.mult, op1=ALU.subtract)\
                            .then_inc(h_ready, 1)

            def att_step(first, g, unit, i):
                if unit in "qk" and not first:
                    attend(i + 8 * (unit == "k"), g - 1)
                if unit == "acc":
                    add_output(att, g - 1, i)

            dve.wait_ge(y_zeroed, 3)
            dve.wait_ge(subw_ready, 1)
            steps(att, 0, ATT_FIRST, lambda u, i: att_step(True, 0, u, i))
            with dve.Fori(0, QG - 1) as t:
                chain.enter(t, 88)
                steps(att, 24, ATT_BODY, lambda u, i: att_step(False, t + 1, u, i), t, 32)
            chain.leave(QG - 1, 88)
            for j in range(15):
                attend(j, QG - 1, LAST_AT)
            steps(att, 120, ACC, lambda u, i: add_output(att, QG - 1, i), urgent=True)
            residual(2)
            normed(3, (48,), (xhi,), (xlo,))
            mlp(mlp1, 3)
            residual(3)

        @block.tensor
        def _(pe):
            te = nc.tensor

            def three(outs, lhs, rhs, start, stop):
                (lh, ll), (rh, rl) = lhs, rhs
                te.matmul(outs, lh, rh, start=start, stop=False, skip_group_check=True)
                te.matmul(outs, lh, rl, start=False, stop=False, skip_group_check=True)
                return te.matmul(outs, ll, rh, start=False, stop=stop, skip_group_check=True)

            def slot(s, tiles):
                return [t[:, s.split, :].rearrange("p (t n) -> p t n", t=tiles) for t in (whi, wlo)]

            def feature_major(s, i, bank, x, tiles=2, cols=BLK, half=0, last_i=7):
                pe.wait_ge(lo_ready, s.n + 1)
                wh, wl = slot(s, tiles)
                for f in range(cols // P):
                    for j in range(tiles):
                        k = i * tiles + j
                        dst = ps[:, bank + f // 2, (f % 2 + half) * S:(f % 2 + half + 1) * S]
                        c = slice(f * P, (f + 1) * P)
                        last = three(dst, (wh[:, j, c], wl[:, j, c]), (x[0][:, k, :], x[1][:, k, :]),
                                     start=(k == 0 and f % 2 + half == 0), stop=(i == last_i and j == tiles - 1))
                last.then_inc(slab_used, 1)

            def token_major(s, i, slabs, bank, x, tiles=2, cols=BLK):
                pe.wait_ge(lo_ready, s.n + 1)
                wh, wl = slot(s, tiles)
                for t in range(MT):
                    for j in range(tiles):
                        k = i * tiles + j
                        c = slice(t * P, (t + 1) * P)
                        if cols == BLK:
                            dst, start = ps[:, bank + t, :], k == 0
                        else:
                            dst, start = ps[:, bank, t * cols:(t + 1) * cols], k == 0 and t == 0
                        last = three(dst, (x[0][:, k, c], x[1][:, k, c]), (wh[:, j, :], wl[:, j, :]),
                                     start=start, stop=(i == slabs - 1 and j == tiles - 1))
                last.then_inc(slab_used, 1)

            def output(ph, s, i, b, which=0):
                nt = i // 2
                if i == 0:
                    pe.wait_ge(h_ready, ph.features(b))
                a = 4 * (ph.block0 + b) + nt
                if i % 2 == 0 and (nt >= 2 or ph in (mlp0, mlp1)):
                    pe.wait_ge(acc_added, a - 1)
                token_major(s, i % 2, 2, 3 + 2 * (nt % 2), (bhi[which], blo[which]))

            def transpose_x(r):
                pe.wait_ge(rms_ready, MT * (r + 1))
                for i in range(KT // 2):
                    for j in range(2):
                        for t in range(MT):
                            k = 2 * i + j
                            last = te.matmul(ps[:, i, j * S + t * P:j * S + (t + 1) * P], h[:, t, k * P:(k + 1) * P],
                                             diag[:, t, :], start=True, stop=True, skip_group_check=True)
                    last.then_inc(xt_done, 1)

            x, xk = (xhi, xlo), (khi, klo)

            pe.wait_ge(consts_ready, 1)
            pe.wait_ge(small_in, 16 * SMALL_LOADS)
            for i in range(4):
                last = te.transpose(ps[:, 0, i * P:(i + 1) * P], par_rows[:, i, :], ident[:, :])
            last.then_inc(par_t, 1)
            pe.wait_ge(par_ready, 1)
            transpose_x(0)
            pe.wait_ge(x_lo, 8)
            token_major(mix.slab(0), 0, 1, 7, x, tiles=16, cols=NH)

            def spread(g):
                pe.wait_ge(silu_done, 2 * g + 2)
                for c in range(MT):
                    for f in range(4):
                        last = te.transpose(ps[:, c, f * P:(f + 1) * P], conv[:, f, c * P:(c + 1) * P], ident[:, :])
                last.then_inc(spread_done, 1)
                te.transpose(ps[:, 2, 0:P], conv[:, 4, 0:P], ident[:, :])
                for c in range(MT):
                    cs = slice(c * P, (c + 1) * P)
                    last = te.matmul(ps[:, 2, (c + 1) * P:(c + 2) * P], conv[:, 4, cs], conv[:, 5, cs],
                                     start=True, stop=True, skip_group_check=True)
                last.then_inc(spread_done, 1)

            def mix_step(first, g, unit, i, s):
                if unit == "xs":
                    feature_major(s, i, 0, x)
                if unit == "bc":
                    if i == 0 and not first:
                        pe.wait_ge(gated, g)
                    feature_major(s, i % 2, 2, x, tiles=8, cols=P, half=i // 2, last_i=1)
                if unit == "z":
                    if i == 0 and not first:
                        pe.wait_ge(acc_added, 4 * g - 1)
                    token_major(s, i, 8, 3, x)
                if unit == "acc":
                    output(mix, s, i, g - 1)
                if (unit, i) == ("xs", 7) and not first:
                    transpose_block(g)
                if first and (unit, i) == ("xs", 3):
                    decays()
                if (unit, i) == SPREAD[first]:
                    spread(g)
                if (unit, i) == STATE[first]:
                    pe.wait_ge(cb_ready, g + 1)
                    pe.wait_ge(pool_ready, g + 1)
                    te.matmul(ps[:, 7, :], bt[:, :], xe[:, :], start=True, stop=True).then_inc(state_done, 1)
                if (unit, i) == ("z", 7):
                    if not first:
                        pe.wait_ge(acc_added, 4 * g)
                    for c in range(MT):
                        pe.wait_ge(mt_ready, 2 * g + c + 1)
                        for r in range(R):
                            te.matmul(ps[:, 5 + c, r * PD:(r + 1) * PD], m[:, c, r, :], xd[:, c, r * PD:(r + 1) * PD],
                                      start=True, stop=True, skip_group_check=True)
                    pe.wait_ge(state_ready, g + 1)
                    te.matmul(ps[:, 2, :], conv[:, 5, P:], state[:, :], start=True, stop=True).then_inc(y_done, 1)

            def decays():
                pe.wait_ge(da_ready, 1)
                for c in range(MT):
                    te.matmul(ps[:, 7, c * NH:(c + 1) * NH], causal[:, :], da[:, c, :], start=True, stop=True,
                              skip_group_check=True)
                te.matmul(ps[:, 7, 2 * NH:3 * NH], ones[:, :], da[:, 0, :], start=True, stop=True,
                          skip_group_check=True).then_inc(cum_done, 1)

            def transpose_block(g):
                pe.wait_ge(g_ready, 2 * g)
                for c in range(MT):
                    for f in range(4):
                        last = te.matmul(ps[:, 5 + f // 2, (f % 2) * S + c * P:(f % 2) * S + (c + 1) * P],
                                         yg[:, c, f * P:(f + 1) * P], diag[:, c, :], start=True, stop=True,
                                         skip_group_check=True)
                last.then_inc(gt_done, 1)

            for k, (unit, i) in enumerate(MIX_FIRST):
                mix_step(True, 0, unit, i, mix.slab(1 + k))
                if (unit, i) == ("xs", 6):
                    pe.wait_ge(cum_ready, 1)
                    for c in range(MT):
                        last = te.transpose(ps[0:NH, 7, c * P:(c + 1) * P], cum[:, c, :], ident[:, :])
                    last.then_inc(cumt_done, 1)
            with pe.Fori(0, G - 1) as t:
                for k, (unit, i) in enumerate(MIX_BODY):
                    mix_step(False, t + 1, unit, i, mix.slab(21 + k, t, 28))
            transpose_block(G)
            for k, (unit, i) in enumerate(ACC):
                output(mix, mix.slab(217 + k), i, G - 1)
            transpose_x(1)

            def mlp(ph, r):
                def up(s, i, b):
                    if i == 0 and above(b):
                        pe.wait_ge(b_hi, ph.features(b - 1))
                    feature_major(s, i, 0, x)

                def step(unit, i, b, s):
                    if unit[:2] == "up":
                        up(s, i, b + {"up": 0, "up1": 1, "up0": 2}[unit])
                    else:
                        output(ph, s, i, b + int(unit[3:]), int(unit[3:]))

                for k, (unit, i) in enumerate(MLP_FIRST):
                    pe.wait_ge(x_lo, 8 * r + max(2, i + 1))
                    step(unit, i, 0, ph.slab(k))
                with pe.Fori(0, 7) as t:
                    for k, (unit, i) in enumerate(MLP_BODY):
                        step(unit, i, 2 * t, ph.slab(8 + k, t, 32))
                for k, (unit, i) in enumerate(MLP_LAST):
                    step(unit, i, 14, ph.slab(232 + k))

            mlp(mlp0, 1)
            transpose_x(2)

            def attend(j, p, q_done, at_steps=HEADS_AT):
                for i in range(HG):
                    n = HG * p + i
                    if j == at_steps[0][i]:
                        if i > 0:
                            pe.wait_ge(lg_ready, n)
                        for c in range(2):
                            cs = slice(c * DH, (c + 1) * DH)
                            te.matmul(ps[:, 2 + 5 * c, 0:S], qt[cs, i, P:], kt_[cs, i, :], start=True, stop=True,
                                      skip_group_check=True)
                            last = te.matmul(ps[:, 2 + 5 * c, S:S + P], qt[cs, i, 0:P], kt_[cs, i, 0:P], start=True,
                                             stop=True, skip_group_check=True)
                        last.then_inc(lg_done, 1)
                    if j == at_steps[0][i] + 6:
                        pe.wait_ge(at_copied, n + 1)
                        if above(n):
                            pe.wait_ge(o_ready, 3 * n)
                        te.matmul(ps[:, 6, P:2 * P], att_t[:, 0:P], v[:, 0, i * P:(i + 1) * P], start=True, stop=False,
                                  skip_group_check=True)
                        te.matmul(ps[:, 6, P:2 * P], att_t[:, P:2 * P], v[:, 1, i * P:(i + 1) * P], start=False, stop=True,
                                  skip_group_check=True)
                        te.matmul(ps[:, 6, 0:P], att_t[:, 2 * P:], v[:, 0, i * P:(i + 1) * P], start=True, stop=True,
                                  skip_group_check=True).then_inc(o_done, 1)
                    if j == at_steps[1][i]:
                        pe.wait_ge(o_ready, 3 * (n + 1))
                        pe.wait_ge(q_copied, q_done)
                        if i >= 2:
                            pe.wait_ge(h_ready, att.ready0 + n - 1)
                        for c in range(MT):
                            last = te.matmul(ps[:, i % 2, c * P:(c + 1) * P], ob[:, c, :], diag[:, c, :],
                                             start=True, stop=True, skip_group_check=True)
                        last.then_inc(ot_done, 1)
                    if j == at_steps[0][i] + 4:
                        pe.wait_ge(at_ready, n + 1)
                        if i > 0:
                            pe.wait_ge(at_copied, n)
                        for b in range(3):
                            last = te.transpose(ps[:, 5, b * P:(b + 1) * P], at[i % 2][:, b * P:(b + 1) * P], ident[:, :])
                        last.then_inc(at_t, 1)

            def att_step(first, g, unit, i, s):
                if unit == "q":
                    feature_major(s, i, 0, x)
                if unit == "k":
                    feature_major(s, i, 3, xk)
                if unit == "v":
                    if i == 0 and not first:
                        pe.wait_ge(o_ready, 3 * HG * g)
                    token_major(s, i, 8, 5, xk)
                if unit == "acc":
                    if i == 0:
                        pe.wait_ge(k_copied, g + 1)
                    if i == 2:
                        pe.wait_ge(v_copied, g + 1)
                    output(att, s, i, g - 1)
                if unit in "qk" and not first:
                    if (unit, i) == ("q", 0):
                        pe.wait_ge(v_copied, g)
                    if (unit, i) == ("q", 3):
                        pe.wait_ge(acc_added, NT * (att.block0 + g - 1))
                    attend(i + 8 * (unit == "k"), g - 1, g + 1)

            for k, (unit, i) in enumerate(ATT_FIRST):
                if k < 8:
                    pe.wait_ge(x_lo, 16 + max(2, i + 1))
                att_step(True, 0, unit, i, att.slab(k))
            with pe.Fori(0, QG - 1) as t:
                for k, (unit, i) in enumerate(ATT_BODY):
                    att_step(False, t + 1, unit, i, att.slab(24 + k, t, 32))
            pe.wait_ge(v_copied, QG)
            for j in range(15):
                attend(j, QG - 1, QG, LAST_AT)
            for k, (unit, i) in enumerate(ACC):
                output(att, att.slab(120 + k), i, QG - 1)
            transpose_x(3)
            mlp(mlp1, 3)


INPUTS = ["x", "a_in_proj", "a_conv_w", "a_conv_b", "a_dt_bias", "a_A_log", "a_D", "a_gate_norm_w", "a_out_proj",
          "kv_norm_w", "w_k", "w_v", "rel_bias", "b_w_q", "b_lambda_q1", "b_lambda_k1", "b_lambda_q2", "b_lambda_k2",
          "b_subln_w", "b_out_proj", "norm_pre_mix", "norm_post_mix", "norm_pre_mlp", "norm_post_mlp",
          "mlp_w1", "mlp_w2"]


def kernel(**inputs):
    import concourse.bacc as bacc
    from concourse.bass_utils import run_bass_kernel_spmd

    nc = bacc.Bacc("TRN2", target_bir_lowering=False, num_devices=1)
    arrays, aps = {}, {}
    for name in INPUTS:
        arrays[name] = np.ascontiguousarray(inputs[name])
        aps[name] = nc.dram_tensor(name, arrays[name].shape, mybir.dt.from_np(arrays[name].dtype),
                                   kind="ExternalInput").ap()
    out = nc.dram_tensor("out", (1, S, D), F32, kind="ExternalOutput").ap()
    build(nc, aps, out)
    return run_bass_kernel_spmd(nc, [arrays], core_ids=[0]).results[0]["out"]
```

```python
from contextlib import ExitStack

import numpy as np
import concourse.bass as bass
from concourse import mybir

F32 = mybir.dt.float32
F32R = mybir.dt.float32r
I32 = mybir.dt.int32
BF16 = mybir.dt.bfloat16
ALU = mybir.AluOpType
ACT = mybir.ActivationFunctionType
AX = mybir.AxisListType.X

P = 128
D = 2048
S = 256
MT = S // P
DI = 2 * D
G = 8
R = 8
PD = 64
NS = 128
NH = G * R
TAPS = 4
XBC0 = DI
B0 = XBC0 + DI
C0 = B0 + G * NS
DT0 = C0 + G * NS
HEADS = 16
HG = 4
QG = HEADS // HG
DH = 64
FF = 4 * D
BLK = 512
KT = D // P
NT = D // BLK
PIECES = 4
BUCKETS = 32
MAX_DISTANCE = 128
LAMBDA_INIT = 0.8 - 0.6 * float(np.exp(-0.3))
MASKED = -1.0e30
LEAD = 4
SLAB = 1024
SMALL_LOADS = 10
RING = 4


def bucket_bounds():
    exact = BUCKETS // 2
    n = np.arange(S)
    large = exact + (np.log(np.maximum(n, 1).astype(np.float32) / exact)
                     / np.float32(np.log(MAX_DISTANCE / exact)) * (BUCKETS - exact)).astype(np.int32)
    bucket = np.where(n < exact, n, np.minimum(large, BUCKETS - 1))
    return [int(np.argmax(bucket >= b)) for b in range(BUCKETS)] + [S]


class Plan:

    def __init__(self, logits, weigh, turn_weights, out, turn_out, weights_bank, out_bank, turned_banks):
        self.logits, self.weigh, self.turn_weights = logits, weigh, turn_weights
        self.out, self.turn_out = out, turn_out
        self.weights_bank, self.out_bank, self.turned_banks = weights_bank, out_bank, turned_banks


USUAL_PLAN = Plan((-7, -4, 0, 2), (-5, -2, 4, 6), (3, 5, 7, 9), (5, 7, 9, 11), (7, 9, 11, 13),
                  5, 6, (7, 2, 7, 2))
LAST_PLAN = Plan((-7, -4, 0, 2), (-5, -2, 2, 4), (1, 3, 5, 6), (3, 5, 6, 7), (8, 9, 10, 11),
                 0, 1, (7, 2, 0, 1))
LAST_STEPS = range(8, 12)


class Slab:

    def __init__(self, n, number):
        self.n = number
        self.raw, self.split = n % RING, n % LEAD
        self.used = number + 1
        self.arrived = 16 * (n // RING + 1)


class Phase:

    def __init__(self, slabs, blocks, before, per_block=1):
        self.slabs, self.blocks, self.per_block, self.next = slabs, blocks, per_block, None
        self.first = self.block0 = self.ready0 = 0
        if before:
            before.next = self
            self.first = before.first + before.slabs
            self.block0 = before.block0 + before.blocks
            self.ready0 = before.ready0 + before.blocks * before.per_block

    def slab(self, k, t=0, per=0):
        if per == 0 and k >= self.slabs:
            return self.next.slab(k - self.slabs) if self.next else None
        assert per % LEAD == 0 and per % RING == 0
        n = self.first + k
        slab = Slab(n, n + t * per)
        slab.arrived += t * (16 * per // RING)
        return slab

    def features(self, b):
        return self.ready0 + self.per_block * (b + 1)


def above(value, floor=0):
    return not isinstance(value, int) or value > floor


def is_last(g, blocks=QG):
    return isinstance(g, int) and g == blocks - 1


class Tally:

    def __init__(self, engine, sem):
        self.engine, self.sem, self.base, self.k, self.at = engine, sem, 0, 0, 0

    def mark(self, ins):
        ins.then_inc(self.sem, 1)
        self.k += 1

    def wait(self, back=0):
        self.engine.wait_ge(self.sem, self.at + self.k - back)

    def enter(self, t, per):
        self.base, self.k = self.base + self.k, 0
        self.at = self.base + t * per

    def leave(self, trips, per):
        assert self.k == per, f"{self.k} marks in the loop body, not {per}"
        self.base, self.k = self.base + per * trips, 0
        self.at = self.base


def column_bcast(ap, n):
    return ap.unsqueeze(2).to_broadcast([ap.shape[0], ap.shape[1], n])


def piece(n):
    return slice(n * D // PIECES, (n + 1) * D // PIECES)


def build(nc, w, out):
    mix = Phase(1 + 20 + 7 * 28 + 8, G, None)
    mlp0 = Phase(8 + 7 * 32 + 24, FF // BLK, mix)
    att = Phase(24 + 3 * 32 + 8, QG, mlp0, per_block=HG)
    mlp1 = Phase(8 + 7 * 32 + 24, FF // BLK, att)

    in_proj, out_proj = w["a_in_proj"][0], w["a_out_proj"][0]
    w_q, w_k, w_v, o_proj = w["b_w_q"][0], w["w_k"], w["w_v"], w["b_out_proj"][0]

    def units(*names):
        return [(n, i) for n, c in names for i in range(c)]

    MIX_FIRST = units(("xs", 8), ("bc", 4), ("z", 8))
    MIX_BODY = units(("xs", 8), ("bc", 4), ("acc", 8), ("z", 8))
    MIX_LAST = units(("xs", 8), ("bc", 4), ("z", 8), ("acc", 8))
    ACC = units(("acc", 8))
    MLP_FIRST = units(("up", 8))
    MLP_BODY = units(("up1", 8), ("acc0", 8), ("up0", 8), ("acc1", 8))
    MLP_LAST = units(("up1", 8), ("acc0", 8), ("acc1", 8))
    ATT_FIRST = units(("q", 8), ("k", 8), ("v", 8))
    ATT_BODY = units(("q", 8), ("k", 8), ("v", 8), ("acc", 8))
    SPREAD = {True: ("z", 3), False: ("acc", 7)}
    STATE = {True: ("z", 6), False: ("z", 3)}
    SILU_BC = {True: ("z", 0), False: ("acc", 0)}
    UP_BANKS = ((0, 1), (2, 7))
    DECAY = {True: ("z", 4), False: ("acc", 3)}
    INTRA = {True: ("z", 4), False: ("acc", 7)}

    ctx = ExitStack()
    with ctx:
        def sb(name, shape, dt=F32, stack=ctx):
            return stack.enter_context(nc.sbuf_tensor(name, shape, dt))

        def sem(name):
            return ctx.enter_context(nc.semaphore(name))

        h = sb("h", [P, MT, D])
        y = sb("y", [P, MT, D])
        raw = sb("raw", [P, RING, SLAB])
        whi = sb("whi", [P, LEAD, SLAB], F32R)
        wlo = sb("wlo", [P, LEAD, SLAB], F32R)
        xhi = sb("xhi", [P, KT, S], F32R)
        xlo = sb("xlo", [P, KT, S], F32R)
        bhi = [sb("bhi0", [P, 4, S], F32R)]
        blo = [sb("blo0", [P, 4, S], F32R)]
        postw = sb("postw", [P, D])
        junk = sb("junk", [P, MT, D], BF16)
        ident = sb("ident", [P, P])
        par = sb("par", [P, 4 * P])
        subw = sb("subw", [P, 1])
        diag = sb("diag", [P, MT, P])
        part = sb("part", [P, MT, NT + PIECES])
        ssy, ssh = part[:, :, 0:NT], part[:, :, NT:]
        stat = sb("stat", [P, 20])
        sum_y, sum_h, rsy, rsh, ssg, rsg, rsa, rs_x, rs_h, rs_a = (stat[:, 2 * i:2 * i + 2] for i in range(10))
        neglam = sb("neglam", [P, 4])
        ps = ctx.enter_context(nc.psum_tensor("ps", [P, 8, BLK], F32))

        mem = ExitStack()

        def mb(name, shape, dt=F32):
            return sb(name, shape, dt, mem)

        par_rows = mb("par_rows", [P, 4, P])
        relrow = mb("relrow", [HEADS, BUCKETS])
        bias_row = mb("bias_row", [HEADS, S + P])
        lamv = mb("lamv", [P, 4, DH])
        pre = mb("pre", [P, 6, TAPS - 1 + S])
        conv = mb("conv", [P, 6, S])
        xs = mb("xs", [P, MT, BLK])
        xd = mb("xd", [P, MT, BLK])
        xe = mb("xe", [P, BLK])
        yg = mb("yg", [P, MT, BLK])
        zs = mb("zs", [P, MT, BLK])
        cumb = mb("cumb", [P, R, S])
        m = mb("m", [P, MT, R, P])
        cbm = mb("cbm", [P, MT, P])
        bt = mb("bt", [P, NS])
        state = mb("state", [NS, BLK])
        causal = mb("causal", [P, P])
        ones = mb("ones", [P, P])
        hd = mb("hd", [P, 3, NH])
        dt = mb("dt", [P, MT, NH])
        da = mb("da", [P, MT, NH])
        cum = mb("cum", [P, MT, NH])
        todend = mb("todend", [P, NH])
        ecum = mb("ecum", [P, NH])
        tmp = mb("tmp", [P, 4, MT, NH])
        cumt = mb("cumt", [NH, S])
        cpar = mb("cpar", [P, TAPS + 1, 6])
        gpar = mb("gpar", [P, 4])
        gcum = mb("gcum", [P, MT, R])
        mem.close()

        mem = ExitStack()
        relu = mb("relu", [P, MT, BLK])
        sq = mb("sq", [P, MT, BLK])
        bhi.append(mb("bhi1", [P, 4, S], F32R))
        blo.append(mb("blo1", [P, 4, S], F32R))
        mem.close()

        mem = ExitStack()
        khi = mb("khi", [P, KT, S], F32R)
        klo = mb("klo", [P, KT, S], F32R)
        qt = mb("qt", [P, HG, S])
        kt_ = mb("kt", [P, HG, S])
        v = mb("v", [P, MT, BLK])
        tab = mb("tab", [P, HG, S])
        lg = [mb(f"lg{i}", [P, 2, S + P]) for i in range(2)]
        at = [mb(f"at{i}", [P, S + P]) for i in range(2)]
        att_t = mb("att_t", [P, S + P])
        ob = mb("ob", [P, HG, MT, P])
        hdiag = mb("hdiag", [P, HG, MT, P])
        ssa = mb("ssa", [P, HG, MT])
        nmax = [mb(f"nmax{i}", [P, 4]) for i in range(2)]
        psum_ = [mb(f"psums{i}", [P, 4]) for i in range(2)]
        rinv = mb("rinv", [P, 4])
        mem.close()

        cum_dram = nc.dram_tensor("cum_scratch", [NH, S], F32, kind="Internal").ap()
        bias_dram = nc.dram_tensor("bias_scratch", [HEADS, P, S + P], F32, kind="Internal").ap()


        raw_in = [sem(f"raw_in{i}") for i in range(RING)]
        hi_ready, lo_ready, slab_used = sem("hi_ready"), sem("lo_ready"), sem("slab_used")
        consts_ready, small_in, x_in = sem("consts_ready"), sem("small_in"), sem("x_in")
        heads_in, rel_in, lam_in = sem("heads_in"), sem("rel_in"), sem("lam_in")
        par_t, par_ready = sem("par_t"), sem("par_ready")
        postw_in, cum_out, cumb_in, bias_out, tab_in = (
            sem("postw_in"), sem("cum_out"), sem("cumb_in"), sem("bias_out"), sem("tab_in"))
        y_zeroed, acc_added = sem("y_zeroed"), sem("acc_added")
        y_sq, yw_ready, h_new, h_sq, rms_ready = sem("y_sq"), sem("yw_ready"), sem("h_new"), sem("h_sq"), sem("rms_ready")
        rows_cleared = sem("rows_cleared")
        xt_done, x_hi, x_lo = sem("xt_done"), sem("x_hi"), sem("x_lo")
        b_hi, h_ready = sem("b_hi"), sem("h_ready")
        dve_chain, act_chain, pool_chain = sem("dve_chain"), sem("act_chain"), sem("pool_chain")
        dt_done, dt_v, dt_e, dt_l, da_ready, cum_done, cum_ready = (
            sem("dt_done"), sem("dt_v"), sem("dt_e"), sem("dt_l"), sem("da_ready"), sem("cum_done"), sem("cum_ready"))
        cumt_done, cumt_ready, expd_ready = sem("cumt_done"), sem("cumt_ready"), sem("expd_ready")
        cpar_ready = sem("cpar_ready")
        pre_ready, conv_done, silu_done = sem("pre_ready"), sem("conv_done"), sem("silu_done")
        seg_done, decay_done = sem("seg_done"), sem("decay_done")
        spread_done, xs_ready, pool_ready, cb_ready, mt_ready = (
            sem("spread_done"), sem("xs_ready"), sem("pool_ready"), sem("cb_ready"), sem("mt_ready"))
        state_done, state_ready, y_done, zs_ready = (
            sem("state_done"), sem("state_ready"), sem("y_done"), sem("zs_ready"))
        gated, g_sq, g_ready, gt_done = sem("gated"), sem("g_sq"), sem("g_ready"), sem("gt_done")
        q_copied, k_copied, v_copied = sem("q_copied"), sem("k_copied"), sem("v_copied")
        lg_done, lg_ready, ex_ready, at_ready, at_t, at_copied = (
            sem("lg_done"), sem("lg_ready"), sem("ex_ready"), sem("at_ready"), sem("at_t"), sem("at_copied"))
        o_done, o_sq, o_ready, ot_done = sem("o_done"), sem("o_sq"), sem("o_ready"), sem("ot_done")
        lam_ready, lam_e, subw_ready = sem("lam_ready"), sem("lam_e"), sem("subw_ready")
        stored = sem("stored")

        block = ctx.enter_context(nc.Block())

        @block.sync
        def _(sp):
            def load(s, src, tiles):
                free = sp.lower_val(s.n + 1 - RING if isinstance(s.n, int) else sp.snap(s.n + 1 - RING))
                dst = raw[:, s.raw, :].rearrange("p (t n) -> p t n", t=tiles)
                dma = sp.dma_start(dst, src.rearrange("(t p) n -> p t n", p=P))
                if above(s.n, RING - 1):
                    dma.wait_op(lo_ready, free, "sem-ge")
                dma.then_inc(raw_in[s.raw], 16)

            def tile(mat, row, rows, col, cols):
                return mat[bass.ds(row, rows), bass.ds(col, cols)]

            def mix_load(s, unit, i, g):
                if unit == "xs":
                    load(s, tile(in_proj, 256 * i, 256, XBC0 + g * BLK, BLK), 2)
                elif unit == "bc":
                    load(s, tile(in_proj, 1024 * (i % 2), 1024, (B0, C0)[i // 2] + g * NS, NS), 8)
                elif unit == "z":
                    load(s, tile(in_proj, 256 * i, 256, g * BLK, BLK), 2)
                else:
                    load(s, tile(out_proj, (g - 1) * BLK + 256 * (i % 2), 256, BLK * (i // 2), BLK), 2)

            for t in range(MT):
                sp.dma_start(h[:, t, :], w["x"][0, t * P:(t + 1) * P, :]).then_inc(x_in, 16)
            sp.wait_ge(small_in, 16 * SMALL_LOADS)
            load(mix.slab(0), in_proj[:, DT0:DT0 + NH], 16)
            for k, (unit, i) in enumerate(MIX_FIRST):
                mix_load(mix.slab(1 + k), unit, i, 0)
            with sp.Fori(0, G - 2) as t:
                for k, (unit, i) in enumerate(MIX_BODY):
                    mix_load(mix.slab(21 + k, t, 28), unit, i, t + 1)
            for k, (unit, i) in enumerate(MIX_LAST):
                mix_load(mix.slab(189 + k), unit, i, G - 1)
            for k, (unit, i) in enumerate(ACC):
                mix_load(mix.slab(217 + k), unit, i, G)

            def mlp(ph, layer):
                w1, w2 = w["mlp_w1"][layer], w["mlp_w2"][layer]

                def up(s, i, b):
                    load(s, tile(w1, 256 * i, 256, b * BLK, BLK), 2)

                def down(s, i, b):
                    load(s, tile(w2, b * BLK + 256 * (i % 2), 256, BLK * (i // 2), BLK), 2)

                for k, (unit, i) in enumerate(MLP_FIRST):
                    up(ph.slab(k), i, 0)
                with sp.Fori(0, 7) as t:
                    for k, (unit, i) in enumerate(MLP_BODY):
                        s = ph.slab(8 + k, t, 32)
                        if unit == "up1":
                            up(s, i, 2 * t + 1)
                        elif unit == "up0":
                            up(s, i, 2 * t + 2)
                        else:
                            down(s, i, 2 * t + (unit == "acc1"))
                for k, (unit, i) in enumerate(MLP_LAST):
                    s = ph.slab(232 + k)
                    if unit == "up1":
                        up(s, i, 15)
                    else:
                        down(s, i, 14 + (unit == "acc1"))

            mlp(mlp0, 0)

            def att_load(s, unit, i, g):
                if unit == "acc":
                    load(s, tile(o_proj, (g - 1) * BLK + 256 * (i % 2), 256, BLK * (i // 2), BLK), 2)
                else:
                    load(s, tile({"q": w_q, "k": w_k, "v": w_v}[unit], 256 * i, 256, g * BLK, BLK), 2)

            for k, (unit, i) in enumerate(ATT_FIRST):
                att_load(att.slab(k), unit, i, 0)
            with sp.Fori(0, QG - 2) as t:
                for k, (unit, i) in enumerate(ATT_BODY):
                    att_load(att.slab(24 + k, t, 32), unit, i, t + 1)
            for k, (unit, i) in enumerate(ATT_BODY):
                att_load(att.slab(88 + k), unit, i, QG - 1)
            for k, (unit, i) in enumerate(ACC):
                att_load(att.slab(120 + k), unit, i, QG)
            mlp(mlp1, 1)
            for n in range(MT * PIECES):
                sp.wait_ge(h_new, 3 * MT * PIECES + n + 1)
                t, cols = n // PIECES, piece(n % PIECES)
                sp.dma_start(out[0, t * P:(t + 1) * P, cols], h[:, t, cols]).then_inc(stored, 16)
            sp.wait_ge(stored, 16 * MT * PIECES)

        @block.gpsimd
        def _(pool):
            chain = Tally(pool, pool_chain)
            g_ = nc.gpsimd

            g_.memset(pre[:, :, 0:TAPS - 1], 0.0)
            g_.memset(ones[:, :], 1.0)
            chain.mark(g_.memset(ident[:, :], 0.0))
            chain.mark(g_.memset(causal[:, :], 1.0))
            chain.wait()
            g_.affine_select(out=ident[:, :], in_=ident[:, :], compare_op=ALU.not_equal, fill=1.0, base=0,
                             pattern=[[-1, P]], channel_multiplier=1)
            g_.affine_select(out=causal[:, :], in_=causal[:, :], compare_op=ALU.is_ge, fill=0.0, base=0,
                             pattern=[[1, P]], channel_multiplier=-1).then_inc(consts_ready, 1)

            for i, name in enumerate(("a_dt_bias", "a_A_log", "a_D")):
                pool.dma_start(hd[:, i, :], w[name][0].partition_broadcast(P)).then_inc(heads_in, 16)
            for i, name in enumerate(("b_lambda_q1", "b_lambda_k1", "b_lambda_q2", "b_lambda_k2")):
                pool.dma_start(lamv[:, i, :], w[name][0].partition_broadcast(P)).then_inc(lam_in, 16)
            pool.dma_start(relrow[:, :], w["rel_bias"].rearrange("b h -> h b"), allow_slow_non_contiguous=True)\
                .then_inc(rel_in, 16)
            pool.dma_start(postw[:, :], w["norm_post_mix"][0].partition_broadcast(P)).then_inc(postw_in, 16)

            pool.wait_ge(rel_in, 16)
            bounds = bucket_bounds()
            g_.memset(bias_row[:, S:S + P], MASKED)
            for b in range(BUCKETS):
                lo, hi = S - bounds[b + 1], S - bounds[b]
                last = g_.tensor_copy(bias_row[:, lo:hi], relrow[:, b:b + 1].to_broadcast([HEADS, hi - lo]))
            chain.mark(last)
            chain.wait()
            pool.dma_start(bias_dram, bias_row[:, :].unsqueeze(1).to_broadcast([HEADS, P, S + P])).then_inc(bias_out, 16)

            def zero_y(r):
                if r > 0:
                    pool.wait_ge(h_new, MT * PIECES * r)
                g_.memset(y[:, :, :], 0.0).then_inc(y_zeroed, 1)

            def weigh_y(r):
                pool.wait_ge(postw_in, 16 * (r + 1))
                for nt in range(NT):
                    pool.wait_ge(y_sq, MT * (NT * r + nt + 1))
                    cols = slice(nt * BLK, (nt + 1) * BLK)
                    g_.tensor_tensor(out=y[:, :, cols], in0=y[:, :, cols],
                                     in1=postw[:, cols].unsqueeze(1).to_broadcast([P, MT, BLK]),
                                     op=ALU.mult).then_inc(yw_ready, 1)

            def next_postw(r, vec):
                pool.wait_ge(yw_ready, NT * r)
                pool.dma_start(postw[:, :], vec.partition_broadcast(P)).then_inc(postw_in, 16)

            zero_y(0)

            def group(g):
                if above(g):
                    pool.wait_ge(silu_done, 2 * g)
                    pool.wait_ge(seg_done, g)
                for lo, n, at0 in ((0, 4, g * 4), (4, 1, 32 + g), (5, 1, 40 + g)):
                    for tp in range(TAPS + 1):
                        col = P * (1 + tp // 2) + 48 * (tp % 2)
                        g_.tensor_copy(cpar[:, tp, lo:lo + n], par[:, bass.ds(col + at0, n)])
                g_.tensor_copy(gcum[:, :, :], cum[:, :, bass.ds(g * R, R)]).then_inc(cpar_ready, 1)
                if not above(g):
                    pool.wait_ge(cumt_ready, 1)
                    pool.dma_start(cum_dram, cumt[:, :]).then_inc(cum_out, 16)
                    pool.wait_ge(cum_out, 16)
                src = cum_dram[bass.ds(g * R, R), :].rearrange("r s -> (r s)").partition_broadcast(P)
                pool.dma_start(cumb[:, :, :].rearrange("p r s -> p (r s)"), src).then_inc(cumb_in, 16)
                pool.wait_ge(xs_ready, g + 1)
                if above(g):
                    pool.wait_ge(gt_done, g)
                    pool.wait_ge(h_ready, g)
                chain.mark(g_.tensor_copy(gpar[:, :], par[:, bass.ds(80 + g * 4, 4)]))
                for c in range(MT):
                    last = g_.tensor_tensor(
                        out=xd[:, c, :].rearrange("p (r d) -> p r d", r=R), in0=xs[:, c, :].rearrange("p (r d) -> p r d", r=R),
                        in1=column_bcast(dt[:, c, bass.ds(g * R, R)], PD), op=ALU.mult)
                    chain.mark(last)
                    if c == 0:
                        chain.wait()
                        g_.tensor_tensor(out=xe[:, :].rearrange("p (r d) -> p r d", r=R),
                                         in0=xd[:, 0, :].rearrange("p (r d) -> p r d", r=R),
                                         in1=column_bcast(todend[:, bass.ds(g * R, R)], PD),
                                         op=ALU.mult)
                for c in range(MT):
                    last = g_.tensor_tensor(
                        out=yg[:, c, :].rearrange("p (r d) -> p r d", r=R), in0=xs[:, c, :].rearrange("p (r d) -> p r d", r=R),
                        in1=column_bcast(hd[:, 2, bass.ds(g * R, R)], PD), op=ALU.mult)
                last.then_inc(pool_ready, 1)

            pool.wait_ge(expd_ready, 1)
            pool.wait_ge(par_ready, 1)
            group(0)
            with pool.Fori(0, G - 1) as t:
                chain.enter(t, 3)
                group(t + 1)
            chain.leave(G - 1, 3)
            pool.wait_ge(bias_out, 16)
            weigh_y(0)
            next_postw(1, w["norm_post_mlp"][0])
            zero_y(1)
            weigh_y(1)
            next_postw(2, w["norm_post_mix"][1])
            zero_y(2)

            def tab_load(g):
                src = bass.AP(tensor=bias_dram.tensor, offset=g * (HG * P * (S + P)) + P - 1,
                              ap=[[S + P - 1, P], [P * (S + P), HG], [1, S]])
                pool.dma_start(tab[:, :, :], src).then_inc(tab_in, 16)

            pool.wait_ge(h_new, 2 * MT * PIECES)
            tab_load(0)
            with pool.Fori(0, QG - 1) as t:
                pool.wait_ge(lg_ready, HG * (t + 1))
                tab_load(t + 1)
            weigh_y(2)
            next_postw(3, w["norm_post_mlp"][1])
            zero_y(3)
            weigh_y(3)

        @block.scalar
        def _(act):
            chain = Tally(act, act_chain)
            sc = nc.scalar

            def split(s):
                act.wait_ge(raw_in[s.raw], s.arrived)
                if above(s.n, LEAD - 1):
                    act.wait_ge(slab_used, s.n - LEAD + 1)
                sc.activation(whi[:, s.split, :], raw[:, s.raw, :], ACT.Copy).then_inc(hi_ready, 1)

            def square_sum(t, src, dst, done, at0=0):
                sc.activation(junk[:, t, at0:at0 + src.shape[-1]], src, ACT.Square, accum_out=dst).then_inc(done, 1)

            def square_sums(r, first_h=False):
                for n in range(MT * PIECES):
                    t, p = n // PIECES, n % PIECES
                    if first_h:
                        act.wait_ge(x_in, 16 * MT)
                    else:
                        act.wait_ge(h_new, MT * PIECES * (r - 1) + n + 1)
                    square_sum(t, h[:, t, piece(p)], ssh[:, t, p:p + 1], h_sq, p * D // PIECES)

            def normed(r, cols, outs):
                for i in range(KT // 2):
                    act.wait_ge(xt_done, 8 * r + i + 1)
                    for dst, col in zip(outs, cols):
                        for j in range(2):
                            k = 2 * i + j
                            last = sc.activation(dst[:, k, :], ps[:, i, j * S:(j + 1) * S], ACT.Copy,
                                                 scale=par[:, col + k:col + k + 1])
                    last.then_inc(x_hi, 1)

            def output_norm(ph, i):
                for nt in {2: (0,), 4: (1,), 6: (2,), 7: (3,)}.get(i, ()):
                    act.wait_ge(acc_added, NT * (ph.block0 + ph.blocks - 1) + nt + 1)
                    for t in range(MT):
                        square_sum(t, y[:, t, nt * BLK:(nt + 1) * BLK], ssy[:, t, nt:nt + 1], y_sq,
                                   nt * BLK)

            def block_hi(bank=5):
                for f in range(4):
                    last = sc.activation(bhi[0][:, f, :], ps[:, bank + f // 2, (f % 2) * S:(f % 2 + 1) * S], ACT.Copy,
                                         scale=gpar[:, f:f + 1])
                last.then_inc(b_hi, 1)

            def rows(dst, lo, vec):
                n = vec.shape[0] // P
                act.dma_start(dst[lo:lo + n, :], vec.rearrange("(r c) -> r c", c=P)).then_inc(small_in, 16)

            act.wait_ge(rows_cleared, 1)
            rows(par_rows[:, 0, :], 0, w["norm_pre_mix"].rearrange("l d -> (l d)"))
            rows(par_rows[:, 0, :], 32, w["norm_pre_mlp"].rearrange("l d -> (l d)"))
            rows(par_rows[:, 0, :], 64, w["kv_norm_w"])
            rows(par_rows[:, 0, :], 80, w["a_gate_norm_w"][0])
            rows(par_rows[:, 0, :], 112, w["b_subln_w"][0])
            for tap in range(TAPS):
                rows(par_rows[:, 1 + tap // 2, :], 48 * (tap % 2), w["a_conv_w"][0, tap])
            rows(par_rows[:, 3, :], 0, w["a_conv_b"][0])
            square_sums(0, True)
            act.wait_ge(par_t, 1)
            sc.activation(par[:, :], ps[:, 0, :], ACT.Copy).then_inc(par_ready, 1)
            act.wait_ge(par_ready, 1)
            sc.mul(subw[:, :], par[:, 112:113], 1.0 - LAMBDA_INIT).then_inc(subw_ready, 1)
            for k in range(2):
                split(mix.slab(k))
            normed(0, (0,), (xhi,))
            for k in range(2, LEAD):
                split(mix.slab(k))
            split(mix.slab(LEAD))
            act.wait_ge(dt_v, 1)
            sc.activation(tmp[:, 1, :, :], tmp[:, 0, :, :], ACT.Exp, scale=-1.0)
            sc.activation(hd[:, 1, :], hd[:, 1, :], ACT.Exp).then_inc(dt_e, 1)
            act.wait_ge(dt_l, 1)
            sc.activation(tmp[:, 3, :, :], tmp[:, 2, :, :], ACT.Ln).then_inc(dt_e, 1)
            act.wait_ge(lam_ready, 1)
            sc.activation(neglam[:, 2:4], neglam[:, 0:2], ACT.Exp).then_inc(lam_e, 1)

            def mix_step(first, g, unit, i):
                z_first = first or is_last(g, G)
                group = g + 1 if unit == "acc" else g
                if ((unit, i) == ("xs", 1) and not first) or ((unit, i) == ("acc", 1) and is_last(g, G)):
                    act.wait_ge(gated, group)
                    for c in range(MT):
                        square_sum(c, yg[:, c, :], ssg[:, c:c + 1], g_sq)
                if (unit, i) == ("xs", 7):
                    if not first:
                        act.wait_ge(silu_done, 2 * g)
                    for b in range(2):
                        sc.activation(pre[:, 2 * b:2 * b + 2, TAPS - 1:], ps[:, b, :].rearrange("p (f s) -> p f s", f=2),
                                      ACT.Copy).then_inc(pre_ready, 1)
                    if first:
                        act.wait_ge(cum_ready, 1)
                        sc.activation(todend[:, :], todend[:, :], ACT.Exp)
                        sc.activation(ecum[:, :], cum[:, 1, :], ACT.Exp).then_inc(expd_ready, 1)
                    else:
                        act.wait_ge(gt_done, g)
                        block_hi()
                if (unit, i) == ("bc", 3):
                    sc.activation(pre[:, 4:6, TAPS - 1:], ps[:, 2, :].rearrange("p (f s) -> p f s", f=2),
                                  ACT.Copy).then_inc(pre_ready, 1)
                    act.wait_ge(conv_done, 2 * g + 1)
                    for f in range(4):
                        last = sc.activation(conv[:, f, :], conv[:, f, :], ACT.Silu, bias=cpar[:, TAPS, f:f + 1])
                    last.then_inc(silu_done, 1)
                if (unit, i) == SILU_BC[z_first]:
                    act.wait_ge(conv_done, 2 * g + 2)
                    for f in range(4, 6):
                        last = sc.activation(conv[:, f, :], conv[:, f, :], ACT.Silu, bias=cpar[:, TAPS, f:f + 1])
                    last.then_inc(silu_done, 1)
                if (unit, i) == DECAY[z_first]:
                    act.wait_ge(seg_done, g + 1)
                    for c in range(MT):
                        sc.activation(m[:, c, :, :], m[:, c, :, :], ACT.Exp).then_inc(decay_done, 1)
                if (unit, i) == SPREAD[z_first]:
                    act.wait_ge(spread_done, 2 * g + 1)
                    for c in range(MT):
                        last = sc.activation(xs[:, c, :], ps[:, c, :], ACT.Copy)
                    last.then_inc(xs_ready, 1)
                if (unit, i) == STATE[z_first]:
                    act.wait_ge(state_done, g + 1)
                    sc.activation(state[:, :], ps[:, 7, :], ACT.Copy).then_inc(state_ready, 1)
                if (unit, i) == ("z", 7):
                    sc.activation(zs[:, :, :], ps[:, 3:5, :], ACT.Silu).then_inc(zs_ready, 1)

            def steps(ph, first_k, order, body, t=0, per=0, urgent=False):
                for k, (unit, i) in enumerate(order):
                    ahead = ph.slab(first_k + k + LEAD, t, per)
                    if urgent and k == len(order) - 1:
                        body(unit, i)
                        if ahead:
                            split(ahead)
                        continue
                    if ahead:
                        split(ahead)
                        act.wait_ge(hi_ready, ahead.used)
                    else:
                        act.wait_ge(slab_used, ph.slab(first_k + k).used)
                    body(unit, i)

            steps(mix, 1, MIX_FIRST, lambda u, i: mix_step(True, 0, u, i))
            with act.Fori(0, G - 2) as t:
                steps(mix, 21, MIX_BODY, lambda u, i: mix_step(False, t + 1, u, i), t, 28)
            steps(mix, 189, MIX_LAST, lambda u, i: mix_step(False, G - 1, u, i))
            act.wait_ge(gt_done, G)
            block_hi(0)
            steps(mix, 217, ACC, lambda u, i: output_norm(mix, i), urgent=True)

            def mlp(ph):
                def up(which, b):
                    if above(b):
                        act.wait_ge(h_ready, ph.features(b - 1))
                    for n in range(2):
                        chain.mark(sc.activation(relu[:, n, :], ps[:, UP_BANKS[which][n], :], ACT.Relu))
                    chain.wait()
                    for n in range(2):
                        last = sc.activation(bhi[which][:, 2 * n:2 * n + 2, :].rearrange("p f s -> p (f s)"),
                                             relu[:, n, :], ACT.Square)
                    last.then_inc(b_hi, 1)

                def step(unit, i, b):
                    if i == 7 and unit[:2] == "up":
                        up(int(unit[2:] or 0), b + {"up": 0, "up1": 1, "up0": 2}[unit])

                steps(ph, 0, MLP_FIRST, lambda u, i: step(u, i, 0))
                with act.Fori(0, 7) as t:
                    chain.enter(t, 4)
                    steps(ph, 8, MLP_BODY, lambda u, i: step(u, i, 2 * t), t, 32)
                chain.leave(7, 4)
                steps(ph, 232, MLP_LAST, lambda u, i: output_norm(ph, i) if u == "acc1" else step(u, i, 14), urgent=True)

            square_sums(1)
            normed(1, (32,), (xhi,))
            mlp(mlp0)
            square_sums(2)
            normed(2, (16, 64), (xhi, khi))

            def attend(j, p, plan=USUAL_PLAN):
                for i in range(HG):
                    n = HG * p + i
                    if j == plan.logits[i] + 1:
                        act.wait_ge(lg_ready, n + 1)
                        for c in range(2):
                            sc.activation(lg[i % 2][:, c, 0:S], lg[i % 2][:, c, 0:S], ACT.Exp,
                                          bias=nmax[i % 2][:, c:c + 1], accum_out=psum_[i % 2][:, c:c + 1])
                            last = sc.activation(lg[i % 2][:, c, S:], lg[i % 2][:, c, S:], ACT.Exp,
                                                 bias=nmax[i % 2][:, 2 + c:3 + c], accum_out=psum_[i % 2][:, 2 + c:3 + c])
                        last.then_inc(ex_ready, 1)
                    if j == plan.turn_weights[i]:
                        act.wait_ge(at_t, n + 1)
                        sc.activation(att_t[:, :], ps[:, plan.weights_bank, 0:S + P], ACT.Copy).then_inc(at_copied, 1)
                    if j == plan.out[i]:
                        act.wait_ge(o_done, n + 1)
                        for c in range(MT):
                            square_sum(c, ps[:, plan.out_bank, c * P:(c + 1) * P], ssa[:, i, c:c + 1], o_sq)
                    if j == plan.turn_out[i]:
                        act.wait_ge(ot_done, n + 1)
                        sc.activation(bhi[0][:, i, :], ps[:, plan.turned_banks[i], 0:S], ACT.Copy, scale=subw[:, :]).then_inc(b_hi, 1)

            def att_step(first, g, unit, i):
                if i == 0 and unit == "k":
                    sc.activation(qt[:, :, :].rearrange("p f s -> p (f s)"), ps[:, 0:2, :].rearrange("p b n -> p (b n)"),
                                  ACT.Copy).then_inc(q_copied, 1)
                if unit in "qk" and not first:
                    attend(i + 8 * (unit == "k"), g - 1)
                if i == 7 and unit == "k":
                    sc.activation(kt_[:, :, :].rearrange("p f s -> p (f s)"), ps[:, 3:5, :].rearrange("p b n -> p (b n)"),
                                  ACT.Copy).then_inc(k_copied, 1)
                if unit == "v":
                    attend(i - 8, g)
                if i == 7 and unit == "v":
                    sc.activation(v[:, :, :], ps[:, 5:7, :], ACT.Copy).then_inc(v_copied, 1)
                if unit == "acc" and is_last(g):
                    attend(i, g, LAST_PLAN)

            steps(att, 0, ATT_FIRST, lambda u, i: att_step(True, 0, u, i))
            with act.Fori(0, QG - 2) as t:
                steps(att, 24, ATT_BODY, lambda u, i: att_step(False, t + 1, u, i), t, 32)
            steps(att, 88, ATT_BODY, lambda u, i: att_step(False, QG - 1, u, i))
            for j in LAST_STEPS:
                attend(j, QG - 1, LAST_PLAN)
            steps(att, 120, ACC, lambda u, i: output_norm(att, i), urgent=True)
            square_sums(3)
            normed(3, (48,), (xhi,))
            mlp(mlp1)

        @block.vector
        def _(dve):
            chain = Tally(dve, dve_chain)
            ve = nc.vector

            def split(s):
                dve.wait_ge(hi_ready, s.n + 1)
                ve.tensor_tensor(out=wlo[:, s.split, :], in0=raw[:, s.raw, :], in1=whi[:, s.split, :].bitcast(F32),
                                 op=ALU.subtract).then_inc(lo_ready, 1)

            def link(ins):
                chain.mark(ins)
                chain.wait()

            def inverse_rms(dst, src, n, eps):
                chain.mark(ve.tensor_scalar(rs_x, src, 1.0 / n, eps, ALU.mult, ALU.add))
                chain.mark(ve.tensor_scalar(rs_h, src, -0.5 / n, -0.5 * eps, ALU.mult, ALU.add))
                chain.wait(back=1)
                link(ve.tensor_scalar(rs_a.bitcast(I32), rs_x.bitcast(I32), 1, None, ALU.logical_shift_right))
                link(ve.tensor_scalar(dst.bitcast(I32), rs_a.bitcast(I32), -1.0, float(0x5F3759DF), ALU.mult, ALU.add))
                for step in range(3):
                    for c in (slice(0, 1), slice(1, 2)):
                        if step > 0:
                            chain.wait(back=1)
                        chain.mark(ve.scalar_tensor_tensor(out=rs_a[:, c], in0=dst[:, c], scalar=rs_h[:, c], in1=dst[:, c],
                                                           op0=ALU.mult, op1=ALU.mult))
                    for c in (slice(0, 1), slice(1, 2)):
                        chain.wait(back=1)
                        chain.mark(ve.scalar_tensor_tensor(out=dst[:, c], in0=rs_a[:, c], scalar=1.5, in1=dst[:, c],
                                                           op0=ALU.add, op1=ALU.mult))
                chain.wait()

            def diagonal(rs, done, dst=diag):
                for t in range(MT):
                    ve.tensor_scalar(dst[:, t, :], ident[:, :], rs[:, t:t + 1], None, ALU.mult).then_inc(done, 1)

            def steps(ph, first_k, order, body, t=0, per=0, urgent=False):
                for k, (unit, i) in enumerate(order):
                    ahead = ph.slab(first_k + k + LEAD, t, per)
                    if urgent and k == len(order) - 1:
                        dve.wait_ge(slab_used, ph.slab(first_k + k).used)
                        body(unit, i)
                        continue
                    if ahead:
                        split(ahead)
                        dve.wait_ge(lo_ready, ahead.used)
                    else:
                        dve.wait_ge(slab_used, ph.slab(first_k + k).used)
                    body(unit, i)

            def add_output(ph, b, i):
                if i % 2 == 0:
                    return
                nt = i // 2
                cols = y[:, :, nt * BLK:(nt + 1) * BLK]
                bank = 3 + 2 * (nt % 2)
                ve.tensor_tensor(out=cols, in0=cols, in1=ps[:, bank:bank + 2, :], op=ALU.add).then_inc(acc_added, 1)

            def normed(r, cols, his, los, waiting):
                dve.wait_ge(h_sq, MT * PIECES * (r + 1))
                link(ve.reduce_sum(sum_h, ssh, AX))
                inverse_rms(rsh, sum_h, D, 1e-6)
                if r == 0:
                    dve.wait_ge(consts_ready, 1)
                diagonal(rsh, rms_ready)
                for slab in waiting:
                    split(slab)
                if r == 0:
                    dve.wait_ge(par_ready, 1)
                for i in range(KT // 2):
                    dve.wait_ge(x_hi, 8 * r + i + 1)
                    for hi, lo, col in zip(his, los, cols):
                        for j in range(2):
                            k = 2 * i + j
                            last = ve.scalar_tensor_tensor(
                                out=lo[:, k, :], in0=ps[:, i, j * S:(j + 1) * S], scalar=par[:, col + k:col + k + 1],
                                in1=hi[:, k, :].bitcast(F32), op0=ALU.mult, op1=ALU.subtract)
                    last.then_inc(x_lo, 1)

            def residual(r):
                dve.wait_ge(y_sq, MT * NT * (r + 1))
                link(ve.reduce_sum(sum_y, ssy, AX))
                inverse_rms(rsy, sum_y, D, 1e-6)
                dve.wait_ge(yw_ready, NT * (r + 1))
                for t in range(MT):
                    for p in range(PIECES):
                        ve.scalar_tensor_tensor(out=h[:, t, piece(p)], in0=y[:, t, piece(p)], scalar=rsy[:, t:t + 1],
                                                in1=h[:, t, piece(p)], op0=ALU.mult, op1=ALU.add).then_inc(h_new, 1)

            def block_lo(bank=5):
                for f in range(4):
                    last = ve.scalar_tensor_tensor(
                        out=blo[0][:, f, :], in0=ps[:, bank + f // 2, (f % 2) * S:(f % 2 + 1) * S], scalar=gpar[:, f:f + 1],
                        in1=bhi[0][:, f, :].bitcast(F32), op0=ALU.mult, op1=ALU.subtract)
                last.then_inc(h_ready, 1)

            ve.memset(par_rows[:, :, :], 0.0).then_inc(rows_cleared, 1)
            normed(0, (0,), (xhi,), (xlo,), [mix.slab(k) for k in range(2)])
            for k in range(2, LEAD):
                split(mix.slab(k))
            split(mix.slab(LEAD))

            dve.wait_ge(heads_in, 48)
            dve.wait_ge(slab_used, mix.slab(0).used)
            link(ve.tensor_tensor(out=dt[:, :, :], in0=ps[:, 7, 0:2 * NH].rearrange("p (c n) -> p c n", c=MT),
                                  in1=hd[:, 0, :].unsqueeze(1).to_broadcast([P, MT, NH]), op=ALU.add))
            link(ve.tensor_scalar(tmp[:, 0, :, :], dt[:, :, :], -1.0, None, ALU.mult))
            ve.tensor_tensor(out=tmp[:, 0, :, :], in0=tmp[:, 0, :, :], in1=dt[:, :, :], op=ALU.max).then_inc(dt_v, 1)
            link(ve.tensor_scalar(dt[:, :, :], dt[:, :, :], 0.0, None, ALU.max))
            dve.wait_ge(dt_e, 1)
            ve.tensor_scalar(tmp[:, 2, :, :], tmp[:, 1, :, :], 1.0, None, ALU.add).then_inc(dt_l, 1)
            dve.wait_ge(dt_l, 1)
            link(ve.tensor_scalar(tmp[:, 0, :, :], tmp[:, 2, :, :], 1.0, None, ALU.is_equal))
            dve.wait_ge(dt_e, 2)
            link(ve.scalar_tensor_tensor(out=tmp[:, 2, :, :], in0=tmp[:, 2, :, :], scalar=-1.0,
                                         in1=tmp[:, 0, :, :], op0=ALU.add, op1=ALU.add))
            link(ve.tensor_tensor(out=tmp[:, 3, :, :], in0=tmp[:, 3, :, :], in1=tmp[:, 0, :, :], op=ALU.add))
            link(ve.reciprocal(tmp[:, 2, :, :], tmp[:, 2, :, :]))
            link(ve.tensor_tensor(out=tmp[:, 3, :, :], in0=tmp[:, 3, :, :], in1=tmp[:, 1, :, :], op=ALU.mult))
            link(ve.tensor_tensor(out=tmp[:, 3, :, :], in0=tmp[:, 3, :, :], in1=tmp[:, 2, :, :], op=ALU.mult))
            link(ve.tensor_tensor(out=dt[:, :, :], in0=dt[:, :, :], in1=tmp[:, 3, :, :], op=ALU.add))
            ve.scalar_tensor_tensor(out=da[:, :, :], in0=dt[:, :, :], scalar=-1.0,
                                    in1=hd[:, 1, :].unsqueeze(1).to_broadcast([P, MT, NH]),
                                    op0=ALU.mult, op1=ALU.mult).then_inc(da_ready, 1)
            dve.wait_ge(lam_in, 64)
            for i in range(2):
                link(ve.tensor_tensor(out=lamv[:, 2 * i, :], in0=lamv[:, 2 * i, :], in1=lamv[:, 2 * i + 1, :], op=ALU.mult))
                last = ve.reduce_sum(neglam[:, i:i + 1], lamv[:, 2 * i, :], AX)
            last.then_inc(lam_ready, 1)
            dve.wait_ge(lam_e, 1)
            link(ve.tensor_tensor(out=neglam[:, 1:2], in0=neglam[:, 3:4], in1=neglam[:, 2:3], op=ALU.subtract))
            link(ve.tensor_scalar(neglam[:, 0:1], neglam[:, 1:2], -LAMBDA_INIT, None, ALU.add))

            def mix_cum():
                dve.wait_ge(cum_done, 1)
                link(ve.tensor_copy(cum[:, :, :], ps[:, 7, 0:2 * NH].rearrange("p (c n) -> p c n", c=MT)))
                ve.tensor_tensor(out=todend[:, :], in0=ps[:, 7, 2 * NH:3 * NH], in1=cum[:, 0, :],
                                 op=ALU.subtract).then_inc(cum_ready, 1)

            def mix_step(first, g, unit, i):
                z_first = first or is_last(g, G)
                if first and (unit, i) == ("xs", 4):
                    mix_cum()
                group = g + 1 if unit == "acc" else g
                if ((unit, i) == ("xs", 2) and not first) or ((unit, i) == ("acc", 2) and is_last(g, G)):
                    dve.wait_ge(g_sq, 2 * group)
                    inverse_rms(rsg, ssg, BLK, 1e-5)
                    diagonal(rsg, g_ready)
                if (unit, i) == (("z", 1) if z_first else ("xs", 4)):
                    dve.wait_ge(cumb_in, 16 * (g + 1))
                    dve.wait_ge(cpar_ready, g + 1)
                    if not first:
                        dve.wait_ge(y_done, g)
                    for c in range(MT):
                        for r in range(R):
                            last = ve.tensor_scalar(m[:, c, r, :], cumb[:, r, c * P:(c + 1) * P], gcum[:, c, r:r + 1], 0.0,
                                                    ALU.subtract, ALU.min)
                    last.then_inc(seg_done, 1)
                if (unit, i) in (("xs", 7), ("bc", 3)):
                    lo, hi = (0, 4) if unit == "xs" else (4, 6)
                    if first and unit == "xs":
                        dve.wait_ge(cumt_done, 1)
                        ve.tensor_copy(cumt[:, :], ps[0:NH, 7, 0:S]).then_inc(cumt_ready, 1)
                    dve.wait_ge(cpar_ready, g + 1)
                    dve.wait_ge(pre_ready, 3 * g + (2 if unit == "xs" else 3))
                    if not first:
                        dve.wait_ge(spread_done, 2 * g)
                        dve.wait_ge(y_done, g)
                    for f in range(lo, hi):
                        chain.mark(ve.tensor_scalar(conv[:, f, :], pre[:, f, 0:S], cpar[:, 0, f:f + 1], None, ALU.mult))
                    for tap in range(1, TAPS):
                        for f in range(lo, hi):
                            chain.wait(back=hi - lo - 1)
                            ins = ve.scalar_tensor_tensor(
                                out=conv[:, f, :], in0=pre[:, f, tap:tap + S], scalar=cpar[:, tap, f:f + 1],
                                in1=conv[:, f, :], op0=ALU.mult, op1=ALU.add)
                            if (tap, f) == (TAPS - 1, hi - 1):
                                ins.then_inc(conv_done, 1)
                            else:
                                chain.mark(ins)
                    if (unit, i) == ("xs", 7) and not first:
                        dve.wait_ge(b_hi, g)
                        block_lo()
                if unit == "acc":
                    add_output(mix, g - 1, i)
                if (unit, i) == SPREAD[z_first]:
                    dve.wait_ge(spread_done, 2 * g + 2)
                    ve.tensor_copy(bt[:, :], ps[:, 2, 0:P])
                    ve.tensor_tensor(out=cbm[:, :, :], in0=ps[:, 2, P:3 * P].rearrange("p (c i) -> p c i", c=MT),
                                     in1=causal[:, :].unsqueeze(1).to_broadcast([P, MT, P]), op=ALU.mult)\
                        .then_inc(cb_ready, 1)
                if (unit, i) == INTRA[z_first]:
                    dve.wait_ge(cb_ready, g + 1)
                    for c in range(MT):
                        dve.wait_ge(decay_done, 2 * g + c + 1)
                        ve.tensor_tensor(out=m[:, c, :, :], in0=m[:, c, :, :],
                                         in1=cbm[:, c, :].unsqueeze(1).to_broadcast([P, R, P]), op=ALU.mult)\
                            .then_inc(mt_ready, 1)
                if (unit, i) == ("z", 7):
                    dve.wait_ge(y_done, g + 1)
                    dve.wait_ge(pool_ready, g + 1)
                    by_head = lambda ap: ap.rearrange("p (r d) -> p r d", r=R)
                    chain.mark(ve.tensor_tensor(out=by_head(xd[:, 1, :]), in0=by_head(ps[:, 2, :]),
                                                in1=column_bcast(ecum[:, bass.ds(g * R, R)], PD), op=ALU.mult))
                    chain.mark(ve.tensor_tensor(out=yg[:, :, :], in0=yg[:, :, :], in1=ps[:, 5:7, :], op=ALU.add))
                    chain.wait()
                    link(ve.tensor_tensor(out=yg[:, 1, :], in0=yg[:, 1, :], in1=xd[:, 1, :], op=ALU.add))
                    dve.wait_ge(zs_ready, g + 1)
                    ve.tensor_tensor(out=yg[:, :, :], in0=yg[:, :, :], in1=zs[:, :, :], op=ALU.mult).then_inc(gated, 1)

            dve.wait_ge(y_zeroed, 1)
            steps(mix, 1, MIX_FIRST, lambda u, i: mix_step(True, 0, u, i))
            with dve.Fori(0, G - 2) as t:
                chain.enter(t, 41)
                steps(mix, 21, MIX_BODY, lambda u, i: mix_step(False, t + 1, u, i), t, 28)
            chain.leave(G - 2, 41)
            steps(mix, 189, MIX_LAST, lambda u, i: mix_step(False, G - 1, u, i))
            dve.wait_ge(b_hi, G)
            block_lo(0)
            steps(mix, 217, ACC, lambda u, i: add_output(mix, G - 1, i), urgent=True)
            residual(0)
            normed(1, (32,), (xhi,), (xlo,), [mlp0.slab(LEAD - 1)])

            def mlp(ph, r):
                def up(which, b):
                    dve.wait_ge(b_hi, ph.features(b))
                    for n in range(2):
                        chain.mark(ve.tensor_tensor(out=sq[:, n, :], in0=relu[:, n, :], in1=relu[:, n, :], op=ALU.mult))
                    for n in range(2):
                        chain.wait(back=1 - n)
                        last = ve.tensor_tensor(
                            out=blo[which][:, 2 * n:2 * n + 2, :].rearrange("p f s -> p (f s)"), in0=sq[:, n, :],
                            in1=bhi[which][:, 2 * n:2 * n + 2, :].rearrange("p f s -> p (f s)").bitcast(F32), op=ALU.subtract)
                    last.then_inc(h_ready, 1)

                def step(unit, i, b):
                    if unit[:2] == "up" and i == 7:
                        up(int(unit[2:] or 0), b + {"up": 0, "up1": 1, "up0": 2}[unit])
                    if unit[:3] == "acc":
                        add_output(ph, b + int(unit[3:]), i)

                dve.wait_ge(y_zeroed, r + 1)
                steps(ph, 0, MLP_FIRST, lambda u, i: step(u, i, 0))
                with dve.Fori(0, 7) as t:
                    chain.enter(t, 4)
                    steps(ph, 8, MLP_BODY, lambda u, i: step(u, i, 2 * t), t, 32)
                chain.leave(7, 4)
                steps(ph, 232, MLP_LAST, lambda u, i: step(u, i, 14), urgent=True)

            mlp(mlp0, 1)
            residual(1)
            normed(2, (16, 64), (xhi, khi), (xlo, klo), [att.slab(LEAD - 1)])

            def attend(j, p, plan=USUAL_PLAN):
                for i in range(HG):
                    n = HG * p + i
                    if j == plan.logits[i]:
                        dve.wait_ge(lg_done, n + 1)
                        dve.wait_ge(tab_in, 16 * (p + 1))
                        l = lg[i % 2]
                        for cols, bias in ((slice(0, S), tab[:, i, :]), (slice(S, S + P), tab[:, i, P:])):
                            for c in range(2):
                                last = ve.scalar_tensor_tensor(out=l[:, c, cols], in0=ps[:, 2 + 5 * c, cols], scalar=DH ** -0.5,
                                                               in1=bias, op0=ALU.mult, op1=ALU.add)
                            chain.mark(last)
                        chain.wait(back=1)
                        ve.tensor_reduce(nmax[i % 2][:, 0:2], l[:, :, 0:S], AX, ALU.max, negate=True)
                        chain.wait()
                        ve.tensor_reduce(nmax[i % 2][:, 2:4], l[:, :, S:], AX, ALU.max, negate=True).then_inc(lg_ready, 1)
                    if j == plan.weigh[i]:
                        dve.wait_ge(ex_ready, n + 1)
                        if i >= 2:
                            dve.wait_ge(at_t, n - 1)
                        l, a = lg[i % 2], at[i % 2]
                        link(ve.reciprocal(rinv[:, :], psum_[i % 2][:, :]))
                        link(ve.tensor_tensor(out=rinv[:, 1:4:2], in0=rinv[:, 1:4:2],
                                              in1=neglam[:, 0:1].to_broadcast([P, 2]), op=ALU.mult))
                        for q, cols in enumerate((slice(0, S), slice(S, S + P))):
                            chain.mark(ve.tensor_scalar(l[:, 1, cols], l[:, 1, cols], rinv[:, 2 * q + 1:2 * q + 2], None,
                                                        ALU.mult))
                        for q, cols in enumerate((slice(0, S), slice(S, S + P))):
                            chain.wait(back=1 - q)
                            last = ve.scalar_tensor_tensor(out=a[:, cols], in0=l[:, 0, cols], scalar=rinv[:, 2 * q:2 * q + 1],
                                                           in1=l[:, 1, cols], op0=ALU.mult, op1=ALU.add)
                        last.then_inc(at_ready, 1)
                    if j == plan.out[i]:
                        dve.wait_ge(o_sq, 2 * n + 2)
                        ve.tensor_copy(ob[:, i, :, :], ps[:, plan.out_bank, 0:S].rearrange("p (c e) -> p c e", c=MT)).then_inc(o_ready, 1)
                        inverse_rms(rsa, ssa[:, i, :], P, 1e-5)
                        diagonal(rsa, o_ready, hdiag[:, i, :, :])
                    if j == plan.turn_out[i]:
                        dve.wait_ge(b_hi, att.ready0 + n + 1)
                        ve.scalar_tensor_tensor(out=blo[0][:, i, :], in0=ps[:, plan.turned_banks[i], 0:S], scalar=subw[:, :],
                                                in1=bhi[0][:, i, :].bitcast(F32), op0=ALU.mult, op1=ALU.subtract)\
                            .then_inc(h_ready, 1)

            def att_step(first, g, unit, i):
                if unit in "qk" and not first:
                    attend(i + 8 * (unit == "k"), g - 1)
                if unit == "v":
                    attend(i - 8, g)
                if unit == "acc":
                    add_output(att, g - 1, i)
                    if is_last(g):
                        attend(i, g, LAST_PLAN)

            dve.wait_ge(y_zeroed, 3)
            dve.wait_ge(subw_ready, 1)
            steps(att, 0, ATT_FIRST, lambda u, i: att_step(True, 0, u, i))
            with dve.Fori(0, QG - 2) as t:
                chain.enter(t, 88)
                steps(att, 24, ATT_BODY, lambda u, i: att_step(False, t + 1, u, i), t, 32)
            chain.leave(QG - 2, 88)
            steps(att, 88, ATT_BODY, lambda u, i: att_step(False, QG - 1, u, i))
            for j in LAST_STEPS:
                attend(j, QG - 1, LAST_PLAN)
            steps(att, 120, ACC, lambda u, i: add_output(att, QG - 1, i), urgent=True)
            residual(2)
            normed(3, (48,), (xhi,), (xlo,), [mlp1.slab(LEAD - 1)])
            mlp(mlp1, 3)
            residual(3)

        @block.tensor
        def _(pe):
            te = nc.tensor

            def three(outs, lhs, rhs, start, stop):
                (lh, ll), (rh, rl) = lhs, rhs
                te.matmul(outs, lh, rh, start=start, stop=False, skip_group_check=True)
                te.matmul(outs, lh, rl, start=False, stop=False, skip_group_check=True)
                return te.matmul(outs, ll, rh, start=False, stop=stop, skip_group_check=True)

            def slot(s, tiles):
                return [t[:, s.split, :].rearrange("p (t n) -> p t n", t=tiles) for t in (whi, wlo)]

            def feature_major(s, i, banks, x, tiles=2, cols=BLK, half=0, last_i=7):
                pe.wait_ge(lo_ready, s.n + 1)
                wh, wl = slot(s, tiles)
                for f in range(cols // P):
                    for j in range(tiles):
                        k = i * tiles + j
                        dst = ps[:, banks[f // 2], (f % 2 + half) * S:(f % 2 + half + 1) * S]
                        c = slice(f * P, (f + 1) * P)
                        last = three(dst, (wh[:, j, c], wl[:, j, c]), (x[0][:, k, :], x[1][:, k, :]),
                                     start=(k == 0 and f % 2 + half == 0), stop=(i == last_i and j == tiles - 1))
                last.then_inc(slab_used, 1)

            def token_major(s, i, slabs, bank, x, tiles=2, cols=BLK):
                pe.wait_ge(lo_ready, s.n + 1)
                wh, wl = slot(s, tiles)
                for t in range(MT):
                    for j in range(tiles):
                        k = i * tiles + j
                        c = slice(t * P, (t + 1) * P)
                        if cols == BLK:
                            dst, start = ps[:, bank + t, :], k == 0
                        else:
                            dst, start = ps[:, bank, t * cols:(t + 1) * cols], k == 0 and t == 0
                        last = three(dst, (x[0][:, k, c], x[1][:, k, c]), (wh[:, j, :], wl[:, j, :]),
                                     start=start, stop=(i == slabs - 1 and j == tiles - 1))
                last.then_inc(slab_used, 1)

            def output(ph, s, i, b, which=0):
                nt = i // 2
                if i == 0:
                    pe.wait_ge(h_ready, ph.features(b))
                a = 4 * (ph.block0 + b) + nt
                if i % 2 == 0 and (nt >= 2 or ph in (mlp0, mlp1) or is_last(b, ph.blocks)):
                    pe.wait_ge(acc_added, a - 1)
                token_major(s, i % 2, 2, 3 + 2 * (nt % 2), (bhi[which], blo[which]))

            def transpose_x(r):
                pe.wait_ge(rms_ready, MT * (r + 1))
                for i in range(KT // 2):
                    for j in range(2):
                        for t in range(MT):
                            k = 2 * i + j
                            last = te.matmul(ps[:, i, j * S + t * P:j * S + (t + 1) * P], h[:, t, k * P:(k + 1) * P],
                                             diag[:, t, :], start=True, stop=True, skip_group_check=True)
                    last.then_inc(xt_done, 1)

            x, xk = (xhi, xlo), (khi, klo)

            pe.wait_ge(consts_ready, 1)
            pe.wait_ge(small_in, 16 * SMALL_LOADS)
            for i in range(4):
                last = te.transpose(ps[:, 0, i * P:(i + 1) * P], par_rows[:, i, :], ident[:, :])
            last.then_inc(par_t, 1)
            pe.wait_ge(par_ready, 1)
            transpose_x(0)
            pe.wait_ge(x_lo, 8)
            token_major(mix.slab(0), 0, 1, 7, x, tiles=16, cols=NH)

            def spread(g):
                pe.wait_ge(silu_done, 2 * g + 2)
                for c in range(MT):
                    for f in range(4):
                        last = te.transpose(ps[:, c, f * P:(f + 1) * P], conv[:, f, c * P:(c + 1) * P], ident[:, :])
                last.then_inc(spread_done, 1)
                te.transpose(ps[:, 2, 0:P], conv[:, 4, 0:P], ident[:, :])
                for c in range(MT):
                    cs = slice(c * P, (c + 1) * P)
                    last = te.matmul(ps[:, 2, (c + 1) * P:(c + 2) * P], conv[:, 4, cs], conv[:, 5, cs],
                                     start=True, stop=True, skip_group_check=True)
                last.then_inc(spread_done, 1)

            def mix_step(first, g, unit, i, s):
                last_group = is_last(g, G)
                z_first = first or last_group
                added = g - 1 if last_group else g
                if unit == "xs":
                    feature_major(s, i, (0, 1), x)
                if unit == "bc":
                    if i == 0 and not first:
                        pe.wait_ge(gated, g)
                    feature_major(s, i % 2, (2,), x, tiles=8, cols=P, half=i // 2, last_i=1)
                if unit == "z":
                    if i == 0 and not first:
                        pe.wait_ge(acc_added, 4 * added - (0 if last_group else 1))
                    token_major(s, i, 8, 3, x)
                if unit == "acc":
                    if last_group and i in (0, 2):
                        pe.wait_ge(*((zs_ready, G) if i == 0 else (gated, G)))
                    output(mix, s, i, g - 1)
                if (unit, i) == ("xs", 7) and not first:
                    transpose_block(g)
                if first and (unit, i) == ("xs", 3):
                    decays()
                if (unit, i) == SPREAD[z_first]:
                    spread(g)
                if (unit, i) == STATE[z_first]:
                    pe.wait_ge(cb_ready, g + 1)
                    pe.wait_ge(pool_ready, g + 1)
                    te.matmul(ps[:, 7, :], bt[:, :], xe[:, :], start=True, stop=True).then_inc(state_done, 1)
                if (unit, i) == ("z", 7):
                    if not first:
                        pe.wait_ge(acc_added, 4 * added)
                    for c in range(MT):
                        pe.wait_ge(mt_ready, 2 * g + c + 1)
                        for r in range(R):
                            te.matmul(ps[:, 5 + c, r * PD:(r + 1) * PD], m[:, c, r, :], xd[:, c, r * PD:(r + 1) * PD],
                                      start=True, stop=True, skip_group_check=True)
                    pe.wait_ge(state_ready, g + 1)
                    te.matmul(ps[:, 2, :], conv[:, 5, P:], state[:, :], start=True, stop=True).then_inc(y_done, 1)

            def decays():
                pe.wait_ge(da_ready, 1)
                for c in range(MT):
                    te.matmul(ps[:, 7, c * NH:(c + 1) * NH], causal[:, :], da[:, c, :], start=True, stop=True,
                              skip_group_check=True)
                te.matmul(ps[:, 7, 2 * NH:3 * NH], ones[:, :], da[:, 0, :], start=True, stop=True,
                          skip_group_check=True).then_inc(cum_done, 1)

            def transpose_block(g, bank=5):
                pe.wait_ge(g_ready, 2 * g)
                for c in range(MT):
                    for f in range(4):
                        last = te.matmul(ps[:, bank + f // 2, (f % 2) * S + c * P:(f % 2) * S + (c + 1) * P],
                                         yg[:, c, f * P:(f + 1) * P], diag[:, c, :], start=True, stop=True,
                                         skip_group_check=True)
                last.then_inc(gt_done, 1)

            for k, (unit, i) in enumerate(MIX_FIRST):
                mix_step(True, 0, unit, i, mix.slab(1 + k))
                if (unit, i) == ("xs", 6):
                    pe.wait_ge(cum_ready, 1)
                    for c in range(MT):
                        last = te.transpose(ps[0:NH, 7, c * P:(c + 1) * P], cum[:, c, :], ident[:, :])
                    last.then_inc(cumt_done, 1)
            with pe.Fori(0, G - 2) as t:
                for k, (unit, i) in enumerate(MIX_BODY):
                    mix_step(False, t + 1, unit, i, mix.slab(21 + k, t, 28))
            for k, (unit, i) in enumerate(MIX_LAST):
                mix_step(False, G - 1, unit, i, mix.slab(189 + k))
            transpose_block(G, 0)
            for k, (unit, i) in enumerate(ACC):
                output(mix, mix.slab(217 + k), i, G - 1)
            transpose_x(1)

            def mlp(ph, r):
                def up(s, i, b, which):
                    if i == 0 and above(b, 1):
                        pe.wait_ge(b_hi, ph.features(b - 2))
                    feature_major(s, i, UP_BANKS[which], x)

                def step(unit, i, b, s):
                    if unit[:2] == "up":
                        up(s, i, b + {"up": 0, "up1": 1, "up0": 2}[unit], int(unit == "up1"))
                    else:
                        output(ph, s, i, b + int(unit[3:]), int(unit[3:]))

                for k, (unit, i) in enumerate(MLP_FIRST):
                    pe.wait_ge(x_lo, 8 * r + max(2, i + 1))
                    step(unit, i, 0, ph.slab(k))
                with pe.Fori(0, 7) as t:
                    for k, (unit, i) in enumerate(MLP_BODY):
                        step(unit, i, 2 * t, ph.slab(8 + k, t, 32))
                for k, (unit, i) in enumerate(MLP_LAST):
                    step(unit, i, 14, ph.slab(232 + k))

            mlp(mlp0, 1)
            transpose_x(2)

            def attend(j, p, plan=USUAL_PLAN):
                for i in range(HG):
                    n = HG * p + i
                    if j == plan.logits[i]:
                        if i > 0:
                            pe.wait_ge(lg_ready, n)
                        for c in range(2):
                            cs = slice(c * DH, (c + 1) * DH)
                            te.matmul(ps[:, 2 + 5 * c, 0:S], qt[cs, i, P:], kt_[cs, i, :], start=True, stop=True,
                                      skip_group_check=True)
                            last = te.matmul(ps[:, 2 + 5 * c, S:S + P], qt[cs, i, 0:P], kt_[cs, i, 0:P], start=True,
                                             stop=True, skip_group_check=True)
                        last.then_inc(lg_done, 1)
                    if j == plan.out[i]:
                        pe.wait_ge(at_copied, n + 1)
                        if i > 0:
                            pe.wait_ge(o_ready, 3 * n - 2)
                        te.matmul(ps[:, plan.out_bank, P:2 * P], att_t[:, 0:P], v[:, 0, i * P:(i + 1) * P], start=True, stop=False,
                                  skip_group_check=True)
                        te.matmul(ps[:, plan.out_bank, P:2 * P], att_t[:, P:2 * P], v[:, 1, i * P:(i + 1) * P], start=False, stop=True,
                                  skip_group_check=True)
                        te.matmul(ps[:, plan.out_bank, 0:P], att_t[:, 2 * P:], v[:, 0, i * P:(i + 1) * P], start=True, stop=True,
                                  skip_group_check=True).then_inc(o_done, 1)
                    if j == plan.turn_out[i]:
                        pe.wait_ge(o_ready, 3 * (n + 1))
                        pe.wait_ge(lg_ready, HG * (p + 1))
                        if i >= 2 and plan is USUAL_PLAN:
                            pe.wait_ge(h_ready, att.ready0 + n - 1)
                        for c in range(MT):
                            last = te.matmul(ps[:, plan.turned_banks[i], c * P:(c + 1) * P], ob[:, i, c, :], hdiag[:, i, c, :],
                                             start=True, stop=True, skip_group_check=True)
                        last.then_inc(ot_done, 1)
                    if j == plan.turn_weights[i]:
                        pe.wait_ge(at_ready, n + 1)
                        if i > 0:
                            pe.wait_ge(at_copied, n)
                        for b in range(3):
                            last = te.transpose(ps[:, plan.weights_bank, b * P:(b + 1) * P], at[i % 2][:, b * P:(b + 1) * P], ident[:, :])
                        last.then_inc(at_t, 1)

            def att_step(first, g, unit, i, s):
                if unit == "q":
                    feature_major(s, i, (0, 1), x)
                if unit == "k":
                    feature_major(s, i, (3, 4), xk)
                if unit == "v":
                    if i == 0 and not first:
                        pe.wait_ge(o_ready, 3 * HG * g)
                    token_major(s, i, 8, 5, xk)
                    if i == 0:
                        pe.wait_ge(k_copied, g + 1)
                        if not first:
                            pe.wait_ge(h_ready, att.features(g - 1))
                    attend(i - 8, g)
                if unit == "acc":
                    if i == 0:
                        pe.wait_ge(k_copied, g + 1)
                    if i == 2:
                        pe.wait_ge(v_copied, g + 1)
                    output(att, s, i, g - 1)
                    if is_last(g):
                        if i == 0:
                            pe.wait_ge(v_copied, g + 1)
                        attend(i, g, LAST_PLAN)
                if unit in "qk" and not first:
                    if (unit, i) == ("q", 0):
                        pe.wait_ge(v_copied, g)
                    if (unit, i) == ("q", 3):
                        pe.wait_ge(acc_added, NT * (att.block0 + g - 1))
                    attend(i + 8 * (unit == "k"), g - 1)

            for k, (unit, i) in enumerate(ATT_FIRST):
                if k < 8:
                    pe.wait_ge(x_lo, 16 + max(2, i + 1))
                att_step(True, 0, unit, i, att.slab(k))
            with pe.Fori(0, QG - 2) as t:
                for k, (unit, i) in enumerate(ATT_BODY):
                    att_step(False, t + 1, unit, i, att.slab(24 + k, t, 32))
            for k, (unit, i) in enumerate(ATT_BODY):
                att_step(False, QG - 1, unit, i, att.slab(88 + k))
            for j in LAST_STEPS:
                attend(j, QG - 1, LAST_PLAN)
            for k, (unit, i) in enumerate(ACC):
                output(att, att.slab(120 + k), i, QG - 1)
            transpose_x(3)
            mlp(mlp1, 3)


INPUTS = ["x", "a_in_proj", "a_conv_w", "a_conv_b", "a_dt_bias", "a_A_log", "a_D", "a_gate_norm_w", "a_out_proj",
          "kv_norm_w", "w_k", "w_v", "rel_bias", "b_w_q", "b_lambda_q1", "b_lambda_k1", "b_lambda_q2", "b_lambda_k2",
          "b_subln_w", "b_out_proj", "norm_pre_mix", "norm_post_mix", "norm_pre_mlp", "norm_post_mlp",
          "mlp_w1", "mlp_w2"]


def kernel(**inputs):
    import concourse.bacc as bacc
    from concourse.bass_utils import run_bass_kernel_spmd

    nc = bacc.Bacc("TRN2", target_bir_lowering=False, num_devices=1)
    arrays, aps = {}, {}
    for name in INPUTS:
        arrays[name] = np.ascontiguousarray(inputs[name])
        aps[name] = nc.dram_tensor(name, arrays[name].shape, mybir.dt.from_np(arrays[name].dtype),
                                   kind="ExternalInput").ap()
    out = nc.dram_tensor("out", (1, S, D), F32, kind="ExternalOutput").ap()
    build(nc, aps, out)
    return run_bass_kernel_spmd(nc, [arrays], core_ids=[0]).results[0]["out"]
```
